# Optimizing a Trainium2 kernel written in Bass

```python
import jax, jax.numpy as jnp
from jax import lax
import numpy as np

D_MODEL = 1024
BATCH = 1
SEQ = 512
DEPTH = 4
DEC_BATCH = 8
DEC_SEQ = 4
PAST_LEN = 2048
PAGE_SIZE = 128

N_MIXERS = 3
N_GLA = (DEPTH + 2) // 3
N_FOX = (DEPTH + 1) // 3
N_CONV = DEPTH // 3

GLA_HEADS = 4
GLA_DK = D_MODEL // 2 // GLA_HEADS
GLA_DV = D_MODEL // GLA_HEADS
GLA_RANK = 16
GLA_TAU = 16.0
GLA_CHUNK = 64

FOX_HEADS = 16
FOX_DH = D_MODEL // FOX_HEADS
FOX_SCALE = FOX_DH ** -0.5
FOX_BIAS_INIT = 6.0
Q_BLOCK = 128
NEG_INF = -1e30

CONV_WIDTH = 31
D_FF = ((8 * D_MODEL // 3 + 255) // 256) * 256
RMS_EPS = 1e-6
LN_EPS = 1e-5

kernel_name = 'hybrid_gla_fox_conformer_decode_step'

def rmsnorm(x, g):
    xf = x.astype(jnp.float32)
    y = xf * lax.rsqrt(jnp.mean(xf * xf, axis=-1, keepdims=True) + RMS_EPS)
    return (y * g.astype(jnp.float32)).astype(x.dtype)

def swiglu_ffn(h, w1, w3, w2):
    return (jax.nn.silu(h @ w1) * (h @ w3)) @ w2

def gla_mixer(x, s0, wq, wk, wv, wg1, wg2, bg, wr, gn, wo):
    b, l, _ = x.shape
    f32 = jnp.float32
    q = (x @ wq).astype(f32).reshape(b, l, GLA_HEADS, GLA_DK) * (GLA_DK ** -0.5)
    k = (x @ wk).astype(f32).reshape(b, l, GLA_HEADS, GLA_DK)
    v = (x @ wv).astype(f32).reshape(b, l, GLA_HEADS, GLA_DV)
    logg = jax.nn.log_sigmoid(((x @ wg1) @ wg2 + bg).astype(f32)).reshape(b, l, GLA_HEADS, GLA_DK) / GLA_TAU
    c = GLA_CHUNK if l % GLA_CHUNK == 0 else l
    n = l // c

    def to_chunks(t):
        return t.reshape(b, n, c, GLA_HEADS, t.shape[-1]).transpose(1, 0, 3, 2, 4)

    causal = jnp.tril(jnp.ones((c, c), dtype=bool))

    def chunk_step(s, inp):
        qc, kc, vc, gc = inp
        cum = jnp.cumsum(gc, axis=2)
        q_e = qc * jnp.exp(cum)
        k_e = kc * jnp.exp(-cum)
        att = jnp.where(causal, jnp.einsum('bhtk,bhsk->bhts', q_e, k_e), 0.0)
        o = jnp.einsum('bhtk,bhkv->bhtv', q_e, s) + jnp.einsum('bhts,bhsv->bhtv', att, vc)
        last = cum[:, :, -1:, :]
        s_new = s * jnp.exp(last)[:, :, 0, :, None] + jnp.einsum('bhsk,bhsv->bhkv', kc * jnp.exp(last - cum), vc)
        return s_new, o

    s_fin, o = lax.scan(chunk_step, s0.astype(f32), (to_chunks(q), to_chunks(k), to_chunks(v), to_chunks(logg)))
    o = o.transpose(1, 0, 3, 2, 4).reshape(b, l, GLA_HEADS, GLA_DV)
    o = o * lax.rsqrt(jnp.mean(o * o, axis=-1, keepdims=True) + RMS_EPS) * gn.astype(f32)
    gate = jax.nn.silu((x @ wr).astype(f32)).reshape(b, l, GLA_HEADS, GLA_DV)
    y = (o * gate).reshape(b, l, GLA_HEADS * GLA_DV).astype(x.dtype) @ wo
    return y, s_fin

def fox_project(x, wq, wk, wv, wf, bf):
    b, l, _ = x.shape
    q = (x @ wq).reshape(b, l, FOX_HEADS, FOX_DH)
    k = (x @ wk).reshape(b, l, FOX_HEADS, FOX_DH)
    v = (x @ wv).reshape(b, l, FOX_HEADS, FOX_DH)
    logf = jax.nn.log_sigmoid((x @ wf + bf).astype(jnp.float32))
    return q, k, v, logf

def fox_prompt(x, wq, wk, wv, wf, bf, wo):
    b, l, _ = x.shape
    q, k, v, logf = fox_project(x, wq, wk, wv, wf, bf)
    cum = jnp.cumsum(logf, axis=1).transpose(0, 2, 1)
    nq = l // Q_BLOCK
    q_blocks = q.reshape(b, nq, Q_BLOCK, FOX_HEADS, FOX_DH).transpose(1, 0, 2, 3, 4)
    c_blocks = cum.reshape(b, FOX_HEADS, nq, Q_BLOCK).transpose(2, 0, 1, 3)
    q_pos = jnp.arange(l).reshape(nq, Q_BLOCK)
    k_pos = jnp.arange(l)

    def block(args):
        qb, cb, pb = args
        logits = (jnp.einsum('bqhd,bkhd->bhqk', qb, k).astype(jnp.float32) * FOX_SCALE
                  + cb[..., :, None] - cum[:, :, None, :])
        logits = jnp.where(pb[:, None] >= k_pos[None, :], logits, NEG_INF)
        p = jax.nn.softmax(logits, axis=-1).astype(v.dtype)
        return jnp.einsum('bhqk,bkhd->bqhd', p, v)

    o = lax.map(block, (q_blocks, c_blocks, q_pos))
    o = o.transpose(1, 0, 2, 3, 4).reshape(b, l, FOX_HEADS * FOX_DH)
    return o @ wo, k, v, logf

def fox_sample(x, k_pool, v_pool, lf_pool, page_table, wq, wk, wv, wf, bf, wo):
    b, n, _ = x.shape
    q, k, v, logf = fox_project(x, wq, wk, wv, wf, bf)
    k_past = k_pool[page_table].reshape(b, -1, FOX_HEADS, FOX_DH)
    v_past = v_pool[page_table].reshape(b, -1, FOX_HEADS, FOX_DH)
    lf_past = lf_pool[page_table].reshape(b, -1, FOX_HEADS).astype(jnp.float32)
    p_len = k_past.shape[1]
    k_all = jnp.concatenate([k_past, k.astype(k_past.dtype)], axis=1)
    v_all = jnp.concatenate([v_past, v.astype(v_past.dtype)], axis=1)
    lf_all = jnp.concatenate([lf_past, logf], axis=1)
    suffix = (lax.cumsum(lf_all, axis=1, reverse=True) - lf_all).transpose(0, 2, 1)
    logits = (jnp.einsum('bqhd,bkhd->bhqk', q.astype(k_all.dtype), k_all).astype(jnp.float32) * FOX_SCALE
              + suffix[:, :, None, :] - suffix[:, :, p_len:, None])
    mask = jnp.arange(p_len + n)[None, :] <= (p_len + jnp.arange(n))[:, None]
    logits = jnp.where(mask, logits, NEG_INF)
    p = jax.nn.softmax(logits, axis=-1).astype(v_all.dtype)
    o = jnp.einsum('bhqk,bkhd->bqhd', p, v_all).reshape(b, n, FOX_HEADS * FOX_DH).astype(x.dtype)
    return o @ wo, k, v, logf

def conv_module(x, buf, w1, b1, wdw, bdw, lng, lnb, w2, b2):
    u = x @ w1 + b1
    a, g = jnp.split(u, 2, axis=-1)
    u = a * jax.nn.sigmoid(g)
    ext = jnp.concatenate([buf.astype(u.dtype), u], axis=1)
    y = lax.conv_general_dilated(ext, wdw[:, None, :].astype(u.dtype), window_strides=(1,), padding='VALID',
                                 dimension_numbers=('NWC', 'WIO', 'NWC'), feature_group_count=D_MODEL) + bdw
    yf = y.astype(jnp.float32)
    mu = jnp.mean(yf, axis=-1, keepdims=True)
    var = jnp.mean(jnp.square(yf - mu), axis=-1, keepdims=True)
    yf = (yf - mu) * lax.rsqrt(var + LN_EPS) * lng.astype(jnp.float32) + lnb.astype(jnp.float32)
    out = jax.nn.silu(yf).astype(x.dtype) @ w2 + b2
    return out, ext[:, -(CONV_WIDTH - 1):, :]

def setup_inputs(seed: int = 0) -> dict:
    key = jax.random.key(seed)
    ks = iter(jax.random.split(key, 48))
    f32 = jnp.float32
    n_pages = PAST_LEN // PAGE_SIZE
    n_pool = (5 * DEC_BATCH * n_pages + 3) // 4

    def nrm(shape, scale=1.0):
        return jax.random.normal(next(ks), shape, f32) * scale

    def w(shape, fan_in):
        return nrm(shape, fan_in ** -0.5)

    d = D_MODEL
    inp = {}
    inp['x_prompt'] = nrm((BATCH, SEQ, d))
    inp['x_sample'] = nrm((DEC_BATCH, DEC_SEQ, d))
    inp['state_gla'] = nrm((N_GLA, DEC_BATCH, GLA_HEADS, GLA_DK, GLA_DV), 0.5)
    inp['cache_fox_k'] = nrm((N_FOX, n_pool, PAGE_SIZE, FOX_HEADS, FOX_DH))
    inp['cache_fox_v'] = nrm((N_FOX, n_pool, PAGE_SIZE, FOX_HEADS, FOX_DH))
    inp['cache_fox_logf'] = jax.nn.log_sigmoid(FOX_BIAS_INIT + nrm((N_FOX, n_pool, PAGE_SIZE, FOX_HEADS), 0.5))
    inp['state_conv'] = nrm((N_CONV, DEC_BATCH, CONV_WIDTH - 1, d), 0.5)
    perm = jax.random.permutation(next(ks), n_pool)
    inp['page_table'] = perm[:DEC_BATCH * n_pages].reshape(DEC_BATCH, n_pages).astype(jnp.int32)
    inp['norm_g'] = 1.0 + nrm((DEPTH, 4, d), 0.05)
    inp['gla_wq'] = w((N_GLA, d, GLA_HEADS * GLA_DK), d)
    inp['gla_wk'] = w((N_GLA, d, GLA_HEADS * GLA_DK), d)
    inp['gla_wv'] = w((N_GLA, d, GLA_HEADS * GLA_DV), d)
    inp['gla_wg1'] = w((N_GLA, d, GLA_RANK), d)
    inp['gla_wg2'] = w((N_GLA, GLA_RANK, GLA_HEADS * GLA_DK), GLA_RANK)
    inp['gla_bg'] = nrm((N_GLA, GLA_HEADS * GLA_DK), 0.1)
    inp['gla_wr'] = w((N_GLA, d, GLA_HEADS * GLA_DV), d)
    inp['gla_gn'] = 1.0 + nrm((N_GLA, GLA_DV), 0.05)
    inp['gla_wo'] = w((N_GLA, GLA_HEADS * GLA_DV, d), GLA_HEADS * GLA_DV)
    inp['fox_wq'] = w((N_FOX, d, d), d)
    inp['fox_wk'] = w((N_FOX, d, d), d)
    inp['fox_wv'] = w((N_FOX, d, d), d)
    inp['fox_wf'] = nrm((N_FOX, d, FOX_HEADS), 0.2 * d ** -0.5)
    inp['fox_bf'] = FOX_BIAS_INIT + nrm((N_FOX, FOX_HEADS), 0.5)
    inp['fox_wo'] = w((N_FOX, d, d), d)
    inp['conv_w1'] = w((N_CONV, d, 2 * d), d)
    inp['conv_b1'] = nrm((N_CONV, 2 * d), 0.02)
    inp['conv_wdw'] = w((N_CONV, CONV_WIDTH, d), CONV_WIDTH)
    inp['conv_bdw'] = nrm((N_CONV, d), 0.02)
    inp['conv_ln_g'] = 1.0 + nrm((N_CONV, d), 0.05)
    inp['conv_ln_b'] = nrm((N_CONV, d), 0.02)
    inp['conv_w2'] = w((N_CONV, d, d), d)
    inp['conv_b2'] = nrm((N_CONV, d), 0.02)
    inp['ffn_w1'] = w((DEPTH, d, D_FF), d)
    inp['ffn_w3'] = w((DEPTH, d, D_FF), d)
    inp['ffn_w2'] = w((DEPTH, D_FF, d), D_FF)
    return inp

def reference(x_prompt, x_sample, state_gla, cache_fox_k, cache_fox_v, cache_fox_logf, state_conv, page_table,
              norm_g, gla_wq, gla_wk, gla_wv, gla_wg1, gla_wg2, gla_bg, gla_wr, gla_gn, gla_wo,
              fox_wq, fox_wk, fox_wv, fox_wf, fox_bf, fox_wo,
              conv_w1, conv_b1, conv_wdw, conv_bdw, conv_ln_g, conv_ln_b, conv_w2, conv_b2,
              ffn_w1, ffn_w3, ffn_w2):
    xp, xs = x_prompt, x_sample
    bp = xp.shape[0]
    gla_p, gla_s = [], []
    fk_p, fv_p, fl_p, fk_s, fv_s, fl_s = [], [], [], [], [], []
    cv_p, cv_s = [], []
    for i in range(DEPTH):
        j = i // N_MIXERS
        kind = i % N_MIXERS
        hp = rmsnorm(xp, norm_g[i, 0])
        hs = rmsnorm(xs, norm_g[i, 0])
        if kind == 0:
            gw = (gla_wq[j], gla_wk[j], gla_wv[j], gla_wg1[j], gla_wg2[j], gla_bg[j], gla_wr[j], gla_gn[j], gla_wo[j])
            s0 = jnp.zeros((bp, GLA_HEADS, GLA_DK, GLA_DV), jnp.float32)
            mp, sp = gla_mixer(hp, s0, *gw)
            ms, ss = gla_mixer(hs, state_gla[j], *gw)
            gla_p.append(sp)
            gla_s.append(ss)
        elif kind == 1:
            fw = (fox_wq[j], fox_wk[j], fox_wv[j], fox_wf[j], fox_bf[j], fox_wo[j])
            mp, kp, vp, lp = fox_prompt(hp, *fw)
            ms, kn, vn, ln = fox_sample(hs, cache_fox_k[j], cache_fox_v[j], cache_fox_logf[j], page_table, *fw)
            fk_p.append(kp)
            fv_p.append(vp)
            fl_p.append(lp)
            fk_s.append(kn)
            fv_s.append(vn)
            fl_s.append(ln)
        else:
            cw = (conv_w1[j], conv_b1[j], conv_wdw[j], conv_bdw[j], conv_ln_g[j], conv_ln_b[j], conv_w2[j], conv_b2[j])
            buf0 = jnp.zeros((bp, CONV_WIDTH - 1, D_MODEL), hp.dtype)
            mp, bufp = conv_module(hp, buf0, *cw)
            ms, bufs = conv_module(hs, state_conv[j], *cw)
            cv_p.append(bufp)
            cv_s.append(bufs)
        xp = xp + rmsnorm(mp, norm_g[i, 1])
        xs = xs + rmsnorm(ms, norm_g[i, 1])
        xp = xp + rmsnorm(swiglu_ffn(rmsnorm(xp, norm_g[i, 2]), ffn_w1[i], ffn_w3[i], ffn_w2[i]), norm_g[i, 3])
        xs = xs + rmsnorm(swiglu_ffn(rmsnorm(xs, norm_g[i, 2]), ffn_w1[i], ffn_w3[i], ffn_w2[i]), norm_g[i, 3])
    return (xp, xs, jnp.stack(gla_p), jnp.stack(gla_s),
            jnp.stack(fk_p), jnp.stack(fv_p), jnp.stack(fl_p),
            jnp.stack(fk_s), jnp.stack(fv_s), jnp.stack(fl_s),
            jnp.stack(cv_p), jnp.stack(cv_s))


_drawn_inputs = setup_inputs


def setup_inputs(seed=0):
    import zlib

    import numpy as np

    out = dict(_drawn_inputs(seed))
    spreads = {}
    factors = {'cache_fox_logf': 5.291, 'conv_ln_b': 4.516}
    for name, (base, spread) in spreads.items():
        noise = np.random.default_rng([zlib.crc32(name.encode()), seed]).standard_normal(out[name].shape)
        drawn = base * np.exp(spread * noise) if base else spread * noise
        out[name] = __import__('jax').numpy.asarray(drawn.astype(out[name].dtype))
    for name, factor in factors.items():
        out[name] = (out[name] * factor).astype(out[name].dtype)
    return out
```

```python
from contextlib import ExitStack

import numpy as np
import concourse.bass as bass
import concourse.mybir as mybir

F32 = mybir.dt.float32
U32 = mybir.dt.uint32
ALU = mybir.AluOpType
ACT = mybir.ActivationFunctionType
AX = mybir.AxisListType
ds = bass.ds

P = 128
RING = 4
GLA_CHUNK = 64
RMS_EPS, LN_EPS = 1e-6, 1e-5
NEG = -1e30


class Tally:

    def __init__(self):
        self.blk = 0
        self.out = [0] * 8
        self.full = [0] * 8
        self.sq = self.h = self.z = self.x = self.o = 0

    def blocks(self, n, banks=(0, 2, 4, 6), uses=0):
        self.blk += n
        for b in banks:
            self.out[b] += uses

    def use(self, bank, n=1):
        self.out[bank] += n
        self.full[bank] += n


def build(nc, T_in, T_out, depth=4):
    (x_prompt, x_sample, state_gla, cache_k, cache_v, cache_lf, state_conv, page_table, norm_g,
     gla_wq, gla_wk, gla_wv, gla_wg1, gla_wg2, gla_bg, gla_wr, gla_gn, gla_wo,
     fox_wq, fox_wk, fox_wv, fox_wf, fox_bf, fox_wo,
     conv_w1, conv_b1, conv_wdw, conv_bdw, conv_ln_g, conv_ln_b, conv_w2, conv_b2,
     ffn_w1, ffn_w3, ffn_w2) = T_in
    (y_prompt, y_sample, gla_sp, gla_ss, fox_kp, fox_vp, fox_lp, fox_ks, fox_vs, fox_ls, cv_p, cv_s) = T_out

    _, SEQ, D = x_prompt.shape
    DB, DS, _ = x_sample.shape
    DEPTH = norm_g.shape[0]
    NS = DB * DS
    TOK = SEQ + NS
    HALF = TOK // 2
    KD = D // P
    D_FF = ffn_w1.shape[2]
    KF = D_FF // P
    KF2 = KF // 2
    PT = SEQ // P
    GH, DK, DV = state_gla.shape[2:]
    RANK = gla_wg1.shape[2]
    VH = DV // P
    NCH = SEQ // GLA_CHUNK
    NPOOL, PAGE, FH, DH = cache_k.shape[1:]
    NPAGES = page_table.shape[1]
    PAIRS = FH // 2
    CW = conv_wdw.shape[1]
    CB = CW - 1
    assert GH * DK == 4 * P and GH * DV == D and FH * DH == D and DH == 64 and PAGE == P and DK == P
    assert HALF <= 512 and KF % 2 == 0 and NS == 32 and DS == 4 and KD == 8 and SEQ == 4 * P

    ctx = ExitStack()

    def sb(name, shape, dt=F32):
        return ctx.enter_context(nc.sbuf_tensor(name, shape, dt))

    def sem(name):
        return ctx.enter_context(nc.semaphore(name))

    with ctx:
        xT = sb("xT", [P, KD, TOK])
        hT = sb("hT", [P, KD, TOK])
        yT = sb("yT", [P, KD, TOK])
        big = sb("big", [P, KF, TOK])
        ring = sb("ring", [P, RING, KF2 * P])
        sil = sb("sil", [P, 2, TOK])
        root = sb("root", [P, TOK])
        rstd = sb("rstd", [P, TOK])
        mix = sb("mix", [P, 17664])
        vecs = sb("vecs", [P, 4 * P])
        ident = sb("ident", [P, P])
        ones = sb("ones", [P, P])
        strict = sb("strict", [P, P])
        causal = sb("causal", [P, P])
        reset = sb("reset", [P, TOK])
        m_chunk = sb("m_chunk", [P, P])
        m_le = sb("m_le", [NS, DB, DS])
        m_gt = sb("m_gt", [NS, DB, DS])
        m_in = sb("m_in", [NS, DB])
        epsb = sb("epsb", [P, 2])
        wg1_sb = sb("wg1_sb", [P, KD, RANK])
        fbias = sb("fbias", [FH, 1])
        pt_sb = sb("pt_sb", [1, DB * NPAGES], mybir.dt.int32)
        wg2_sb = sb("wg2_sb", [RANK, GH * DK])
        lowr = sil[0:RANK, 0, :]
        acc = ctx.enter_context(nc.psum_tensor("acc", [P, 8, 512], F32))

        def acc2(bank):
            return acc[:, bank:bank + 2, 0:HALF]

        def accflat(bank):
            return acc[:, bank:bank + 2, :].rearrange("p b n -> p (b n)")[:, 0:TOK]

        def two(ap):
            return ap.rearrange("p (h t) -> p h t", h=2)

        def part(at, n, rows=P):
            return mix[0:rows, at:at + n]

        v_nat = part(0, (PT + 1) * D).rearrange("p (t n) -> p t n", t=PT + 1)
        M0 = (PT + 1) * D
        kd_nat = part(M0, (PT + 1) * GH * DK).rearrange("p (t h k) -> p t h k", t=PT + 1, h=GH)
        g_diff = part(M0, GH * TOK).rearrange("p (h t) -> p h t", h=GH)
        M1 = M0 + (PT + 1) * GH * DK
        att = part(M1, PT * GH * P).rearrange("p (t h s) -> p t h s", t=PT, h=GH)
        M2 = M1 + PT * GH * P
        att_s = part(M2, GH * NS, NS).rearrange("p (h s) -> p h s", h=GH)
        M3 = M2 + GH * NS
        S = part(M3, GH * DV).rearrange("p (h v) -> p h v", h=GH)
        M4 = M3 + GH * DV
        st = part(M4, 2 * 2 * GH * DV).rearrange("p (r b h v) -> p r b h v", r=2, b=2, h=GH)
        M5 = M4 + 4 * GH * DV
        kd_b = part(M5, 2 * GH * DK, NS).rearrange("p (r h k) -> p r h k", r=2, h=GH)
        assert M5 + 2 * GH * DK <= 17664
        pages = part(M0, 8 * D).rearrange("p (r n) -> p r n", r=8)
        F1 = M0 + 8 * D
        kT = part(F1, 2 * D).rearrange("p (r m k) -> p r m k", r=2, m=PAIRS)
        F2 = F1 + 2 * D
        suf = part(F2, DB * NPAGES * FH).rearrange("p (b g h) -> p b g h", b=DB, g=NPAGES)
        assert F2 + DB * NPAGES * FH <= 17664
        pT = part(M0 + 4 * D, 2 * PT * SEQ).rearrange("p (r k q) -> p r k q", r=2, k=PT)
        k_rows = part(M0, PT * D).rearrange("p (t n) -> p t n", t=PT)
        probs = part(F1, 2 * SEQ).rearrange("p (r k) -> p r k", r=2)
        k_rows_s = part(F1 + 2 * SEQ, D, NS)
        yflat = yT[:].rearrange("p k t -> p (k t)")
        LFN = DB * NPAGES * FH
        lf = yflat[:, 0:LFN].rearrange("p (b g h) -> p b g h", b=DB, g=NPAGES)
        later = yflat[:, LFN:2 * LFN].rearrange("p (b g h) -> p b g h", b=DB, g=NPAGES)
        HI = FH * DS
        z = yflat[:, LFN:LFN + (NPAGES + 1) * HI].rearrange("p (g n) -> p g n", g=NPAGES + 1)
        zsm = yflat[:, LFN + (NPAGES + 1) * HI:]
        mx, sm, rc = (zsm[:, i * HI:(i + 1) * HI] for i in range(3))
        m64, dg = zsm[0:HI, 3 * HI:3 * HI + 1], zsm[0:HI, 3 * HI + 4:3 * HI + 4 + HI]
        mflat = big[:, 2 * KD:KF, :].rearrange("p k t -> p (k t)")
        at_m = [0]

        def small_part(n, rows=P):
            at_m[0] += n
            assert at_m[0] <= mflat.shape[1]
            return mflat[0:rows, at_m[0] - n:at_m[0]]

        logf = small_part(TOK, FH)
        ncum = small_part(SEQ, FH)
        cumq = small_part(PT * FH).rearrange("p (t h) -> p t h", t=PT)
        lnat = small_part((PT + 1) * FH).rearrange("p (t h) -> p t h", t=PT + 1)
        dn = small_part(DB * HI, NS)
        rb = small_part(DB * HI)
        dt_ = small_part(DB * FH, NS)
        totn = small_part(DB * FH)
        sufn = small_part(FH, NS)
        qblk = small_part(DB * PAIRS * 2 * DS).rearrange("p (b m e i) -> p b m e i", b=DB, m=PAIRS, e=2)
        l_e, l_u, l_m = (sil[0:FH, 0, :], sil[0:FH, 1, :], root[0:FH, :])
        nmax, rsum = small_part(4), small_part(4)
        HB = DB // 2
        SR = HB * CB
        st_rows = part(0, 2 * D, SR).rearrange("p (r n) -> p r n", r=2)
        cs_rows = part(2 * D, 2 * D, SR).rearrange("p (r n) -> p r n", r=2)
        cp_rows = part(4 * D, D, CB)
        st_new = part(5 * D, KD * DB * CB).rearrange("p (k b w) -> p k b w", k=KD, b=DB)
        bflat = big[:].rearrange("p k t -> p (k t)")
        EP, ES = CB + SEQ, CB + DS
        ext_p = bflat[:, 0:KD * EP].rearrange("p (k t) -> p k t", k=KD)
        ext_s = bflat[:, KD * EP:KD * (EP + DB * ES)].rearrange("p (k b t) -> p k b t", k=KD, b=DB)
        dw0 = KD * (EP + DB * ES)
        dw = bflat[:, dw0:dw0 + KD * TOK].rearrange("p (k t) -> p k t", k=KD)

        setup_in = sem("setup_in")
        vec_in = sem("vec_in")
        w_in = [sem(f"w_in{i}") for i in range(RING)]
        const_made = sem("const_made")
        blk_done = sem("blk_done")
        acc_full = [sem(f"acc_full{i}") for i in range(8)]
        acc_out = [sem(f"acc_out{i}") for i in range(8)]
        sq_done = sem("sq_done")
        rstd_done = sem("rstd_done")
        z_done = sem("z_done")
        x_done = sem("x_done")
        h_done = sem("h_done")
        o_done = sem("o_done")
        s_act = sem("s_act")
        s_dve = sem("s_dve")
        abs_done = sem("abs_done")
        soft_done = sem("soft_done")
        cum_done = sem("cum_done")
        decay_done = sem("decay_done")
        diff_done = sem("diff_done")
        kdec_done = sem("kdec_done")
        keys_done = sem("keys_done")
        state_out = sem("state_out")
        rows_in = sem("rows_in")
        ext_done = sem("ext_done")
        packed = sem("packed")
        conv_done = sem("conv_done")
        mean_done = sem("mean_done")
        scaled_done = sem("scaled_done")
        silu_done = sem("silu_done")
        pt_in = sem("pt_in")
        lf_in = sem("lf_in")
        pages_in = [sem(f"pages_in{i}") for i in range(8)]
        nat_out = sem("nat_out")
        fabs_done = sem("fabs_done")
        fexp_done = sem("fexp_done")
        fln_done = sem("fln_done")
        fu_done = sem("fu_done")
        logf_done = sem("logf_done")
        dmat_done = sem("dmat_done")
        later_done = sem("later_done")
        qblk_done = sem("qblk_done")
        pmax_done = sem("pmax_done")
        pexp_done = sem("pexp_done")
        p_done = sem("p_done")
        pv_full = sem("pv_full")
        pv_out = sem("pv_out")
        page_turned = sem("page_turned")
        kt_out = sem("kt_out")
        v_used = sem("v_used")
        zx_done = sem("zx_done")
        zexp_done = sem("zexp_done")
        mx_done = sem("mx_done")
        dg_done = sem("dg_done")
        sm_done = sem("sm_done")
        kdb_done = sem("kdb_done")
        out_in = sem("out_in")
        st_in = [sem("st_in0"), sem("st_in1")]
        st_out = [sem("st_out0"), sem("st_out1")]

        VROWS = [("norm", norm_g.rearrange("l w (k p) -> (l w k) p", p=P))]
        small = [("bg", gla_bg), ("gn", gla_gn), ("b1", conv_b1), ("bdw", conv_bdw), ("lng", conv_ln_g),
                 ("lnb", conv_ln_b), ("b2", conv_b2)]
        col, at = {"norm": 0}, P
        for name, v in small:
            VROWS.append((name, v.rearrange("l (k p) -> (l k) p", p=P)))
            col[name] = at
            at += v.shape[0] * v.shape[1] // P
        col["wdw"] = at = 2 * P
        taps = conv_wdw.rearrange("l w (k p) -> (l w k) p", p=P)
        VN = [P, sum(v.shape[0] * v.shape[1] for _, v in small) // P, P, CW * KD - P]
        vrow = [big[:, 5 * 2, i * P:(i + 1) * P] for i in range(4)]

        def vcol(name, k=0):
            c = col[name] + k
            return vecs[:, c:c + 1]

        def gcol(layer, which, k):
            return vcol("norm", (layer * 4 + which) * KD + k)

        xin = big[:, 0:10, :].rearrange("p u t -> p (u t)")[:, 0:(PT + 1) * D].rearrange("p (t n) -> p t n", t=PT + 1)

        SETUP_DMAS = 2 + 1 + len(small) + 2

        def w_view(w):
            return w.rearrange("(k p) n -> p k n", p=P)

        outputs = []
        N_CONST = 24
        VEC_FOX = 64

        block = ctx.enter_context(nc.Block())

        @block.sync
        def _(sp):
            t = Tally()
            def load(view, ktiles, k0, m, slot, n):
                if n is not None:
                    sp.wait_ge(blk_done, n - (RING - 1))
                sp.dma_start(ring[:, slot, 0:ktiles * P].rearrange("p (k n) -> p k n", k=ktiles),
                             view[:, k0:k0 + ktiles, ds(m * P, P)]).then_inc(w_in[slot], 16)

            def load_plain(view, tiles):
                if t.blk == 0:
                    for j in range(RING):
                        load(view, KD, 0, j, j, None)
                    assert tiles == RING
                elif tiles == RING:
                    for j in range(RING):
                        load(view, KD, 0, j, j, t.blk + j)
                else:
                    with sp.Fori(0, tiles // RING) as it:
                        for j in range(RING):
                            load(view, KD, 0, it * RING + j, j, it * RING + (t.blk + j))
                t.blocks(tiles)

            def load_pairs(va, vb, tiles):
                with sp.Fori(0, tiles // 2) as it:
                    for j in range(RING):
                        load(va if j % 2 == 0 else vb, KD, 0, it * 2 + j // 2, j, it * RING + (t.blk + j))
                t.blocks(2 * tiles)

            def store(dst, src):
                sp.dma_start(dst, src).then_inc(out_in, 16)
                outputs.append(dst)

            sp.dma_start(xin[:, 0:PT, :], x_prompt[0].rearrange("(t p) n -> p t n", p=P)).then_inc(setup_in, 16)
            sp.dma_start(xin[0:NS, PT, :], x_sample.rearrange("b s n -> (b s) n")).then_inc(setup_in, 16)
            sp.dma_start(vrow[0], VROWS[0][1]).then_inc(setup_in, 16)
            for name, v in VROWS[1:]:
                r = col[name] - P
                sp.dma_start(vrow[1][r:r + v.shape[0], :], v).then_inc(setup_in, 16)
            sp.dma_start(vrow[2], taps[0:P]).then_inc(setup_in, 16)
            sp.dma_start(vrow[3][0:VN[3], :], taps[P:CW * KD]).then_inc(setup_in, 16)

            def gla(j):
                if j > 0:
                    sp.wait_ge(blk_done, t.blk)
                sp.dma_start(wg1_sb[:], gla_wg1[j].rearrange("(k p) r -> p k r", p=P)).then_inc(vec_in, 16)
                sp.dma_start(wg2_sb[:], gla_wg2[j]).then_inc(vec_in, 16)
                load_plain(w_view(gla_wq[j]), GH)
                load_plain(w_view(gla_wk[j]), GH)
                load_plain(w_view(gla_wr[j]), KD)
                load_plain(w_view(gla_wv[j]), KD)
                for g in range(DB // 2):
                    if g >= 2:
                        sp.wait_ge(st_out[g % 2], 16 * (g // 2 + 2 * j))
                    elif j > 0:
                        sp.wait_ge(st_out[g % 2], 16 * 2 * j)
                    sp.dma_start(st[:, g % 2], state_gla[j, 2 * g:2 * g + 2].rearrange("b h k v -> k b h v"))\
                      .then_inc(st_in[g % 2], 16)
                load_plain(w_view(gla_wo[j]), KD)
                sp.dma_start(gla_sp[j, 0].rearrange("h k v -> k h v"), S).then_inc(state_out, 16)

            def ffn(i):
                load_pairs(w_view(ffn_w1[i]), w_view(ffn_w3[i]), KF)
                w2 = w_view(ffn_w2[i])
                with sp.Fori(0, KD // 4) as it:
                    for b in range(8):
                        load(w2, KF2, (b % 2) * KF2, it * 4 + b // 2, b % RING, it * 8 + (t.blk + b))
                t.blocks(2 * KD)

            def fox():
                sp.wait_ge(blk_done, t.blk)
                sp.dma_start(wg1_sb[:], fox_wf[0].rearrange("(k p) r -> p k r", p=P)).then_inc(vec_in, 16)
                sp.dma_start(fbias[:], fox_bf.rearrange("a h -> h a")).then_inc(vec_in, 16)
                sp.dma_start(pt_sb[:], page_table.rearrange("(a b) g -> a (b g)", a=1)).then_inc(pt_in, 16)
                load_plain(w_view(fox_wq[0]), KD)
                load_plain(w_view(fox_wk[0]), KD)

                sp.wait_ge(pt_in, 16)
                load_plain(w_view(fox_wv[0]), KD)
                sp.wait_ge(nat_out, 16 * (PT + 5))
                sp.wait_ge(pv_out, PAIRS)
                sp.nop()

                regs = [sp.alloc_register(f"page{g}") for g in range(NPAGES)]

                def page_numbers(b):
                    sp.load(regs, pt_sb[0:1, ds(b * NPAGES, NPAGES)])
                    return [sp.snap(r, min_val=0, max_val=NPOOL - 1) for r in regs]

                def load_page(numbers, s):
                    cache = cache_k if s < NPAGES else cache_v
                    sp.dma_start(pages[:, s % 8, :],
                                 cache[0, ds(numbers[s % NPAGES], 1)].rearrange("a p h d -> p (a h d)"))\
                      .then_inc(pages_in[s % 8], 16)

                def first_pages(b, numbers, reuse):
                    for s in range(8):
                        if reuse:
                            sp.wait_ge(v_used, b * NPAGES + (s + 24 - NPAGES + 1 - NPAGES))
                        load_page(numbers, s)

                def other_pages(b, numbers):
                    for s in range(8, 2 * NPAGES):
                        if s - 8 < NPAGES:
                            sp.wait_ge(page_turned, b * NPAGES + (s - 8 + 1))
                        else:
                            sp.wait_ge(v_used, b * NPAGES + (s - 8 - NPAGES + 1))
                        load_page(numbers, s)

                first_pages(0, page_numbers(0), False)
                with sp.Fori(0, DB - 1) as b:
                    other_pages(b, page_numbers(b))
                    first_pages(b + 1, page_numbers(b + 1), True)
                other_pages(DB - 1, page_numbers(DB - 1))
                load_plain(w_view(fox_wo[0]), KD)

            def conv():
                sp.wait_ge(blk_done, t.blk - 3)
                sp.dma_start(st_rows, state_conv[0].rearrange("(r b) w n -> (b w) r n", r=2)).then_inc(rows_in, 16)
                w1 = w_view(conv_w1[0])
                load_pairs(w1[:, :, 0:D], w1[:, :, D:2 * D], KD)
                load_plain(w_view(conv_w2[0]), KD)

            for i in range(depth):
                kind, j = i % 3, i // 3
                if kind == 0:
                    gla(j)
                elif kind == 1:
                    fox()
                else:
                    conv()
                ffn(i)

        @block.gpsimd
        def _(pool):
            made = [0]

            def made_by(ins):
                made[0] += 1
                ins.then_inc(const_made, 1)

            def select(out, pattern, base, mult, fill, compare=ALU.is_ge):
                pool.wait_ge(const_made, made[0])
                made_by(pool.affine_select(out=out, in_=out, compare_op=compare, fill=fill, base=base,
                                           pattern=pattern, channel_multiplier=mult))

            made_by(pool.memset(ident[:], 0.0))
            select(ident[:], [[-1, P]], 0, 1, 1.0, ALU.not_equal)
            made_by(pool.memset(ones[:], 1.0))
            made_by(pool.memset(epsb[:, 0:1], RMS_EPS))
            made_by(pool.memset(epsb[:, 1:2], LN_EPS))
            made_by(pool.memset(strict[:], 1.0))
            select(strict[:], [[-1, P]], -1, 1, 0.0)
            made_by(pool.memset(causal[:], 0.0))
            select(causal[:], [[-1, P]], 0, 1, NEG)
            made_by(pool.memset(reset[:], 1.0))
            pool.wait_ge(const_made, made[0])
            made_by(pool.memset(reset[:, 0:SEQ:GLA_CHUNK], 0.0))
            made_by(pool.memset(reset[:, SEQ:TOK:DS], 0.0))
            made_by(pool.memset(m_chunk[:], 1.0))
            mc = m_chunk[:].rearrange("p (c t) -> p c t", t=GLA_CHUNK)
            select(mc, [[-GLA_CHUNK, P // GLA_CHUNK], [0, GLA_CHUNK]], 0, 1, 0.0)
            select(mc, [[GLA_CHUNK, P // GLA_CHUNK], [1, GLA_CHUNK]], 0, -1, 0.0)
            made_by(pool.memset(m_le[:], 1.0))
            select(m_le[:], [[-DS, DB], [0, DS]], 0, 1, 0.0)
            select(m_le[:], [[DS, DB], [1, DS]], 0, -1, 0.0)
            made_by(pool.memset(m_gt[:], 1.0))
            select(m_gt[:], [[-DS, DB], [-1, DS]], -1, 1, 0.0)
            select(m_gt[:], [[DS, DB], [0, DS]], DS - 1, -1, 0.0)
            made_by(pool.memset(m_in[:], 1.0))
            select(m_in[:], [[-DS, DB]], 0, 1, 0.0)
            select(m_in[:], [[DS, DB]], DS - 1, -1, 0.0)
            assert made[0] == N_CONST, made[0]

            n_post = [0]
            for n in range(2 * depth):
                if n == 2:
                    pool.wait_ge(x_done, 2 * KD)
                    pool.wait_ge(pt_in, 16)
                    with pool.Fori(0, DB) as b:
                        for g in range(NPAGES):
                            page = pool.value_load(pt_sb[0:1, ds(b * NPAGES + g, 1)], min_val=0, max_val=NPOOL - 1)
                            pool.dma_start(lf[:, ds(b, 1), g, :].rearrange("p a h -> p (a h)"),
                                           cache_lf[0, ds(page, 1)].rearrange("a p h -> p (a h)")).then_inc(lf_in, 16)
                for k in range(KD):
                    pool.wait_ge(z_done, KD * n_post[0] + k + 1)
                    pool.tensor_tensor(xT[:, k, :], xT[:, k, :], yT[:, k, :], ALU.add).then_inc(x_done, 1)
                n_post[0] += 1

        @block.tensor
        def _(pe):
            t = Tally()
            def block_mm(slot, bank, ktiles, k0, rhs, start, stop):
                for k in range(ktiles):
                    for h in range(2):
                        last = pe.matmul(acc[:, bank + h, 0:HALF], ring[:, slot, k * P:(k + 1) * P],
                                         rhs[:, k0 + k, h * HALF:(h + 1) * HALF],
                                         start=start and k == 0, stop=stop and k == ktiles - 1)
                last.then_inc(blk_done, 1)

            def project(tiles, first=False):
                b0, o = t.blk, list(t.out)

                def body(it):
                    for j in range(RING):
                        pe.wait_ge(w_in[j], 16 * (it + (b0 // RING + 1)))
                        pe.wait_ge(acc_out[2 * j], it + o[2 * j])
                        block_mm(j, 2 * j, KD, 0, hT, True, True)

                if tiles == RING:
                    body(0)
                else:
                    with pe.Fori(0, tiles // RING) as it:
                        body(it)
                t.blocks(tiles, uses=tiles // RING)

            def project_tokens(tiles):
                b0, o = t.blk, list(t.out)
                with pe.Fori(0, tiles // RING) as it:
                    for j in range(RING):
                        pe.wait_ge(w_in[j], 16 * (it + (b0 // RING + 1)))
                        pe.wait_ge(acc_out[2 * j], it + o[2 * j])
                        for tt in range(PT + 1):
                            n = P if tt < PT else NS
                            for k in range(KD):
                                last = pe.matmul(acc[0:n, 2 * j + tt // PT, (tt % PT) * P:(tt % PT + 1) * P],
                                                 hT[:, k, tt * P:tt * P + n], ring[:, j, k * P:(k + 1) * P],
                                                 start=(k == 0), stop=(k == KD - 1))
                        last.then_inc(blk_done, 1)
                t.blocks(tiles, uses=tiles // RING)

            def wait_banks(banks=range(8)):
                for b in banks:
                    if t.out[b]:
                        pe.wait_ge(acc_out[b], t.out[b])

            def norm_sum(squares, evacuated):
                pe.wait_ge(acc_out[0], t.out[0])
                for k in range(KD):
                    if evacuated:
                        pe.wait_ge(acc_out[2 * (k % 4)], t.out[2 * (k % 4)] - 1 + k // 4)
                    else:
                        pe.wait_ge(sq_done, t.sq + k + 1)
                    for h in range(2):
                        last = pe.matmul(acc[:, h, 0:HALF], ones[:], squares[:, k, h * HALF:(h + 1) * HALF],
                                         start=(k == 0), stop=(k == KD - 1))
                last.then_inc(acc_full[0], 1)
                if not evacuated:
                    t.sq += KD
                t.use(0)

            def h_ready():
                t.h += KD
                pe.wait_ge(h_done, t.h)

            def o_ready():
                t.o += KD
                pe.wait_ge(o_done, t.o)

            pe.wait_ge(const_made, 2)
            pe.wait_ge(setup_in, 16 * SETUP_DMAS)
            for k in range(KD):
                bank = 2 * (k % 4)
                if k >= 4:
                    pe.wait_ge(acc_out[bank], 1)
                for tt in range(PT):
                    pe.transpose(acc[:, bank, tt * P:(tt + 1) * P], xin[:, tt, k * P:(k + 1) * P], ident[:])
                pe.transpose(acc[:, bank + 1, 0:NS], xin[0:NS, PT, k * P:(k + 1) * P], ident[0:NS, 0:NS])\
                  .then_inc(acc_full[bank], 1)
                t.use(bank)
            pe.wait_ge(acc_out[0], t.out[0])
            for g in range(4):
                last = pe.transpose(acc[:, 0, g * P:g * P + VN[g]], vrow[g][0:VN[g], :], ident[0:VN[g], 0:VN[g]])
            last.then_inc(acc_full[0], 1)
            t.use(0)
            pe.wait_ge(const_made, N_CONST)

            def gla(j):
                norm_sum(hT, False)
                h_ready()
                project(GH)
                project(GH)
                pe.wait_ge(vec_in, 32 * (j + 1) + (32 if j else 0))
                pe.wait_ge(acc_out[0], t.out[0])
                for k in range(KD):
                    for h in range(2):
                        last = pe.matmul(acc[0:RANK, h, 0:HALF], wg1_sb[:, k, :], hT[:, k, h * HALF:(h + 1) * HALF],
                                         start=(k == 0), stop=(k == KD - 1))
                last.then_inc(acc_full[0], 1)
                t.use(0)
                pe.wait_ge(acc_out[0], t.out[0])
                for m in range(GH):
                    bank = 2 * ((m + 1) % 4)
                    pe.wait_ge(acc_out[bank], t.out[bank])
                    for h in range(2):
                        last = pe.matmul(acc[:, bank + h, 0:HALF], wg2_sb[:, m * P:(m + 1) * P],
                                         lowr[:, h * HALF:(h + 1) * HALF], start=True, stop=True)
                    last.then_inc(acc_full[bank], 1)
                    t.use(bank)
                project(KD)
                project_tokens(KD)

                wait_banks()
                pe.wait_ge(keys_done, j + 1)
                for tt in range(PT + 1):
                    n = P if tt < PT else NS
                    bank = 4 * (tt % 2)
                    pe.wait_ge(acc_out[bank], t.out[bank])
                    pe.wait_ge(acc_out[bank + 1], t.out[bank + 1])
                    for h in range(GH):
                        last = pe.transpose(acc[0:n, bank, h * DK:(h + 1) * DK], big[:, 4 + h, tt * P:tt * P + n],
                                            ident[:])
                    last.then_inc(acc_full[bank], 1)
                    for h in range(GH):
                        last = pe.matmul(acc[0:n, bank + 1, h * P:h * P + n], yT[:, h, tt * P:tt * P + n],
                                         big[:, h, tt * P:tt * P + n], start=True, stop=True)
                    last.then_inc(acc_full[bank + 1], 1)
                    t.use(bank)
                    t.use(bank + 1)
                wait_banks((0, 1, 4, 5))
                for c in range(NCH):
                    tt, r0 = c // 2, GLA_CHUNK * (c % 2)
                    t0 = c * GLA_CHUNK
                    ob, ub = (0, 1)[c % 2], (2, 4)[c % 2]
                    pe.wait_ge(acc_out[ub], t.out[ub])
                    for h in range(GH):
                        last = pe.matmul(acc[:, ub + h // 2, (h % 2) * DV:(h % 2 + 1) * DV],
                                         kd_nat[r0:r0 + GLA_CHUNK, tt, h, :],
                                         v_nat[r0:r0 + GLA_CHUNK, tt, h * DV:(h + 1) * DV], start=True, stop=True)
                    last.then_inc(acc_full[ub], 1)
                    t.use(ub)
                    pe.wait_ge(acc_out[ob], t.out[ob])
                    if c > 0:
                        prev = (2, 4)[(c - 1) % 2]
                        pe.wait_ge(acc_out[prev], t.out[prev])
                    for h in range(GH):
                        for v in range(VH):
                            u = h * VH + v
                            dst = acc[:, ob, u * GLA_CHUNK:(u + 1) * GLA_CHUNK]
                            last = pe.matmul(dst, v_nat[:, tt, u * P:(u + 1) * P],
                                             att[:, tt, h, r0:r0 + GLA_CHUNK], start=True, stop=(c == 0))
                            if c > 0:
                                last = pe.matmul(dst, S[:, h, v * P:(v + 1) * P],
                                                 big[:, h, t0:t0 + GLA_CHUNK], start=False, stop=True)
                    last.then_inc(acc_full[ob], 1)
                    t.use(ob)
                pe.wait_ge(acc_out[0], t.out[0])
                for g in range(DB // 2):
                    pe.wait_ge(st_in[g % 2], 16 * (g // 2 + 1 + 2 * j))
                    if g == 0:
                        for u in range(KD):
                            pe.matmul(acc[:, 0, u * NS:(u + 1) * NS], v_nat[0:NS, PT, u * P:(u + 1) * P],
                                      att_s[:, u // VH, :], start=(u == 0), stop=False, skip_group_check=True)
                    for bb in range(2):
                        b = 2 * g + bb
                        for u in range(KD):
                            h, v = u // VH, u % VH
                            last = pe.matmul(acc[:, 0, u * NS + b * DS:u * NS + (b + 1) * DS],
                                             st[:, g % 2, bb, h, v * P:(v + 1) * P],
                                             big[:, h, SEQ + b * DS:SEQ + (b + 1) * DS],
                                             start=False, stop=(g == DB // 2 - 1), skip_group_check=True)
                        if b == DB - 1:
                            last.then_inc(acc_full[0], 1)
                            t.use(0)
                        ub = (2, 4)[b % 2]
                        pe.wait_ge(acc_out[ub], t.out[ub])
                        pe.wait_ge(kdb_done, DB * j + b + 1)
                        for h in range(GH):
                            last = pe.matmul(acc[:, ub + h // 2, (h % 2) * DV:(h % 2 + 1) * DV], kd_b[:, b % 2, h, :],
                                             v_nat[0:NS, PT, h * DV:(h + 1) * DV], start=True, stop=True)
                        last.then_inc(acc_full[ub], 1)
                        t.use(ub)
                wait_banks()
                for h in range(GH):
                    for v in range(VH):
                        pe.wait_ge(sq_done, t.sq + h * VH + v + 1)
                        for q in range(2):
                            last = pe.matmul(acc[:, 2 * h + q, 0:HALF], ones[:],
                                             yT[:, h * VH + v, q * HALF:(q + 1) * HALF],
                                             start=(v == 0), stop=(v == VH - 1))
                    last.then_inc(acc_full[2 * h], 1)
                    t.use(2 * h)
                t.sq += KD
                o_ready()
                project(KD)
                norm_sum(big, True)

            def ffn():
                norm_sum(hT, False)
                h_ready()
                b0, o = t.blk, list(t.out)
                with pe.Fori(0, KF // 2) as it:
                    for j in range(RING):
                        pe.wait_ge(w_in[j], 16 * (it + (b0 // RING + 1)))
                        pe.wait_ge(acc_out[2 * j], it + o[2 * j])
                        block_mm(j, 2 * j, KD, 0, hT, True, True)
                t.blocks(2 * KF, uses=KF // 2)
                b0, o = t.blk, list(t.out)
                with pe.Fori(0, KD // 4) as it:
                    for b in range(8):
                        j, bank = b % RING, b // 2 * 2
                        pe.wait_ge(w_in[j], 16 * (it * 2 + (b0 // RING + b // RING + 1)))
                        if b == 0:
                            pe.wait_ge(acc_out[2], o[2])
                            pe.wait_ge(acc_out[6], o[6])
                        if b % 2 == 0:
                            pe.wait_ge(acc_out[bank], it + o[bank])
                        block_mm(j, bank, KF2, (b % 2) * KF2, big, b % 2 == 0, b % 2 == 1)
                t.blocks(2 * KD, uses=KD // 4)
                norm_sum(hT, True)

            def prompt_attention():
                items = [(h, q) for h in range(FH) for q in range(PT)]
                due = []
                for i in range(len(items) + 3):
                    if i < len(items):
                        h, q = items[i]
                        r0, bank = DH * (h % 2), i % 2
                        if i >= 2:
                            pe.wait_ge(acc_out[bank], t.out[bank])
                        n = (q + 1) * P
                        pe.matmul(acc[:, bank, 0:n], big[r0:r0 + DH, h // 2, q * P:(q + 1) * P],
                                  big[r0:r0 + DH, KD + h // 2, 0:n], start=True, stop=False)
                        pe.matmul(acc[:, bank, 0:n], ident[0:FH, h:h + 1].to_broadcast([FH, P]), ncum[:, 0:n],
                                  start=False, stop=True).then_inc(acc_full[bank], 1)
                        t.use(bank)
                    for h in due:
                        pe.wait_ge(acc_out[3], t.out[3])
                        r0, bank = DH * (h % 2), 4 + (h // 2) % 2
                        if h % 2 == 0 and h >= 4:
                            pe.wait_ge(pv_out, h // 2 - 1)
                        for k in range(PT):
                            last = pe.matmul(acc[r0:r0 + DH, bank, k * P:SEQ], v_nat[:, k, h * DH:(h + 1) * DH],
                                             pT[:, h % 2, k, k * P:SEQ], start=(k == 0), stop=(k == PT - 1))
                        last.then_inc(pv_full, 1)
                    due = []
                    if 2 <= i < len(items) + 2:
                        h, q = items[i - 2]
                        bank = 2 + (i % 2)
                        pe.wait_ge(p_done, i - 1)
                        pe.wait_ge(acc_out[bank], t.out[bank])
                        for k in range(q + 1):
                            last = pe.transpose(acc[:, bank, k * P:(k + 1) * P], probs[:, i % 2, k * P:(k + 1) * P], ident[:])
                        last.then_inc(acc_full[bank], 1)
                        t.use(bank)
                        if q == PT - 1:
                            due = [h]

            def sample_attention():
                o = list(t.out)
                with pe.Fori(0, DB) as b:
                    def scores(g):
                        pe.wait_ge(kt_out, b * NPAGES + (g + 1))
                        if g % 8 == 0:
                            pe.wait_ge(acc_out[4 + g // 8], b + o[4 + g // 8])
                        for m in range(PAIRS):
                            at = (g % 8) * HI + m * 2 * DS
                            last = pe.matmul(acc[:, 4 + g // 8, at:at + 2 * DS], kT[:, g % 2, m, :],
                                             qblk[:, ds(b, 1), m].rearrange("p a e i -> p (a e i)"), start=True, stop=True)
                        if g % 8 == 7:
                            last.then_inc(acc_full[4 + g // 8], 1)

                    pe.wait_ge(acc_out[6], b * 4 + o[6])
                    for m in range(PAIRS):
                        last = pe.matmul(acc[0:NS, 6, m * 2 * DS:(m + 1) * 2 * DS], big[:, KD + m, SEQ:TOK],
                                         qblk[:, ds(b, 1), m].rearrange("p a e i -> p (a e i)"), start=True, stop=True)
                    last.then_inc(acc_full[6], 1)
                    for g in range(NPAGES):
                        bank = 2 * (g % 2)
                        pe.wait_ge(pages_in[g % 8], b * 64 + 16 * (g // 8 + 1))
                        if g >= 2:
                            pe.wait_ge(kt_out, b * NPAGES + (g - 1))
                        for m in range(PAIRS):
                            last = pe.transpose(acc[:, bank + m // 4, (m % 4) * P:(m % 4 + 1) * P],
                                                pages[:, g % 8, m * P:(m + 1) * P], ident[:])
                        last.then_inc(page_turned, 1)
                        if g >= 1:
                            scores(g - 1)
                    scores(NPAGES - 1)
                    pe.wait_ge(mx_done, b + 1)
                    pe.wait_ge(acc_out[6], b * 4 + (o[6] + 1))
                    pe.transpose(acc[:, 6, P:2 * P], zsm[:, 0:2 * HI], ident[:]).then_inc(acc_full[6], 1)
                    pe.wait_ge(dg_done, b + 1)
                    pe.wait_ge(acc_out[6], b * 4 + (o[6] + 2))
                    pe.matmul(acc[:, 6, 0:HI], ones[0:HI, :], dg, start=True, stop=True).then_inc(acc_full[6], 1)
                    pe.wait_ge(zexp_done, b * 2 + 1)
                    pe.wait_ge(acc_out[7], b + o[7])
                    for m in range(PAIRS):
                        pe.matmul(acc[:, 7, m * 2 * DS:(m + 1) * 2 * DS], v_nat[0:NS, PT, m * P:(m + 1) * P],
                                  z[0:NS, NPAGES, m * 2 * DS:(m + 1) * 2 * DS], start=(m == 0), stop=False,
                                  skip_group_check=True)
                    pe.wait_ge(zexp_done, b * 2 + 2)
                    for g in range(NPAGES):
                        slot = (NPAGES + g) % 8
                        pe.wait_ge(pages_in[slot], b * 64 + 16 * ((NPAGES + g) // 8 + 1))
                        for m in range(PAIRS):
                            last = pe.matmul(acc[:, 7, m * 2 * DS:(m + 1) * 2 * DS], pages[:, slot, m * P:(m + 1) * P],
                                             z[:, g, m * 2 * DS:(m + 1) * 2 * DS], start=False, stop=(g == NPAGES - 1),
                                             skip_group_check=True)
                        last.then_inc(v_used, 1)
                        if g == 7:
                            pe.wait_ge(sm_done, b + 1)
                            pe.wait_ge(acc_out[6], b * 4 + (o[6] + 3))
                            pe.matmul(acc[:, 6, 0:HI], ones[:], sm, start=True, stop=True).then_inc(acc_full[6], 1)
                for bank, n in ((4, 1), (5, 1), (6, 4)):
                    t.use(bank, DB * n)
                t.out[7] += DB

            def fox():
                norm_sum(hT, False)
                h_ready()
                project(KD)
                project(KD)
                pe.wait_ge(vec_in, VEC_FOX)
                pe.wait_ge(acc_out[0], t.out[0])
                for k in range(KD):
                    for h in range(2):
                        last = pe.matmul(acc[0:FH, h, 0:HALF], wg1_sb[:, k, :], hT[:, k, h * HALF:(h + 1) * HALF],
                                         start=(k == 0), stop=(k == KD - 1))
                last.then_inc(acc_full[0], 1)
                t.use(0)
                project_tokens(KD)
                wait_banks()
                for tt in range(PT + 1):
                    n = P if tt < PT else NS
                    bank = 2 * (tt % 4)
                    pe.wait_ge(acc_out[bank], t.out[bank])
                    for k in range(KD):
                        last = pe.transpose(acc[0:n, bank + k // 4, (k % 4) * P:(k % 4 + 1) * P],
                                            big[:, KD + k, tt * P:tt * P + n], ident[:])
                    last.then_inc(acc_full[bank], 1)
                    t.use(bank)
                pe.wait_ge(logf_done, 1)
                pe.wait_ge(acc_out[0], t.out[0])
                for tt in range(PT + 1):
                    n = P if tt < PT else NS
                    last = pe.transpose(acc[0:n, 0, tt * FH:(tt + 1) * FH], logf[:, tt * P:tt * P + n], ident[0:FH, 0:FH])
                last.then_inc(acc_full[0], 1)
                t.use(0)
                for tt in range(PT):
                    last = pe.transpose(acc[:, 1, tt * FH:(tt + 1) * FH], ncum[:, tt * P:(tt + 1) * P], ident[0:FH, 0:FH])
                last.then_inc(acc_full[1], 1)
                t.use(1)
                pe.wait_ge(dmat_done, 1)
                wait_banks((2, 4))
                pe.matmul(acc[:, 2, 0:DB * HI], ones[0:NS, :], dn, start=True, stop=True).then_inc(acc_full[2], 1)
                t.use(2)
                pe.matmul(acc[:, 4, 0:DB * FH], ones[0:NS, :], dt_, start=True, stop=True)
                pe.matmul(acc[0:NS, 4, DB * FH:(DB + 1) * FH], m_gt[:].rearrange("p b i -> p (b i)"), lnat[0:NS, PT, :],
                          start=True, stop=True).then_inc(acc_full[4], 1)
                t.use(4)
                wait_banks()
                prompt_attention()
                wait_banks((0, 1, 2, 3))
                pe.wait_ge(pv_out, PAIRS)
                pe.wait_ge(later_done, 1)
                flat = [a.rearrange("p b g h -> p (b g h)") for a in (lf, later)]
                for c in range(LFN // 512):
                    bank = 2 * (c % 4)
                    pe.wait_ge(acc_out[bank], t.out[bank])
                    pe.matmul(acc[:, bank, :], strict[:], flat[0][:, c * 512:(c + 1) * 512], start=True, stop=False)
                    pe.matmul(acc[:, bank, :], ones[:], flat[1][:, c * 512:(c + 1) * 512], start=False, stop=True)\
                      .then_inc(acc_full[bank], 1)
                    t.use(bank)
                wait_banks()
                pe.wait_ge(qblk_done, 1)
                sample_attention()
                o_ready()
                wait_banks()
                project(KD)
                norm_sum(big, True)

            def conv():
                norm_sum(hT, False)
                pe.wait_ge(rows_in, 16)
                for k in range(KD):
                    bank = 2 * (k % 4)
                    pe.wait_ge(acc_out[bank], t.out[bank])
                    for r in range(2):
                        last = pe.transpose(acc[:, bank, r * SR:(r + 1) * SR], st_rows[:, r, k * P:(k + 1) * P],
                                            ident[0:SR, 0:SR])
                    last.then_inc(acc_full[bank], 1)
                    t.use(bank)
                h_ready()
                b0, o = t.blk, list(t.out)
                with pe.Fori(0, KD // 2) as it:
                    for j in range(RING):
                        pe.wait_ge(w_in[j], 16 * (it + (b0 // RING + 1)))
                        pe.wait_ge(acc_out[2 * j], it + o[2 * j])
                        block_mm(j, 2 * j, KD, 0, hT, True, True)
                t.blocks(2 * KD, uses=KD // 2)
                wait_banks()
                for k in range(KD):
                    pe.wait_ge(conv_done, k // 2 + 1)
                    for h in range(2):
                        last = pe.matmul(acc[:, h, 0:HALF], ones[:], dw[:, k, h * HALF:(h + 1) * HALF],
                                         start=(k == 0), stop=(k == KD - 1))
                last.then_inc(acc_full[0], 1)
                t.use(0)
                for k in range(KD):
                    last = pe.transpose(acc[0:CB, 2 + k // 4, (k % 4) * P:(k % 4 + 1) * P], ext_p[:, k, SEQ:EP], ident[:])
                last.then_inc(acc_full[2], 1)
                t.use(2)
                pe.wait_ge(packed, 1)
                for r in range(2):
                    for k in range(KD):
                        last = pe.transpose(acc[0:SR, 4 + 2 * r + k // 4, (k % 4) * P:(k % 4 + 1) * P],
                                            st_new[:, k, r * HB:(r + 1) * HB, :].rearrange("p b w -> p (b w)"), ident[:])
                    last.then_inc(acc_full[4 + 2 * r], 1)
                    t.use(4 + 2 * r)
                norm_sum(hT, False)
                pe.wait_ge(silu_done, KD)
                wait_banks()
                project(KD)
                norm_sum(big, True)

            for i in range(depth):
                kind, j = i % 3, i // 3
                if kind == 0:
                    gla(j)
                elif kind == 1:
                    fox()
                else:
                    conv()
                ffn()
            pe.wait_ge(x_done, 2 * depth * KD)
            for tt in range(PT + 1):
                n = P if tt < PT else NS
                bank = 2 * (tt % 4)
                pe.wait_ge(acc_out[bank], t.out[bank])
                for k in range(KD):
                    last = pe.transpose(acc[0:n, bank + k // 4, (k % 4) * P:(k % 4 + 1) * P],
                                        xT[:, k, tt * P:tt * P + n], ident[:])
                last.then_inc(acc_full[bank], 1)
                t.use(bank)

        @block.vector
        def _(dve):
            t = Tally()
            steps = [0]

            def step(ins):
                steps[0] += 1
                ins.then_inc(s_dve, 1)

            def stepped():
                dve.wait_ge(s_dve, steps[0])

            rstds = [0]

            def reciprocal_root():
                t.use(0)
                dve.wait_ge(acc_out[0], t.out[0])
                dve.reciprocal(rstd[:], root[:]).then_inc(rstd_done, 1)
                rstds[0] += 1
                dve.wait_ge(rstd_done, rstds[0])

            def norm_pre(layer, which):
                reciprocal_root()
                for k in range(KD):
                    dve.scalar_tensor_tensor(out=hT[:, k, :], in0=xT[:, k, :], scalar=gcol(layer, which, k),
                                             in1=rstd[:], op0=ALU.mult, op1=ALU.mult).then_inc(h_done, 1)
                t.h += KD

            def norm_post(layer, which):
                reciprocal_root()
                for k in range(KD):
                    dve.scalar_tensor_tensor(out=yT[:, k, :], in0=yT[:, k, :], scalar=gcol(layer, which, k),
                                             in1=rstd[:], op0=ALU.mult, op1=ALU.mult).then_inc(z_done, 1)
                t.z += KD

            for k in range(KD):
                bank = 2 * (k % 4)
                if k % 2 == 1:
                    dve.wait_ge(acc_full[bank], t.full[bank] + 1)
                    dve.tensor_copy(xT[:, k, :], accflat(bank)).then_inc(acc_out[bank], 1)
                t.use(bank)
            t.use(0)
            dve.wait_ge(const_made, N_CONST)

            def gla(j):
                norm_pre(3 * j, 0)
                t.blocks(2 * GH, uses=2)
                t.use(0)
                step(dve.memset(part(M1, M3 - M1), 0.0))
                for m in range(GH):
                    bank = 2 * ((m + 1) % 4)
                    dve.wait_ge(abs_done, GH * j + m + 1)
                    dve.tensor_scalar(two(big[:, 8 + m, :]), acc2(bank), vcol("bg", GH * j + m), 0.0, ALU.add, ALU.min)\
                       .then_inc(acc_out[bank], 1)
                    t.use(bank)
                dve.wait_ge(soft_done, j + 1)
                for m in range(GH):
                    dve.wait_ge(acc_out[2 * ((m + 1) % 4)], t.out[2 * ((m + 1) % 4)])
                step(dve.tensor_tensor(big[:, 8:12, :], big[:, 8:12, :], yT[:, 4:8, :], ALU.subtract))
                stepped()
                for m in range(GH):
                    dve.tensor_tensor_scan(yT[:, 4 + m, :], reset[:], big[:, 8 + m, :], 0.0, ALU.mult, ALU.add)\
                       .then_inc(cum_done, 1)
                dve.wait_ge(cum_done, GH * (j + 1))
                for t0, n, c in ((0, SEQ, GLA_CHUNK), (SEQ, NS, DS)):
                    for h in range(GH):
                        cum = yT[:, 4 + h, t0:t0 + n].rearrange("p (c t) -> p c t", t=c)
                        last = dve.tensor_tensor(g_diff[:, h, t0:t0 + n].rearrange("p (c t) -> p c t", t=c),
                                                 cum[:, :, c - 1:c].to_broadcast([P, n // c, c]), cum, ALU.subtract)
                last.then_inc(diff_done, 1)
                dve.wait_ge(decay_done, 2 * j + 1)
                dve.tensor_tensor(big[:, 0:4, :], big[:, 0:4, :], big[:, 8:12, :], ALU.mult)
                dve.wait_ge(decay_done, 2 * j + 2)
                dve.tensor_tensor(yT[:, 0:4, :], yT[:, 0:4, :], big[:, 4:8, :], ALU.mult)
                dve.wait_ge(kdec_done, j + 1)
                dve.tensor_tensor(big[:, 4:8, :], big[:, 4:8, :], g_diff, ALU.mult).then_inc(keys_done, 1)
                t.blocks(KD, uses=2)
                b0 = t.blk
                with dve.Fori(0, KD // RING) as it:
                    for a in range(RING):
                        dve.wait_ge(blk_done, it * RING + (b0 + a + 1))
                        dve.tensor_copy(v_nat[:, 0:PT, ds((it * RING + a) * P, P)],
                                        acc[:, 2 * a, :].rearrange("p (t n) -> p t n", t=PT))
                        dve.tensor_copy(v_nat[0:NS, PT, ds((it * RING + a) * P, P)], acc[0:NS, 2 * a + 1, 0:P])\
                           .then_inc(acc_out[2 * a], 1)
                t.blocks(KD, uses=2)
                stepped()
                for tt in range(PT + 1):
                    bank = 4 * (tt % 2)
                    t.use(bank)
                    dve.wait_ge(acc_full[bank + 1], t.full[bank + 1] + 1)
                    if tt < PT:
                        dve.copy_predicated(att[:, tt], m_chunk[:].bitcast(U32).rearrange("p (a t) -> p a t", a=1)
                                            .to_broadcast([P, GH, P]),
                                            acc[:, bank + 1, :].rearrange("p (h t) -> p h t", h=GH))\
                           .then_inc(acc_out[bank + 1], 1)
                    else:
                        mle = m_le[:].rearrange("p b t -> p (b t)").bitcast(U32).rearrange("p (a t) -> p a t", a=1)
                        dve.copy_predicated(att_s, mle.to_broadcast([NS, GH, NS]),
                                            acc[0:NS, bank + 1, :].rearrange("p (h t) -> p h t", h=GH)[:, :, 0:NS])\
                           .then_inc(acc_out[bank + 1], 1)
                    t.use(bank + 1)
                for c in range(NCH):
                    ob, ub = (0, 1)[c % 2], (2, 4)[c % 2]
                    dve.wait_ge(acc_full[ub], t.full[ub] + 1)
                    t.use(ub)
                    dve.wait_ge(acc_full[ob], t.full[ob] + 1)
                    t.use(ob)
                    if c > 0:
                        prev = (2, 4)[(c - 1) % 2]
                        dve.wait_ge(acc_out[prev], t.out[prev])
                    for h in range(GH):
                        add = acc[:, ub + h // 2, (h % 2) * DV:(h % 2 + 1) * DV]
                        end = (c + 1) * GLA_CHUNK - 1
                        if c == 0:
                            last = dve.tensor_copy(S[:, h, :], add)
                        else:
                            last = dve.scalar_tensor_tensor(out=S[:, h, :], in0=S[:, h, :],
                                                            scalar=big[:, 8 + h, end:end + 1], in1=add,
                                                            op0=ALU.mult, op1=ALU.add)
                    last.then_inc(acc_out[ub], 1)

                def keys_of(b):
                    dve.tensor_scalar(kd_b[:, b % 2], kd_nat[0:NS, PT], m_in[:, b:b + 1], None, ALU.mult)\
                       .then_inc(kdb_done, 1)

                bank = 4 * (PT % 2)
                dve.wait_ge(acc_out[0], t.out[0])
                keys_of(0)
                keys_of(1)
                for b in range(DB):
                    ub = (2, 4)[b % 2]
                    if b == DB - 1:
                        t.use(0)
                    dve.wait_ge(acc_full[ub], t.full[ub] + 1)
                    t.use(ub)
                    for h in range(GH):
                        end = SEQ + b * DS + DS - 1
                        state = st[:, (b // 2) % 2, b % 2, h, :]
                        last = dve.scalar_tensor_tensor(out=state, in0=state, scalar=big[:, 8 + h, end:end + 1],
                                                        in1=acc[:, ub + h // 2, (h % 2) * DV:(h % 2 + 1) * DV],
                                                        op0=ALU.mult, op1=ALU.add)
                    last.then_inc(acc_out[ub], 1)
                    if b + 2 < DB:
                        keys_of(b + 2)
                for h in range(GH):
                    t.use(2 * h)
                    dve.wait_ge(acc_out[2 * h], t.out[2 * h])
                    step(dve.reciprocal(big[:, h, :], big[:, h, :]))
                    stepped()
                    for v in range(VH):
                        u = h * VH + v
                        step(dve.scalar_tensor_tensor(out=hT[:, u, :], in0=hT[:, u, :], scalar=vcol("gn", VH * j + v),
                                                      in1=big[:, h, :], op0=ALU.mult, op1=ALU.mult))
                    stepped()
                    for u in range(h * VH, (h + 1) * VH):
                        dve.tensor_tensor(hT[:, u, :], hT[:, u, :], big[:, 12 + u, :], ALU.mult).then_inc(o_done, 1)
                t.blocks(KD, uses=2)
                norm_post(3 * j, 1)

            def ffn(i):
                norm_pre(i, 2)
                b0, o = t.blk, list(t.out)
                with dve.Fori(0, KF // 2) as it:
                    for a in range(2):
                        dve.wait_ge(acc_out[4 * a], it + (o[4 * a] + 1))
                        dve.wait_ge(blk_done, it * RING + (b0 + 2 * a + 2))
                        dve.tensor_tensor(two(big[:, ds(it * 2 + a, 1), :].rearrange("p a t -> p (a t)")),
                                          two(sil[:, a, :]), acc2(4 * a + 2), ALU.mult).then_inc(acc_out[4 * a + 2], 1)
                t.blocks(2 * KF, uses=KF // 2)
                t.blocks(2 * KD, uses=KD // 4)
                norm_post(i, 3)

            def prompt_scores(i, h, q):
                bank = i % 2
                dve.wait_ge(acc_full[bank], t.full[bank] + 1)
                if i >= 2:
                    tb = 2 + (i % 2)
                    dve.wait_ge(acc_full[tb], t.full[tb] + 1)
                if q:
                    dve.tensor_scalar(probs[:, i % 2, 0:q * P], acc[:, bank, 0:q * P], cumq[:, q, h:h + 1], None, ALU.add)
                dve.scalar_tensor_tensor(out=probs[:, i % 2, q * P:(q + 1) * P], in0=acc[:, bank, q * P:(q + 1) * P],
                                         scalar=cumq[:, q, h:h + 1], in1=causal[:], op0=ALU.add, op1=ALU.add)\
                   .then_inc(acc_out[bank], 1)
                t.use(bank)
                dve.wait_ge(acc_out[bank], t.out[bank])
                dve.tensor_reduce(nmax[:, i % 4:i % 4 + 1], probs[:, i % 2, 0:(q + 1) * P], AX.X, ALU.max, negate=True)\
                   .then_inc(pmax_done, 1)

            def prompt_probs(i, h, q):
                dve.wait_ge(pexp_done, i + 1)
                step(dve.reciprocal(rsum[:, i % 4:i % 4 + 1], rsum[:, i % 4:i % 4 + 1]))
                stepped()
                dve.tensor_scalar(probs[:, i % 2, 0:(q + 1) * P], probs[:, i % 2, 0:(q + 1) * P],
                                  rsum[:, i % 4:i % 4 + 1], None, ALU.mult).then_inc(p_done, 1)

            def sample_attention():
                f, o = list(t.full), list(t.out)
                dve.memset(sm, 0.0)
                with dve.Fori(0, DB) as b:
                    base = steps[0]
                    n = [0]
                    PER = 4

                    def step_b(ins):
                        n[0] += 1
                        ins.then_inc(s_dve, 1)

                    def stepped_b():
                        dve.wait_ge(s_dve, b * PER + (base + n[0]))

                    zp = z[:, 0:NPAGES, :]
                    for c in range(2):
                        dve.wait_ge(acc_full[4 + c], b + (f[4 + c] + 1))
                        dve.tensor_tensor(z[:, 8 * c:8 * c + 8, :].rearrange("p g (h i) -> p g h i", h=FH),
                                          acc[:, 4 + c, :].rearrange("p (g h i) -> p g h i", g=8, h=FH),
                                          suf[:, ds(b, 1), 8 * c:8 * c + 8, :].rearrange("p a g (h i) -> p (a g) h i", i=1)
                                          .to_broadcast([P, 8, FH, DS]), ALU.add).then_inc(acc_out[4 + c], 1)
                    dve.wait_ge(acc_full[6], b * 4 + (f[6] + 1))
                    dve.tensor_tensor(z[0:NS, NPAGES, :], acc[0:NS, 6, 0:HI], dn[:, ds(b * HI, HI)], ALU.add)\
                       .then_inc(acc_out[6], 1)
                    for c in range(2):
                        dve.wait_ge(acc_out[4 + c], b + (o[4 + c] + 1))
                    dve.wait_ge(acc_out[6], b * 4 + (o[6] + 1))
                    rbb = rb[:, ds(b * HI, HI)].rearrange("p (g n) -> p g n", g=1)
                    step_b(dve.tensor_tensor(zp, zp, rbb.to_broadcast([P, NPAGES, HI]), ALU.subtract))
                    step_b(dve.tensor_tensor(z[0:NS, NPAGES, :], z[0:NS, NPAGES, :], rb[0:NS, ds(b * HI, HI)], ALU.subtract))
                    stepped_b()
                    step_b(dve.tensor_reduce(mx, zp.rearrange("p g n -> p n g"), AX.X, ALU.max))
                    stepped_b()
                    dve.tensor_tensor(mx[0:NS], mx[0:NS], z[0:NS, NPAGES, :], ALU.max).then_inc(mx_done, 1)
                    dve.wait_ge(acc_full[6], b * 4 + (f[6] + 2))
                    dve.tensor_reduce(m64, acc[0:HI, 6, P:2 * P], AX.X, ALU.max).then_inc(acc_out[6], 1)
                    dve.wait_ge(acc_out[6], b * 4 + (o[6] + 2))
                    dve.tensor_scalar(dg, ident[0:HI, 0:HI], m64, None, ALU.mult).then_inc(dg_done, 1)
                    dve.wait_ge(acc_full[6], b * 4 + (f[6] + 3))
                    dve.tensor_tensor(z[0:NS, NPAGES, :], z[0:NS, NPAGES, :], acc[0:NS, 6, 0:HI], ALU.subtract)\
                       .then_inc(zx_done, 1)
                    dve.tensor_tensor(zp, zp, acc[:, 6:7, 0:HI].to_broadcast([P, NPAGES, HI]), ALU.subtract)\
                       .then_inc(acc_out[6], 1)
                    dve.wait_ge(zexp_done, b * 2 + 2)
                    step_b(dve.tensor_reduce(sm, zp.rearrange("p g n -> p n g"), AX.X, ALU.add))
                    stepped_b()
                    dve.tensor_tensor(sm[0:NS], sm[0:NS], z[0:NS, NPAGES, :], ALU.add).then_inc(sm_done, 1)
                    dve.wait_ge(acc_full[6], b * 4 + (f[6] + 4))
                    dve.reciprocal(rc, acc[:, 6, 0:HI]).then_inc(acc_out[6], 1)
                    dve.wait_ge(acc_out[6], b * 4 + (o[6] + 4))
                    dve.wait_ge(v_used, b * NPAGES + NPAGES)
                    rcv = rc.rearrange("p (m e i) -> p m e i", m=PAIRS, e=2)
                    ov = acc[:, 7, 0:HI].rearrange("p (m e i) -> p m e i", m=PAIRS, e=2)
                    for e in range(2):
                        rows = slice(e * DH, (e + 1) * DH)
                        last = dve.tensor_tensor(hT[rows, :, ds(b * DS + SEQ, DS)], ov[rows, :, e, :], rcv[rows, :, e, :],
                                                 ALU.mult)
                    last.then_inc(acc_out[7], 1)
                    assert n[0] == PER, n[0]
                steps[0] += PER * DB
                for bank, n in ((4, 1), (5, 1), (6, 4)):
                    t.use(bank, DB * n)
                t.out[7] += DB

            def fox():
                norm_pre(1, 0)
                t.blocks(2 * KD, uses=4)
                t.use(0)
                dve.wait_ge(fabs_done, 1)
                dve.tensor_scalar(two(logf), acc[0:FH, 0:2, 0:HALF], fbias[:, 0:1], 0.0, ALU.add, ALU.min)\
                   .then_inc(acc_out[0], 1)
                dve.wait_ge(fexp_done, 1)
                dve.tensor_scalar(l_u, l_e, 1.0, None, ALU.add).then_inc(fu_done, 1)
                dve.wait_ge(fln_done, 1)
                step(dve.tensor_scalar(l_u, l_u, -1.0, None, ALU.add))
                stepped()
                step(dve.tensor_scalar(l_m, l_u, 0.0, None, ALU.is_equal))
                stepped()
                step(dve.tensor_tensor(l_u, l_u, l_m, ALU.add))
                step(dve.tensor_tensor(l_m, l_m, rstd[0:FH, :], ALU.add))
                stepped()
                step(dve.reciprocal(l_u, l_u))
                step(dve.tensor_tensor(l_m, l_m, l_e, ALU.mult))
                stepped()
                step(dve.tensor_tensor(l_m, l_m, l_u, ALU.mult))
                stepped()
                step(dve.tensor_tensor(logf, logf, l_m, ALU.subtract))
                stepped()
                step(dve.tensor_tensor_scan(ncum, ones[0:FH, 0:1].to_broadcast([FH, SEQ]), logf[:, 0:SEQ], 0.0,
                                            ALU.mult, ALU.subtract))
                stepped()
                dve.tensor_copy(l_u[:, 0:1], ncum[:, 0:1]).then_inc(logf_done, 1)
                step(dve.memset(qblk, 0.0))
                stepped()
                for e in range(2):
                    rows = slice(e * DH, (e + 1) * DH)
                    last = dve.tensor_copy(qblk[rows, :, :, e, :],
                                           big[rows, 0:KD, SEQ:TOK].rearrange("p m (b i) -> p b m i", b=DB))
                last.then_inc(qblk_done, 1)
                b0 = t.blk
                with dve.Fori(0, KD // RING) as it:
                    for a in range(RING):
                        dve.wait_ge(blk_done, it * RING + (b0 + a + 1))
                        dve.tensor_copy(v_nat[:, 0:PT, ds((it * RING + a) * P, P)],
                                        acc[:, 2 * a, :].rearrange("p (t n) -> p t n", t=PT))
                        dve.tensor_copy(v_nat[0:NS, PT, ds((it * RING + a) * P, P)], acc[0:NS, 2 * a + 1, 0:P])\
                           .then_inc(acc_out[2 * a], 1)
                t.blocks(KD, uses=2)
                for tt in range(PT + 1):
                    t.use(2 * (tt % 4))
                dve.wait_ge(acc_full[0], t.full[0] + 1)
                dve.tensor_copy(lnat[:, 0:PT, :], acc[:, 0, 0:PT * FH].rearrange("p (t h) -> p t h", t=PT))
                dve.tensor_copy(lnat[0:NS, PT, :], acc[0:NS, 0, PT * FH:(PT + 1) * FH]).then_inc(acc_out[0], 1)
                t.use(0)
                dve.wait_ge(acc_full[1], t.full[1] + 1)
                dve.tensor_scalar(cumq, acc[:, 1, 0:PT * FH].rearrange("p (t h) -> p t h", t=PT), -1.0, None, ALU.mult)\
                   .then_inc(acc_out[1], 1)
                t.use(1)
                dve.wait_ge(acc_out[0], t.out[0])
                ls = lnat[0:NS, PT, :]
                step(dve.tensor_tensor(dn.rearrange("p (b h i) -> p b h i", b=DB, h=FH),
                                  ls.rearrange("p (b h i) -> p b h i", b=1, i=1).to_broadcast([NS, DB, FH, DS]),
                                  m_gt[:].rearrange("p b (h i) -> p b h i", h=1).to_broadcast([NS, DB, FH, DS]), ALU.mult))
                dve.tensor_tensor(dt_.rearrange("p (b h) -> p b h", b=DB),
                                  ls.rearrange("p (b h) -> p b h", b=1).to_broadcast([NS, DB, FH]),
                                  m_in[:].rearrange("p (b h) -> p b h", h=1).to_broadcast([NS, DB, FH]), ALU.mult)\
                   .then_inc(dmat_done, 1)
                dve.wait_ge(acc_full[2], t.full[2] + 1)
                dve.tensor_copy(rb, acc[:, 2, 0:DB * HI]).then_inc(acc_out[2], 1)
                t.use(2)
                dve.wait_ge(acc_full[4], t.full[4] + 1)
                step(dve.tensor_copy(totn, acc[:, 4, 0:DB * FH]))
                dve.tensor_copy(sufn, acc[0:NS, 4, DB * FH:(DB + 1) * FH]).then_inc(acc_out[4], 1)
                t.use(4)
                step(dve.tensor_scalar(dt_[:, 0:NS], m_le[:].rearrange("p b i -> p (b i)"), -1.0, -NEG, ALU.add, ALU.mult))
                stepped()
                dve.wait_ge(acc_out[4], t.out[4])
                step(dve.tensor_tensor(dn.rearrange("p (b h i) -> p b h i", b=DB, h=FH),
                                  sufn.rearrange("p (b h i) -> p b h i", b=1, i=1).to_broadcast([NS, DB, FH, DS]),
                                  dt_[:, 0:NS].rearrange("p (b h i) -> p b h i", b=DB, h=1).to_broadcast([NS, DB, FH, DS]),
                                  ALU.add))
                stepped()
                items = [(h, q) for h in range(FH) for q in range(PT)]
                for i in range(len(items) + 1):
                    if i >= 1:
                        prompt_probs(i - 1, *items[i - 1])
                    if i < len(items):
                        prompt_scores(i, *items[i])
                    if i >= 2 or i == len(items):
                        t.use(2 + (i % 2))
                t.use(2 + (len(items) + 1) % 2)
                dve.wait_ge(lf_in, 16 * DB * NPAGES)
                step(dve.memset(later[:, :, NPAGES - 1, :], 0.0))
                for g in reversed(range(NPAGES - 1)):
                    stepped()
                    step(dve.tensor_tensor(later[:, :, g, :], later[:, :, g + 1, :], lf[:, :, g + 1, :], ALU.add))
                stepped()
                dve.tensor_copy(l_u[:, 0:1], ncum[:, 0:1]).then_inc(later_done, 1)
                for c in range(LFN // 512):
                    bank = 2 * (c % 4)
                    dve.wait_ge(acc_full[bank], t.full[bank] + 1)
                    tot = totn[:, 2 * c * FH:2 * (c + 1) * FH].rearrange("p (b g h) -> p b g h", b=2, g=1)
                    dve.tensor_tensor(suf[:, 2 * c:2 * c + 2], acc[:, bank, :].rearrange("p (b g h) -> p b g h", b=2, g=NPAGES),
                                      tot.to_broadcast([P, 2, NPAGES, FH]), ALU.add).then_inc(acc_out[bank], 1)
                    t.use(bank)
                stepped()
                sample_attention()
                dve.wait_ge(acc_out[7], t.out[7])
                dve.tensor_copy(l_u[:, 0:1], l_m[:, 0:1]).then_inc(o_done, KD)
                t.blocks(KD, uses=2)
                norm_post(1, 1)

            def conv():
                for k in range(KD):
                    t.use(2 * (k % 4))
                norm_pre(2, 0)
                step(dve.memset(ext_p[:, :, 0:CB], 0.0))
                b0, o = t.blk, list(t.out)
                base = steps[0]
                with dve.Fori(0, KD // 2) as it:
                    for a in range(2):
                        dve.wait_ge(acc_out[4 * a + 2], it + (o[4 * a + 2] + 1))
                        dve.wait_ge(blk_done, it * RING + (b0 + 2 * a + 1))
                        bias = vecs[:, ds(it * 2 + (col["b1"] + a), 1)]
                        gate, bank = sil[:, a, :], 4 * a
                        m = it * 2 + a
                        dve.scalar_tensor_tensor(out=ext_p[:, ds(m, 1), CB:CB + HALF].rearrange("p a t -> p (a t)"),
                                                 in0=acc[:, bank, 0:HALF], scalar=bias, in1=gate[:, 0:HALF],
                                                 op0=ALU.add, op1=ALU.mult)
                        dve.scalar_tensor_tensor(out=ext_p[:, ds(m, 1), CB + HALF:EP].rearrange("p a t -> p (a t)"),
                                                 in0=acc[:, bank + 1, 0:SEQ - HALF], scalar=bias,
                                                 in1=gate[:, HALF:SEQ], op0=ALU.add, op1=ALU.mult)
                        dve.scalar_tensor_tensor(out=ext_s[:, ds(m, 1), :, CB:ES].rearrange("p a b t -> p (a b) t"),
                                                 in0=acc[:, bank + 1, SEQ - HALF:HALF].rearrange("p (b t) -> p b t", b=DB),
                                                 scalar=bias, in1=gate[:, SEQ:TOK].rearrange("p (b t) -> p b t", b=DB),
                                                 op0=ALU.add, op1=ALU.mult).then_inc(acc_out[bank], 1)
                    for a in range(2):
                        dve.wait_ge(acc_out[4 * a], it + (o[4 * a] + 1))
                    for w in range(CW):
                        for a in range(2):
                            m = it * 2 + a
                            tap = vecs[:, ds(it * 2 + (col["wdw"] + w * KD + a), 1)]
                            for q in range(2):
                                if q == 0:
                                    src = ext_p[:, ds(m, 1), w:w + SEQ].rearrange("p a t -> p (a t)")
                                    dst = dw[:, ds(m, 1), 0:SEQ].rearrange("p a t -> p (a t)")
                                else:
                                    src = ext_s[:, ds(m, 1), :, w:w + DS].rearrange("p a b t -> p (a b) t")
                                    dst = dw[:, ds(m, 1), SEQ:TOK].rearrange("p a (b t) -> p (a b) t", b=DB)
                                if w == 0:
                                    ins = dve.tensor_scalar(dst, src, tap, vecs[:, ds(it * 2 + (col["bdw"] + a), 1)],
                                                            ALU.mult, ALU.add)
                                else:
                                    dve.wait_ge(s_dve, it * (4 * CW - 4) + (base + 4 * w + 2 * a + q - 3))
                                    ins = dve.scalar_tensor_tensor(out=dst, in0=src, scalar=tap, in1=dst,
                                                                   op0=ALU.mult, op1=ALU.add)
                                if w == CW - 1 and a == 1 and q == 1:
                                    ins.then_inc(conv_done, 1)
                                elif w == CW - 1:
                                    pass
                                else:
                                    ins.then_inc(s_dve, 1)
                steps[0] += (4 * CW - 4) * (KD // 2)
                t.blocks(2 * KD, uses=KD // 2)
                t.use(0)
                dve.wait_ge(acc_out[0], t.out[0])
                dve.wait_ge(conv_done, KD // 2)
                for k in range(KD):
                    dve.tensor_tensor(dw[:, k, :], dw[:, k, :], root[:], ALU.subtract).then_inc(mean_done, 1)
                for b in (2, 4, 6):
                    t.use(b)
                reciprocal_root()
                for k in range(KD):
                    dve.tensor_tensor(dw[:, k, :], dw[:, k, :], rstd[:], ALU.mult).then_inc(scaled_done, 1)
                t.blocks(KD, uses=2)
                norm_post(2, 1)

            for i in range(depth):
                kind, j = i % 3, i // 3
                if kind == 0:
                    gla(j)
                elif kind == 1:
                    fox()
                else:
                    conv()
                ffn(i)

        @block.scalar
        def _(act):
            t = Tally()
            steps = [0]

            def step(ins):
                steps[0] += 1
                ins.then_inc(s_act, 1)

            def stepped():
                act.wait_ge(s_act, steps[0])

            rstds = [0]

            def root_of_mean(eps=0):
                act.wait_ge(acc_full[0], t.full[0] + 1)
                if rstds[0]:
                    act.wait_ge(rstd_done, rstds[0])
                act.activation(two(root[:]), acc2(0), ACT.Sqrt, bias=epsb[:, eps:eps + 1], scale=1.0 / D).then_inc(acc_out[0], 1)
                t.use(0)
                rstds[0] += 1

            def squares_of_x():
                for k in range(KD):
                    if t.x:
                        act.wait_ge(x_done, t.x - KD + k + 1)
                    act.activation(hT[:, k, :], xT[:, k, :], ACT.Square).then_inc(sq_done, 1)
                t.sq += KD
                root_of_mean()

            def read_y(blocks_each, squares):
                b0 = t.blk
                with act.Fori(0, KD // 4) as it:
                    for a in range(4):
                        act.wait_ge(blk_done, it * (4 * blocks_each) + (b0 + blocks_each * (a + 1)))
                        act.activation(two(yT[:, ds(it * 4 + a, 1), :].rearrange("p a t -> p (a t)")), acc2(2 * a), ACT.Copy)
                        act.activation(two(squares[:, ds(it * 4 + a, 1), :].rearrange("p a t -> p (a t)")), acc2(2 * a),
                                       ACT.Square).then_inc(acc_out[2 * a], 1)
                t.blocks(KD * blocks_each, uses=KD // 4)
                root_of_mean()
                t.x += KD

            for k in range(KD):
                bank = 2 * (k % 4)
                if k % 2 == 0:
                    act.wait_ge(acc_full[bank], t.full[bank] + 1)
                    act.activation(xT[:, k, :], accflat(bank), ACT.Copy).then_inc(acc_out[bank], 1)
                t.use(bank)
            act.wait_ge(acc_full[0], t.full[0] + 1)
            step(act.activation(vecs[:, 0:P + VN[1]], acc[:, 0, 0:P + VN[1]], ACT.Copy))
            act.activation(vecs[:, 2 * P:3 * P + VN[3]], acc[:, 0, 2 * P:3 * P + VN[3]], ACT.Copy).then_inc(acc_out[0], 1)
            t.use(0)
            for b in (0, 2, 4, 6):
                act.wait_ge(acc_out[b], t.out[b])
            act.wait_ge(const_made, N_CONST)

            def gla(j):
                squares_of_x()
                for base, scale in ((0, DK ** -0.5), (GH, 1.0)):
                    for m in range(GH):
                        act.wait_ge(blk_done, t.blk + m + 1)
                        act.activation(two(big[:, base + m, :]), acc2(2 * m), ACT.Copy, scale=scale)\
                           .then_inc(acc_out[2 * m], 1)
                    t.blocks(GH, uses=1)
                act.wait_ge(acc_full[0], t.full[0] + 1)
                act.activation(two(lowr), acc[0:RANK, 0:2, 0:HALF], ACT.Copy).then_inc(acc_out[0], 1)
                t.use(0)
                for m in range(GH):
                    bank = 2 * ((m + 1) % 4)
                    act.wait_ge(acc_full[bank], t.full[bank] + 1)
                    act.activation(two(yT[:, 4 + m, :]), acc2(bank), ACT.Abs, bias=vcol("bg", GH * j + m))\
                       .then_inc(abs_done, 1)
                    t.use(bank)
                act.wait_ge(abs_done, GH * (j + 1))
                step(act.activation(yT[:, 4:8, :], yT[:, 4:8, :], ACT.Exp, scale=-1.0))
                stepped()
                act.activation(yT[:, 4:8, :], yT[:, 4:8, :], ACT.Ln, bias=1.0).then_inc(soft_done, 1)
                act.wait_ge(cum_done, GH * (j + 1))
                act.activation(big[:, 8:12, :], yT[:, 4:8, :], ACT.Exp, scale=1.0 / 16).then_inc(decay_done, 1)
                act.activation(yT[:, 0:4, :], yT[:, 4:8, :], ACT.Exp, scale=-1.0 / 16).then_inc(decay_done, 1)
                act.wait_ge(diff_done, j + 1)
                act.activation(g_diff, g_diff, ACT.Exp, scale=1.0 / 16).then_inc(kdec_done, 1)
                b0 = t.blk
                with act.Fori(0, KD // RING) as it:
                    for a in range(RING):
                        act.wait_ge(blk_done, it * RING + (b0 + a + 1))
                        act.activation(two(big[:, ds(it * RING + (12 + a), 1), :].rearrange("p a t -> p (a t)")),
                                       acc2(2 * a), ACT.Silu).then_inc(acc_out[2 * a], 1)
                t.blocks(KD, uses=2)
                t.blocks(KD, uses=2)
                for tt in range(PT + 1):
                    n = P if tt < PT else NS
                    bank = 4 * (tt % 2)
                    act.wait_ge(acc_full[bank], t.full[bank] + 1)
                    act.activation(kd_nat[0:n, tt], acc[0:n, bank, :].rearrange("p (h k) -> p h k", h=GH), ACT.Copy)\
                       .then_inc(acc_out[bank], 1)
                    t.use(bank)
                    t.use(bank + 1)
                for c in range(NCH):
                    ob, ub = (0, 1)[c % 2], (2, 4)[c % 2]
                    act.wait_ge(acc_full[ob], t.full[ob] + 1)
                    act.activation(hT[:, :, c * GLA_CHUNK:(c + 1) * GLA_CHUNK],
                                   acc[:, ob, :].rearrange("p (u t) -> p u t", u=KD), ACT.Copy).then_inc(acc_out[ob], 1)
                    t.use(ub)
                    t.use(ob)
                for b in range(DB):
                    ub = (2, 4)[b % 2]
                    if b == DB - 1:
                        act.wait_ge(acc_full[0], t.full[0] + 1)
                        act.activation(hT[:, :, SEQ:TOK], acc[:, 0, 0:KD * NS].rearrange("p (u t) -> p u t", u=KD),
                                       ACT.Copy).then_inc(acc_out[0], 1)
                        t.use(0)
                    t.use(ub)
                    if b % 2 == 1:
                        for q in (2, 4):
                            act.wait_ge(acc_out[q], t.out[q])
                        act.dma_start(gla_ss[j, b - 1:b + 1].rearrange("b h k v -> k b h v"), st[:, (b // 2) % 2])\
                           .then_inc(st_out[(b // 2) % 2], 16)
                act.wait_ge(acc_out[0], t.out[0])
                act.wait_ge(acc_out[1], t.out[1])
                for u in range(KD):
                    act.activation(yT[:, u, :], hT[:, u, :], ACT.Square).then_inc(sq_done, 1)
                t.sq += KD
                for h in range(GH):
                    act.wait_ge(acc_full[2 * h], t.full[2 * h] + 1)
                    act.activation(two(big[:, h, :]), acc2(2 * h), ACT.Sqrt, bias=epsb[:, 0:1], scale=1.0 / DV)\
                       .then_inc(acc_out[2 * h], 1)
                    t.use(2 * h)
                for q in st_out:
                    act.wait_ge(q, 16 * (DB // 4) * (j + 1))
                read_y(1, big)

            def ffn():
                squares_of_x()
                b0, o = t.blk, list(t.out)
                with act.Fori(0, KF // 2) as it:
                    for a in range(2):
                        act.wait_ge(blk_done, it * RING + (b0 + 2 * a + 1))
                        act.wait_ge(acc_out[4 * a + 2], it + o[4 * a + 2])
                        act.activation(two(sil[:, a, :]), acc2(4 * a), ACT.Silu).then_inc(acc_out[4 * a], 1)
                t.blocks(2 * KF, uses=KF // 2)
                read_y(2, hT)

            def store(dst, src, done=out_in):
                act.dma_start(dst, src).then_inc(done, 16)
                outputs.append(dst) if done is out_in else None

            def fox():
                squares_of_x()
                act.wait_ge(state_out, 16)
                for base, scale in ((0, DH ** -0.5), (KD, 1.0)):
                    b0 = t.blk
                    with act.Fori(0, KD // RING) as it:
                        for a in range(RING):
                            act.wait_ge(blk_done, it * RING + (b0 + a + 1))
                            act.activation(two(big[:, ds(it * RING + (base + a), 1), :].rearrange("p a t -> p (a t)")),
                                           acc2(2 * a), ACT.Copy, scale=scale).then_inc(acc_out[2 * a], 1)
                    t.blocks(KD, uses=2)
                act.wait_ge(acc_full[0], t.full[0] + 1)
                act.activation(two(l_e), acc[0:FH, 0:2, 0:HALF], ACT.Abs, bias=fbias[:, 0:1]).then_inc(fabs_done, 1)
                t.use(0)
                act.wait_ge(fabs_done, 1)
                act.activation(l_e, l_e, ACT.Exp, scale=-1.0).then_inc(fexp_done, 1)
                act.wait_ge(fu_done, 1)
                act.activation(rstd[0:FH, :], l_u, ACT.Ln).then_inc(fln_done, 1)
                t.blocks(KD, uses=2)
                for b in (0, 2, 4, 6):
                    act.wait_ge(acc_out[b], t.out[b])
                store(fox_vp[0, 0].rearrange("(t p) h d -> p t (h d)", p=P), v_nat[:, 0:PT, :], nat_out)
                store(fox_vs[0].rearrange("b s h d -> (b s) (h d)"), v_nat[0:NS, PT, :], nat_out)
                for tt in range(PT + 1):
                    n = P if tt < PT else NS
                    bank = 2 * (tt % 4)
                    rows = k_rows[:, tt, :] if tt < PT else k_rows_s
                    act.wait_ge(acc_full[bank], t.full[bank] + 1)
                    act.activation(rows, acc[0:n, bank:bank + 2, :].rearrange("p b n -> p (b n)"), ACT.Copy)\
                       .then_inc(acc_out[bank], 1)
                    t.use(bank)
                    act.wait_ge(acc_out[bank], t.out[bank])
                    store(fox_kp[0, 0, tt * P:(tt + 1) * P].rearrange("p h d -> p (h d)") if tt < PT
                          else fox_ks[0].rearrange("b s h d -> (b s) (h d)"), rows, nat_out)
                t.use(0)
                act.wait_ge(acc_out[0], t.out[0])
                store(fox_lp[0, 0].rearrange("(t p) h -> p t h", p=P), lnat[:, 0:PT, :], nat_out)
                store(fox_ls[0].rearrange("b s h -> (b s) h"), lnat[0:NS, PT, :], nat_out)
                for b in (1, 2, 4):
                    t.use(b)
                items = [(h, q) for h in range(FH) for q in range(PT)]
                for i in range(len(items) + 3):
                    if i < len(items):
                        h, q = items[i]
                        act.wait_ge(pmax_done, i + 1)
                        act.activation(probs[:, i % 2, 0:(q + 1) * P], probs[:, i % 2, 0:(q + 1) * P], ACT.Exp,
                                       bias=nmax[:, i % 4:i % 4 + 1], accum_out=rsum[:, i % 4:i % 4 + 1])\
                           .then_inc(pexp_done, 1)
                        t.use(i % 2)
                    if 2 <= i < len(items) + 2:
                        h, q = items[i - 2]
                        bank = 2 + (i % 2)
                        if q == 0 and h >= 2:
                            act.wait_ge(pv_full, h - 1)
                        act.wait_ge(acc_full[bank], t.full[bank] + 1)
                        act.activation(pT[:, h % 2, 0:q + 1, q * P:(q + 1) * P],
                                       acc[:, bank, 0:(q + 1) * P].rearrange("p (k n) -> p k n", n=P), ACT.Copy)\
                           .then_inc(acc_out[bank], 1)
                        t.use(bank)
                    if i >= 3:
                        h, q = items[i - 3]
                        if q == PT - 1 and h % 2 == 1:
                            act.wait_ge(pv_full, h + 1)
                            act.activation(hT[:, h // 2, 0:SEQ], acc[:, 4 + (h // 2) % 2, :], ACT.Copy).then_inc(pv_out, 1)
                for b in (0, 2, 4, 6):
                    t.use(b)
                with act.Fori(0, DB) as b:
                    for g in range(NPAGES):
                        act.wait_ge(page_turned, b * NPAGES + (g + 1))
                        bank = 2 * (g % 2)
                        act.activation(kT[:, g % 2].rearrange("p m k -> p (m k)"),
                                       acc[:, bank:bank + 2, :].rearrange("p b n -> p (b n)"), ACT.Copy).then_inc(kt_out, 1)
                    act.wait_ge(zx_done, b + 1)
                    act.activation(z[0:NS, NPAGES, :], z[0:NS, NPAGES, :], ACT.Exp).then_inc(zexp_done, 1)
                    act.wait_ge(acc_out[6], b * 4 + (t.out[6] + 3))
                    act.activation(z[:, 0:NPAGES, :], z[:, 0:NPAGES, :], ACT.Exp).then_inc(zexp_done, 1)
                for bank, n in ((4, 1), (5, 1), (6, 4)):
                    t.use(bank, DB * n)
                t.out[7] += DB
                read_y(1, big)

            def conv():
                for k in range(KD):
                    act.wait_ge(x_done, t.x - KD + k + 1)
                    act.activation(hT[:, k, :], xT[:, k, :], ACT.Square).then_inc(sq_done, 1)
                t.sq += KD
                root_of_mean()
                for k in range(KD):
                    bank = 2 * (k % 4)
                    act.wait_ge(acc_full[bank], t.full[bank] + 1)
                    act.activation(ext_s[:, k, :, 0:CB], acc[:, bank, 0:2 * SR].rearrange("p (b w) -> p b w", b=DB),
                                   ACT.Copy).then_inc(acc_out[bank], 1)
                    t.use(bank)
                b0, o = t.blk, list(t.out)
                with act.Fori(0, KD // 2) as it:
                    for a in range(2):
                        act.wait_ge(blk_done, it * RING + (b0 + 2 * a + 2))
                        act.wait_ge(acc_out[4 * a], it + o[4 * a])
                        act.activation(two(sil[:, a, :]), acc2(4 * a + 2), ACT.Sigmoid,
                                       bias=vecs[:, ds(it * 2 + (col["b1"] + KD + a), 1)]).then_inc(acc_out[4 * a + 2], 1)
                t.blocks(2 * KD, uses=KD // 2)
                for a in (0, 4):
                    act.wait_ge(acc_out[a], t.out[a])
                act.activation(st_new, ext_s[:, :, :, DS:ES], ACT.Copy).then_inc(packed, 1)
                act.wait_ge(acc_full[0], t.full[0] + 1)
                act.wait_ge(rstd_done, rstds[0])
                act.activation(two(root[:]), acc2(0), ACT.Copy, scale=1.0 / D).then_inc(acc_out[0], 1)
                t.use(0)
                base = t.x
                for k in range(KD):
                    act.wait_ge(mean_done, k + 1)
                    act.activation(hT[:, k, :], dw[:, k, :], ACT.Square).then_inc(sq_done, 1)
                t.sq += KD
                act.wait_ge(acc_full[2], t.full[2] + 1)
                act.activation(cp_rows, acc[0:CB, 2:4, :].rearrange("p b n -> p (b n)"), ACT.Copy).then_inc(acc_out[2], 1)
                t.use(2)
                for r in range(2):
                    bank = 4 + 2 * r
                    act.wait_ge(acc_full[bank], t.full[bank] + 1)
                    act.activation(cs_rows[:, r, :], acc[0:SR, bank:bank + 2, :].rearrange("p b n -> p (b n)"), ACT.Copy)\
                       .then_inc(acc_out[bank], 1)
                    t.use(bank)
                root_of_mean(eps=1)
                for b in (2, 4, 6):
                    act.wait_ge(acc_out[b], t.out[b])
                store(cv_p[0, 0], cp_rows, nat_out)
                store(cv_s[0].rearrange("(r b) w n -> (b w) r n", r=2), cs_rows, nat_out)
                for k in range(KD):
                    act.wait_ge(scaled_done, k + 1)
                    act.activation(hT[:, k, :], dw[:, k, :], ACT.Silu, bias=vcol("lnb", k), scale=vcol("lng", k))\
                       .then_inc(silu_done, 1)
                for m in range(KD):
                    act.wait_ge(blk_done, t.blk + m + 1)
                    act.activation(two(yT[:, m, :]), acc2(2 * (m % 4)), ACT.Identity, bias=vcol("b2", m))
                    act.activation(two(big[:, m, :]), acc2(2 * (m % 4)), ACT.Square, bias=vcol("b2", m))\
                       .then_inc(acc_out[2 * (m % 4)], 1)
                t.blocks(KD, uses=2)
                root_of_mean()
                t.x += KD
                act.wait_ge(nat_out, 16 * (PT + 7))

            for i in range(depth):
                kind, j = i % 3, i // 3
                if kind == 0:
                    gla(j)
                elif kind == 1:
                    fox()
                else:
                    conv()
                ffn()
            act.wait_ge(x_done, t.x)
            for tt in range(PT + 1):
                n = P if tt < PT else NS
                bank = 2 * (tt % 4)
                act.wait_ge(acc_full[bank], t.full[bank] + 1)
                act.activation(xin[0:n, tt, :], acc[0:n, bank:bank + 2, :].rearrange("p b n -> p (b n)"), ACT.Copy)\
                   .then_inc(acc_out[bank], 1)
                t.use(bank)
                act.wait_ge(acc_out[bank], t.out[bank])
                dst = y_prompt[0, tt * P:(tt + 1) * P, :] if tt < PT else y_sample.rearrange("b s n -> (b s) n")
                act.dma_start(dst, xin[0:n, tt, :]).then_inc(out_in, 16)
                outputs.append(dst)
            act.wait_ge(out_in, 16 * len(outputs))
            act.wait_ge(state_out, 16 * ((depth + 2) // 3))


_OUTS = [("y_prompt", (1, 512, 1024)), ("y_sample", (8, 4, 1024)),
         ("gla_sp", (2, 1, 4, 128, 256)), ("gla_ss", (2, 8, 4, 128, 256)),
         ("fox_kp", (1, 1, 512, 16, 64)), ("fox_vp", (1, 1, 512, 16, 64)), ("fox_lp", (1, 1, 512, 16)),
         ("fox_ks", (1, 8, 4, 16, 64)), ("fox_vs", (1, 8, 4, 16, 64)), ("fox_ls", (1, 8, 4, 16)),
         ("cv_p", (1, 1, 30, 1024)), ("cv_s", (1, 8, 30, 1024))]
_INS = ['x_prompt', 'x_sample', 'state_gla', 'cache_fox_k', 'cache_fox_v', 'cache_fox_logf', 'state_conv', 'page_table',
        'norm_g', 'gla_wq', 'gla_wk', 'gla_wv', 'gla_wg1', 'gla_wg2', 'gla_bg', 'gla_wr', 'gla_gn', 'gla_wo',
        'fox_wq', 'fox_wk', 'fox_wv', 'fox_wf', 'fox_bf', 'fox_wo', 'conv_w1', 'conv_b1', 'conv_wdw', 'conv_bdw',
        'conv_ln_g', 'conv_ln_b', 'conv_w2', 'conv_b2', 'ffn_w1', 'ffn_w3', 'ffn_w2']


def kernel(**inputs):
    import numpy as _np
    import concourse.bacc as _bacc
    from concourse import mybir as _mybir
    from concourse.bass_utils import run_bass_kernel_spmd as _run

    nc = _bacc.Bacc("TRN2", target_bir_lowering=False, num_devices=1)
    arrays, ins = {}, []
    for name in _INS:
        a = _np.ascontiguousarray(inputs[name])
        arrays[f"in_{name}"] = a
        ins.append(nc.dram_tensor(f"in_{name}", a.shape, _mybir.dt.from_np(a.dtype), kind="ExternalInput").ap())
    outs = [nc.dram_tensor(f"out_{n}", s, _mybir.dt.float32, kind="ExternalOutput").ap() for n, s in _OUTS]
    build(nc, ins, outs)
    r = _run(nc, [arrays], core_ids=[0])
    return tuple(r.results[0][f"out_{n}"] for n, _ in _OUTS)
```

```python
from contextlib import ExitStack

import numpy as np
import concourse.bass as bass
import concourse.mybir as mybir

F32 = mybir.dt.float32
F32R = mybir.dt.float32r
U32 = mybir.dt.uint32
ALU = mybir.AluOpType
ACT = mybir.ActivationFunctionType
AX = mybir.AxisListType
ds = bass.ds

P = 128
RING = 4
GLA_CHUNK = 64
RMS_EPS, LN_EPS = 1e-6, 1e-5
NEG = -1e30


class Tally:

    def __init__(self):
        self.blk = 0
        self.out = [0] * 8
        self.full = [0] * 8
        self.split = 0
        self.pair = 0
        self.sum = 0
        self.sq = self.h = self.hhi = self.z = self.x = self.o = 0

    def blocks(self, n, banks=(0, 2, 4, 6), uses=0):
        self.blk += n
        for b in banks:
            self.out[b] += uses

    def use(self, bank, n=1):
        self.out[bank] += n
        self.full[bank] += n


def build(nc, T_in, T_out, depth=4):
    (x_prompt, x_sample, state_gla, cache_k, cache_v, cache_lf, state_conv, page_table, norm_g,
     gla_wq, gla_wk, gla_wv, gla_wg1, gla_wg2, gla_bg, gla_wr, gla_gn, gla_wo,
     fox_wq, fox_wk, fox_wv, fox_wf, fox_bf, fox_wo,
     conv_w1, conv_b1, conv_wdw, conv_bdw, conv_ln_g, conv_ln_b, conv_w2, conv_b2,
     ffn_w1, ffn_w3, ffn_w2) = T_in
    (y_prompt, y_sample, gla_sp, gla_ss, fox_kp, fox_vp, fox_lp, fox_ks, fox_vs, fox_ls, cv_p, cv_s) = T_out

    _, SEQ, D = x_prompt.shape
    DB, DS, _ = x_sample.shape
    DEPTH = norm_g.shape[0]
    NS = DB * DS
    TOK = SEQ + NS
    HALF = TOK // 2
    KD = D // P
    D_FF = ffn_w1.shape[2]
    KF = D_FF // P
    KF2 = KF // 2
    PT = SEQ // P
    GH, DK, DV = state_gla.shape[2:]
    RANK = gla_wg1.shape[2]
    VH = DV // P
    NCH = SEQ // GLA_CHUNK
    NPOOL, PAGE, FH, DH = cache_k.shape[1:]
    NPAGES = page_table.shape[1]
    PAIRS = FH // 2
    CW = conv_wdw.shape[1]
    CB = CW - 1
    assert GH * DK == 4 * P and GH * DV == D and FH * DH == D and DH == 64 and PAGE == P and DK == P
    assert HALF <= 512 and KF % 2 == 0 and NS == 32 and DS == 4 and KD == 8 and SEQ == 4 * P

    ctx = ExitStack()

    def sb(name, shape, dt=F32):
        return ctx.enter_context(nc.sbuf_tensor(name, shape, dt))

    def sem(name):
        return ctx.enter_context(nc.semaphore(name))

    with ctx:
        at_sb = [(nc.sbuf_base + 31) // 32 * 32]

        def placed(name, shape):
            where = at_sb[0]
            at_sb[0] += 4 * int(np.prod(shape[1:]))
            return sb(name, shape), where

        xT, _ = placed("xT", [P, KD, TOK])
        hT, hT_at = placed("hT", [P, KD, TOK])
        yT, yT_at = placed("yT", [P, KD, TOK])
        big, big_at = placed("big", [P, KF, TOK])
        mix, mix_at = placed("mix", [P, 17664])
        ring = sb("ring", [P, RING, KF2 * P])
        sil = sb("sil", [P, 2, TOK])
        root = sb("root", [P, TOK])
        rstd = sb("rstd", [P, TOK])
        vecs = sb("vecs", [P, 4 * P])
        ident = sb("ident", [P, P])
        ones = sb("ones", [P, P])
        strict = sb("strict", [P, P])
        causal = sb("causal", [P, P])
        reset = sb("reset", [P, TOK])
        m_chunk = sb("m_chunk", [P, P])
        m_le = sb("m_le", [NS, DB, DS])
        m_gt = sb("m_gt", [NS, DB, DS])
        m_in = sb("m_in", [NS, DB])
        epsb = sb("epsb", [P, 2])
        onehot = sb("onehot", [P, FH])
        sel_i = sb("sel_i", [DS, P])
        newm = sb("newm", [DS, DB, NS])
        wg1_sb = sb("wg1_sb", [P, KD, RANK])
        fbias = sb("fbias", [FH, 1])
        pt_sb = sb("pt_sb", [1, DB * NPAGES], mybir.dt.int32)
        SPLITS = 2
        h_hi = nc.alloc_sbuf_tensor_at("h_hi", [P, KD, TOK], F32R, offset=yT_at)
        h_lo = nc.alloc_sbuf_tensor_at("h_lo", [P, KD, TOK], F32R, offset=hT_at)
        g_hi = nc.alloc_sbuf_tensor_at("g_hi", [P, KF, TOK], F32R, offset=big_at)
        g_lo = nc.alloc_sbuf_tensor_at("g_lo", [P, KF, TOK], F32R, offset=mix_at)
        wsp = nc.alloc_sbuf_tensor_at("wsp", [P, SPLITS, 2, KF2 * P], F32R, offset=mix_at + 4 * KF * TOK)
        assert KF * TOK + SPLITS * 2 * KF2 * P <= 17664
        wg2_sb = sil[0:RANK, 1, 0:GH * DK]
        lowr = sil[0:RANK, 0, :]
        acc = ctx.enter_context(nc.psum_tensor("acc", [P, 8, 512], F32))

        def acc2(bank):
            return acc[:, bank:bank + 2, 0:HALF]

        def accflat(bank):
            return acc[:, bank:bank + 2, :].rearrange("p b n -> p (b n)")[:, 0:TOK]

        def two(ap):
            return ap.rearrange("p (h t) -> p h t", h=2)

        def part(at, n, rows=P):
            return mix[0:rows, at:at + n]

        v_nat = part(0, (PT + 1) * D).rearrange("p (t n) -> p t n", t=PT + 1)
        M0 = (PT + 1) * D
        kd_nat = part(M0, (PT + 1) * GH * DK).rearrange("p (t h k) -> p t h k", t=PT + 1, h=GH)
        g_diff = part(M0, GH * TOK).rearrange("p (h t) -> p h t", h=GH)
        M1 = M0 + (PT + 1) * GH * DK
        att = part(M1, PT * GH * P).rearrange("p (t h s) -> p t h s", t=PT, h=GH)
        M2 = M1 + PT * GH * P
        att_s = part(M2, GH * NS, NS).rearrange("p (h s) -> p h s", h=GH)
        M3 = M2 + GH * NS
        S = part(M3, GH * DV).rearrange("p (h v) -> p h v", h=GH)
        M4 = M3 + GH * DV
        st = part(M4, 2 * 2 * GH * DV).rearrange("p (r b h v) -> p r b h v", r=2, b=2, h=GH)
        M5 = M4 + 4 * GH * DV
        kd_b = part(M5, 2 * GH * DK, NS).rearrange("p (r h k) -> p r h k", r=2, h=GH)
        assert M5 + 2 * GH * DK <= 17664
        pages = part(M0, 8 * D).rearrange("p (r n) -> p r n", r=8)
        F1 = M0 + 8 * D
        kT = part(F1, 2 * D).rearrange("p (r m k) -> p r m k", r=2, m=PAIRS)
        F2 = F1 + 2 * D
        GR = 4
        GH4 = FH // GR
        ROWS = GH4 * DS
        lfx = part(F2, NPAGES * FH * DS).rearrange("p (g n) -> p g n", g=NPAGES)
        picked = part(F2, DB * NPAGES * FH).rearrange("p (b g h) -> p b g h", b=DB, g=NPAGES)
        assert F2 + DB * NPAGES * FH <= 17664
        pT = part(M0 + 4 * D, 2 * PT * SEQ).rearrange("p (r k q) -> p r k q", r=2, k=PT)
        k_rows = part(M0, PT * D).rearrange("p (t n) -> p t n", t=PT)
        probs = part(F1, 2 * SEQ).rearrange("p (r k) -> p r k", r=2)
        k_rows_s = part(F1 + 2 * SEQ, D, NS)
        yflat = yT[:].rearrange("p k t -> p (k t)")
        LFN = DB * NPAGES * FH
        lf = yflat[:, 0:LFN].rearrange("p (b g h) -> p b g h", b=DB, g=NPAGES)
        later = yflat[:, LFN:2 * LFN].rearrange("p (b g h) -> p b g h", b=DB, g=NPAGES)
        KEYS = NPAGES * PAGE
        z = yflat[:, LFN:LFN + KEYS + NS]
        mflat = big[:, 2 * KD:KF, :].rearrange("p k t -> p (k t)")
        at_m = [0]

        def small_part(n, rows=P):
            at_m[0] += n
            assert at_m[0] <= mflat.shape[1]
            return mflat[0:rows, at_m[0] - n:at_m[0]]

        logf = small_part(TOK, FH)
        ncum = small_part(SEQ, FH)
        cumq = small_part(PT * FH).rearrange("p (t h) -> p t h", t=PT)
        lnat = small_part((PT + 1) * FH).rearrange("p (t h) -> p t h", t=PT + 1)
        qblk = small_part(DB * PAIRS * 2 * DS).rearrange("p (b m n) -> p b m n", b=DB, m=PAIRS)
        qz = small_part(GR * 2 * 32).rearrange("p (j q n) -> p j q n", j=GR, q=2)
        behind = small_part(DB * NPAGES)
        tot, aft = small_part(DB), small_part(DB)
        sufn = small_part(NS)
        newb = small_part(DB * NS).rearrange("p (b k) -> p b k", b=DB)
        lnx, lng = small_part(P, NS), small_part(P, NS)
        gt4 = small_part(DS, NS)
        orow = small_part(2 * P)
        nmx, ssum = small_part(1), small_part(1)
        ptb = sil[:, :, 0:512]
        l_e, l_u, l_m = (sil[0:FH, 0, :], sil[0:FH, 1, :], root[0:FH, :])
        nmax, rsum = small_part(4), small_part(4)
        HB = DB // 2
        SR = HB * CB
        st_rows = part(0, 2 * D, SR).rearrange("p (r n) -> p r n", r=2)
        cs_rows = part(2 * D, 2 * D, SR).rearrange("p (r n) -> p r n", r=2)
        cp_rows = part(4 * D, D, CB)
        st_new = part(5 * D, KD * DB * CB).rearrange("p (k b w) -> p k b w", k=KD, b=DB)
        bflat = big[:].rearrange("p k t -> p (k t)")
        EP, ES = CB + SEQ, CB + DS
        ext_p = bflat[:, 0:KD * EP].rearrange("p (k t) -> p k t", k=KD)
        ext_s = bflat[:, KD * EP:KD * (EP + DB * ES)].rearrange("p (k b t) -> p k b t", k=KD, b=DB)
        dw0 = KD * (EP + DB * ES)
        dw = bflat[:, dw0:dw0 + KD * TOK].rearrange("p (k t) -> p k t", k=KD)

        setup_in = sem("setup_in")
        vec_in = sem("vec_in")
        w_in = [sem(f"w_in{i}") for i in range(RING)]
        const_made = sem("const_made")
        blk_done = sem("blk_done")
        acc_full = [sem(f"acc_full{i}") for i in range(8)]
        acc_out = [sem(f"acc_out{i}") for i in range(8)]
        whi_done = sem("whi_done")
        wlo_done = sem("wlo_done")
        hhi_done = sem("hhi_done")
        silu_made = sem("silu_made")
        prod_done = sem("prod_done")
        g_done = sem("g_done")
        sum_done = sem("sum_done")
        xsq_done = sem("xsq_done")
        sq_done = sem("sq_done")
        rstd_done = sem("rstd_done")
        z_done = sem("z_done")
        x_done = sem("x_done")
        h_done = sem("h_done")
        o_done = sem("o_done")
        s_act = sem("s_act")
        s_dve = sem("s_dve")
        abs_done = sem("abs_done")
        soft_done = sem("soft_done")
        cum_done = sem("cum_done")
        decay_done = sem("decay_done")
        diff_done = sem("diff_done")
        kdec_done = sem("kdec_done")
        keys_done = sem("keys_done")
        state_out = sem("state_out")
        rows_in = sem("rows_in")
        ext_done = sem("ext_done")
        packed = sem("packed")
        conv_done = sem("conv_done")
        mean_done = sem("mean_done")
        scaled_done = sem("scaled_done")
        silu_done = sem("silu_done")
        pt_in = sem("pt_in")
        lf_in = sem("lf_in")
        pages_in = [sem(f"pages_in{i}") for i in range(8)]
        nat_out = sem("nat_out")
        fabs_done = sem("fabs_done")
        fexp_done = sem("fexp_done")
        fln_done = sem("fln_done")
        fu_done = sem("fu_done")
        logf_done = sem("logf_done")
        dmat_done = sem("dmat_done")
        later_done = sem("later_done")
        qblk_done = sem("qblk_done")
        pmax_done = sem("pmax_done")
        pexp_done = sem("pexp_done")
        p_done = sem("p_done")
        pv_full = sem("pv_full")
        pv_out = sem("pv_out")
        page_turned = sem("page_turned")
        kt_out = sem("kt_out")
        v_used = sem("v_used")
        prepared = sem("prepared")
        picked_done = sem("picked_done")
        scores_full = sem("scores_full")
        scores_out = sem("scores_out")
        mx_done = sem("mx_done")
        probs_done = sem("probs_done")
        pt_full = sem("pt_full")
        pt_out = sem("pt_out")
        orow_done = sem("orow_done")
        ot_full = sem("ot_full")
        ot_out = sem("ot_out")
        kdb_done = sem("kdb_done")
        out_in = sem("out_in")
        st_in = [sem("st_in0"), sem("st_in1")]
        st_out = [sem("st_out0"), sem("st_out1")]

        VROWS = [("norm", norm_g.rearrange("l w (k p) -> (l w k) p", p=P))]
        small = [("bg", gla_bg), ("gn", gla_gn), ("b1", conv_b1), ("bdw", conv_bdw), ("lng", conv_ln_g),
                 ("lnb", conv_ln_b), ("b2", conv_b2)]
        col, at = {"norm": 0}, P
        for name, v in small:
            VROWS.append((name, v.rearrange("l (k p) -> (l k) p", p=P)))
            col[name] = at
            at += v.shape[0] * v.shape[1] // P
        col["wdw"] = at = 2 * P
        taps = conv_wdw.rearrange("l w (k p) -> (l w k) p", p=P)
        VN = [P, sum(v.shape[0] * v.shape[1] for _, v in small) // P, P, CW * KD - P]
        vrow = [big[:, 5 * 2, i * P:(i + 1) * P] for i in range(4)]

        def vcol(name, k=0):
            c = col[name] + k
            return vecs[:, c:c + 1]

        def gcol(layer, which, k):
            return vcol("norm", (layer * 4 + which) * KD + k)

        xin = big[:, 0:10, :].rearrange("p u t -> p (u t)")[:, 0:(PT + 1) * D].rearrange("p (t n) -> p t n", t=PT + 1)

        SETUP_DMAS = 2 + 1 + len(small) + 2

        def w_view(w):
            return w.rearrange("(k p) n -> p k n", p=P)

        outputs = []
        N_CONST = 32
        VEC_FOX = 64

        block = ctx.enter_context(nc.Block())

        @block.sync
        def _(sp):
            t = Tally()
            def load(view, ktiles, k0, m, slot, used, n):
                if used is not None:
                    sp.wait_ge(used, n)
                sp.dma_start(ring[:, slot, 0:ktiles * P].rearrange("p (k n) -> p k n", k=ktiles),
                             view[:, k0:k0 + ktiles, ds(m * P, P)]).then_inc(w_in[slot], 16)

            first_peeled = [0]

            def first(of, tiles, fresh=[True]):
                if t.blk == 0 or split_before[0]:
                    for j in range(RING):
                        view, m = of(j)
                        if t.blk == 0:
                            load(view, KD, 0, m, j, None, 0)
                        else:
                            load(view, KD, 0, m, j, wlo_done, t.split - (RING - 1) + j)
                    split_before[0] = False
                    first_peeled[0] = 1

            split_before = [False]

            def load_plain(view, tiles):
                first(lambda m: (view, m), tiles)
                if tiles > RING:
                    with sp.Fori(0, tiles // RING - first_peeled[0]) as it:
                        for j in range(RING):
                            load(view, KD, 0, (it + first_peeled[0]) * RING + j, j, blk_done,
                                 (it + first_peeled[0]) * RING + (t.blk + j + 1 - RING))
                elif not first_peeled[0]:
                    for j in range(RING):
                        load(view, KD, 0, j, j, blk_done, t.blk + j + 1 - RING)
                first_peeled[0] = 0
                t.blocks(tiles)

            def load_pairs(va, vb, tiles):
                first(lambda j: (va if j % 2 == 0 else vb, j // 2), tiles)
                with sp.Fori(0, tiles // 2 - 1) as it:
                    for j in range(RING):
                        load(va if j % 2 == 0 else vb, KD, 0, (it + 1) * 2 + j // 2, j, blk_done,
                             it * RING + (t.blk + j + 1))
                first_peeled[0] = 0
                t.blocks(2 * tiles)

            def store(dst, src):
                sp.dma_start(dst, src).then_inc(out_in, 16)
                outputs.append(dst)

            sp.dma_start(xin[:, 0:PT, :], x_prompt[0].rearrange("(t p) n -> p t n", p=P)).then_inc(setup_in, 16)
            sp.dma_start(xin[0:NS, PT, :], x_sample.rearrange("b s n -> (b s) n")).then_inc(setup_in, 16)
            sp.dma_start(vrow[0], VROWS[0][1]).then_inc(setup_in, 16)
            for name, v in VROWS[1:]:
                r = col[name] - P
                sp.dma_start(vrow[1][r:r + v.shape[0], :], v).then_inc(setup_in, 16)
            sp.dma_start(vrow[2], taps[0:P]).then_inc(setup_in, 16)
            sp.dma_start(vrow[3][0:VN[3], :], taps[P:CW * KD]).then_inc(setup_in, 16)

            def gla(j):
                if j > 0:
                    sp.wait_ge(blk_done, t.blk)
                sp.dma_start(wg1_sb[:], gla_wg1[j].rearrange("(k p) r -> p k r", p=P)).then_inc(vec_in, 16)
                sp.dma_start(wg2_sb, gla_wg2[j]).then_inc(vec_in, 16)
                load_plain(w_view(gla_wq[j]), GH)
                load_plain(w_view(gla_wk[j]), GH)
                load_plain(w_view(gla_wr[j]), KD)
                load_plain(w_view(gla_wv[j]), KD)
                for g in range(DB // 2):
                    if g >= 2:
                        sp.wait_ge(st_out[g % 2], 16 * (g // 2 + 2 * j))
                    elif j > 0:
                        sp.wait_ge(st_out[g % 2], 16 * 2 * j)
                    sp.dma_start(st[:, g % 2], state_gla[j, 2 * g:2 * g + 2].rearrange("b h k v -> k b h v"))\
                      .then_inc(st_in[g % 2], 16)
                load_plain(w_view(gla_wo[j]), KD)
                sp.dma_start(gla_sp[j, 0].rearrange("h k v -> k h v"), S).then_inc(state_out, 16)

            def ffn(i):
                up = (w_view(ffn_w1[i]), w_view(ffn_w3[i]))
                for j in range(RING):
                    load(up[j % 2], KD, 0, j // 2, j, blk_done, t.blk + j + 1 - RING)
                with sp.Fori(0, KF // 2 - 1) as it:
                    for j in range(RING):
                        load(up[j % 2], KD, 0, (it + 1) * 2 + j // 2, j, wlo_done, it * RING + (t.split + j + 1))
                w2 = w_view(ffn_w2[i])
                t.blocks(2 * KF)
                t.split += 2 * KF
                with sp.Fori(0, KD // 4) as it:
                    for b in range(8):
                        load(w2, KF2, (b % 2) * KF2, it * 4 + b // 2, b % RING, wlo_done,
                             it * 8 + (t.split + b + 1 - RING))
                t.blocks(2 * KD)
                t.split += 2 * KD
                split_before[0] = True

            def fox():
                sp.wait_ge(blk_done, t.blk)
                sp.dma_start(wg1_sb[:], fox_wf[0].rearrange("(k p) r -> p k r", p=P)).then_inc(vec_in, 16)
                sp.dma_start(fbias[:], fox_bf.rearrange("a h -> h a")).then_inc(vec_in, 16)
                sp.dma_start(pt_sb[:], page_table.rearrange("(a b) g -> a (b g)", a=1)).then_inc(pt_in, 16)
                load_plain(w_view(fox_wq[0]), KD)
                load_plain(w_view(fox_wk[0]), KD)

                sp.wait_ge(pt_in, 16)
                load_plain(w_view(fox_wv[0]), KD)
                sp.wait_ge(nat_out, 16 * (PT + 5))
                sp.wait_ge(pv_out, PAIRS)
                sp.nop()

                regs = [sp.alloc_register(f"page{g}") for g in range(NPAGES)]

                def page_numbers(b):
                    sp.load(regs, pt_sb[0:1, ds(b * NPAGES, NPAGES)])
                    return [sp.snap(r, min_val=0, max_val=NPOOL - 1) for r in regs]

                def load_page(numbers, s):
                    cache = cache_k if s < NPAGES else cache_v
                    sp.dma_start(pages[:, s % 8, :],
                                 cache[0, ds(numbers[s % NPAGES], 1)].rearrange("a p h d -> p (a h d)"))\
                      .then_inc(pages_in[s % 8], 16)

                def first_pages(b, numbers, reuse):
                    for s in range(8):
                        if reuse:
                            sp.wait_ge(v_used, b * NPAGES + (s + 24 - NPAGES + 1 - NPAGES))
                        load_page(numbers, s)

                def other_pages(b, numbers):
                    for s in range(8, 2 * NPAGES):
                        if s - 8 < NPAGES:
                            sp.wait_ge(page_turned, b * NPAGES + (s - 8 + 1))
                        else:
                            sp.wait_ge(v_used, b * NPAGES + (s - 8 - NPAGES + 1))
                        load_page(numbers, s)

                first_pages(0, page_numbers(0), False)
                with sp.Fori(0, DB - 1) as b:
                    other_pages(b, page_numbers(b))
                    first_pages(b + 1, page_numbers(b + 1), True)
                other_pages(DB - 1, page_numbers(DB - 1))
                load_plain(w_view(fox_wo[0]), KD)

            def conv():
                w1 = w_view(conv_w1[0])
                first(lambda j: (w1[:, :, (j % 2) * D:(j % 2 + 1) * D], j // 2), KD)
                sp.wait_ge(blk_done, t.blk)
                sp.dma_start(st_rows, state_conv[0].rearrange("(r b) w n -> (b w) r n", r=2)).then_inc(rows_in, 16)
                load_pairs(w1[:, :, 0:D], w1[:, :, D:2 * D], KD)
                load_plain(w_view(conv_w2[0]), KD)

            for i in range(depth):
                kind, j = i % 3, i // 3
                if kind == 0:
                    gla(j)
                elif kind == 1:
                    fox()
                else:
                    conv()
                ffn(i)

        @block.gpsimd
        def _(pool):
            made = [0]

            def made_by(ins):
                made[0] += 1
                ins.then_inc(const_made, 1)

            def select(out, pattern, base, mult, fill, compare=ALU.is_ge):
                pool.wait_ge(const_made, made[0])
                made_by(pool.affine_select(out=out, in_=out, compare_op=compare, fill=fill, base=base,
                                           pattern=pattern, channel_multiplier=mult))

            made_by(pool.memset(ident[:], 0.0))
            select(ident[:], [[-1, P]], 0, 1, 1.0, ALU.not_equal)
            made_by(pool.memset(ones[:], 1.0))
            made_by(pool.memset(epsb[:, 0:1], RMS_EPS))
            made_by(pool.memset(epsb[:, 1:2], LN_EPS))
            made_by(pool.memset(strict[:], 1.0))
            select(strict[:], [[-1, P]], -1, 1, 0.0)
            made_by(pool.memset(causal[:], 0.0))
            select(causal[:], [[-1, P]], 0, 1, NEG)
            made_by(pool.memset(reset[:], 1.0))
            pool.wait_ge(const_made, made[0])
            made_by(pool.memset(reset[:, 0:SEQ:GLA_CHUNK], 0.0))
            made_by(pool.memset(reset[:, SEQ:TOK:DS], 0.0))
            made_by(pool.memset(m_chunk[:], 1.0))
            mc = m_chunk[:].rearrange("p (c t) -> p c t", t=GLA_CHUNK)
            select(mc, [[-GLA_CHUNK, P // GLA_CHUNK], [0, GLA_CHUNK]], 0, 1, 0.0)
            select(mc, [[GLA_CHUNK, P // GLA_CHUNK], [1, GLA_CHUNK]], 0, -1, 0.0)
            made_by(pool.memset(m_le[:], 1.0))
            select(m_le[:], [[-DS, DB], [0, DS]], 0, 1, 0.0)
            select(m_le[:], [[DS, DB], [1, DS]], 0, -1, 0.0)
            made_by(pool.memset(m_gt[:], 1.0))
            select(m_gt[:], [[-DS, DB], [-1, DS]], -1, 1, 0.0)
            select(m_gt[:], [[DS, DB], [0, DS]], DS - 1, -1, 0.0)
            made_by(pool.memset(m_in[:], 1.0))
            select(m_in[:], [[-DS, DB]], 0, 1, 0.0)
            select(m_in[:], [[DS, DB]], DS - 1, -1, 0.0)
            made_by(pool.memset(onehot[:], 1.0))
            oh = onehot[:].rearrange("p (j c) -> p j c", j=GR)
            select(oh, [[-32, GR], [-DS, GH4]], 0, 1, 0.0)
            select(oh, [[32, GR], [DS, GH4]], DS - 1, -1, 0.0)
            made_by(pool.memset(sel_i[:], 1.0))
            select(sel_i[:].rearrange("p (g i) -> p g i", i=DS), [[0, P // DS], [1, DS]], 0, -1, 0.0, ALU.is_equal)
            made_by(pool.memset(newm[:], 0.0))
            nm = newm[:].rearrange("p b (c j) -> p b c j", j=DS)
            select(nm, [[-1, DB], [1, DB], [0, DS]], 0, 0, NEG, ALU.is_equal)
            select(nm, [[0, DB], [0, DB], [-1, DS]], 0, 1, NEG)
            assert made[0] == N_CONST, made[0]

            n_post = [0]
            for n in range(2 * depth):
                if n == 2:
                    pool.wait_ge(x_done, 2 * KD)
                    pool.wait_ge(pt_in, 16)
                    with pool.Fori(0, DB) as b:
                        for g in range(NPAGES):
                            page = pool.value_load(pt_sb[0:1, ds(b * NPAGES + g, 1)], min_val=0, max_val=NPOOL - 1)
                            pool.dma_start(lf[:, ds(b, 1), g, :].rearrange("p a h -> p (a h)"),
                                           cache_lf[0, ds(page, 1)].rearrange("a p h -> p (a h)")).then_inc(lf_in, 16)

                    def prepare(b):
                        for q in range(2):
                            pool.tensor_copy(qz[:, :, q, q * 2 * DS:(q + 1) * 2 * DS],
                                             qblk[:, ds(b, 1), q:PAIRS:2, :].rearrange("p a m n -> p (a m) n"))
                        pool.tensor_copy(lfx.rearrange("p g (h i) -> p g h i", i=DS),
                                         lf[:, ds(b, 1)].rearrange("p a g (h i) -> p (a g) h i", i=1)
                                         .to_broadcast([P, NPAGES, FH, DS])).then_inc(prepared, 1)

                    pool.wait_ge(qblk_done, 1)
                    pool.wait_ge(lf_in, 16 * DB * NPAGES)
                    pool.wait_ge(picked_done, 1)
                    prepare(0)
                    with pool.Fori(0, DB - 1) as b:
                        pool.wait_ge(scores_full, b * 5 + 5)
                        prepare(b + 1)
                for k in range(KD):
                    pool.wait_ge(z_done, KD * n_post[0] + k + 1)
                    pool.tensor_tensor(xT[:, k, :], xT[:, k, :], yT[:, k, :], ALU.add).then_inc(x_done, 1)
                n_post[0] += 1

        @block.tensor
        def _(pe):
            t = Tally()
            def block_mm(slot, bank, ktiles, k0, rhs, start, stop):
                for k in range(ktiles):
                    for h in range(2):
                        last = pe.matmul(acc[:, bank + h, 0:HALF], ring[:, slot, k * P:(k + 1) * P],
                                         rhs[:, k0 + k, h * HALF:(h + 1) * HALF],
                                         start=start and k == 0, stop=stop and k == ktiles - 1)
                last.then_inc(blk_done, 1)

            def project(tiles, first=False):
                b0, o = t.blk, list(t.out)

                def body(it):
                    for j in range(RING):
                        pe.wait_ge(w_in[j], 16 * (it + (b0 // RING + 1)))
                        pe.wait_ge(acc_out[2 * j], it + o[2 * j])
                        block_mm(j, 2 * j, KD, 0, hT, True, True)

                if tiles == RING:
                    body(0)
                else:
                    with pe.Fori(0, tiles // RING) as it:
                        body(it)
                t.blocks(tiles, uses=tiles // RING)

            def project_tokens(tiles):
                b0, o = t.blk, list(t.out)
                with pe.Fori(0, tiles // RING) as it:
                    for j in range(RING):
                        pe.wait_ge(w_in[j], 16 * (it + (b0 // RING + 1)))
                        pe.wait_ge(acc_out[2 * j], it + o[2 * j])
                        for tt in range(PT + 1):
                            n = P if tt < PT else NS
                            for k in range(KD):
                                last = pe.matmul(acc[0:n, 2 * j + tt // PT, (tt % PT) * P:(tt % PT + 1) * P],
                                                 hT[:, k, tt * P:tt * P + n], ring[:, j, k * P:(k + 1) * P],
                                                 start=(k == 0), stop=(k == KD - 1))
                        last.then_inc(blk_done, 1)
                t.blocks(tiles, uses=tiles // RING)

            def wait_banks(banks=range(8)):
                for b in banks:
                    if t.out[b]:
                        pe.wait_ge(acc_out[b], t.out[b])

            def split_mm(s, bank, ktiles, k0, hi, lo, start, stop, ready=None):
                for k in range(ktiles):
                    if ready:
                        ready(k)
                    for w, rhs in ((0, hi), (0, lo), (1, hi)):
                        for h in range(2):
                            last = pe.matmul(acc[:, bank + h, 0:HALF], wsp[:, s, w, k * P:(k + 1) * P],
                                             rhs[:, k0 + k, h * HALF:(h + 1) * HALF],
                                             start=start and k == 0 and w == 0 and rhs is hi,
                                             stop=stop and k == ktiles - 1 and w == 1)
                last.then_inc(blk_done, 1)

            def norm_total(bank, steps):
                t.sum += steps
                pe.wait_ge(sum_done, t.sum)
                pe.wait_ge(acc_out[bank], t.out[bank])
                for h in range(2):
                    last = pe.matmul(acc[:, bank + h, 0:HALF], ones[:], rstd[:, h * HALF:(h + 1) * HALF],
                                     start=True, stop=True)
                last.then_inc(acc_full[bank], 1)
                t.use(bank)

            def norm_sum(squares, evacuated):
                pe.wait_ge(acc_out[0], t.out[0])
                for k in range(KD):
                    if evacuated:
                        pe.wait_ge(acc_out[2 * (k % 4)], t.out[2 * (k % 4)] - 1 + k // 4)
                    else:
                        pe.wait_ge(sq_done, t.sq + k + 1)
                    for h in range(2):
                        last = pe.matmul(acc[:, h, 0:HALF], ones[:], squares[:, k, h * HALF:(h + 1) * HALF],
                                         start=(k == 0), stop=(k == KD - 1))
                last.then_inc(acc_full[0], 1)
                if not evacuated:
                    t.sq += KD
                t.use(0)

            def h_ready():
                t.h += KD
                pe.wait_ge(h_done, t.h)

            def o_ready():
                t.o += KD
                pe.wait_ge(o_done, t.o)

            pe.wait_ge(const_made, 2)
            pe.wait_ge(setup_in, 16 * SETUP_DMAS)
            for k in range(KD):
                bank = 2 * (k % 4)
                if k >= 4:
                    pe.wait_ge(acc_out[bank], 1)
                for tt in range(PT):
                    pe.transpose(acc[:, bank, tt * P:(tt + 1) * P], xin[:, tt, k * P:(k + 1) * P], ident[:])
                pe.transpose(acc[:, bank + 1, 0:NS], xin[0:NS, PT, k * P:(k + 1) * P], ident[0:NS, 0:NS])\
                  .then_inc(acc_full[bank], 1)
                t.use(bank)
            pe.wait_ge(acc_out[0], t.out[0])
            for g in range(4):
                last = pe.transpose(acc[:, 0, g * P:g * P + VN[g]], vrow[g][0:VN[g], :], ident[0:VN[g], 0:VN[g]])
            last.then_inc(acc_full[0], 1)
            t.use(0)
            pe.wait_ge(const_made, N_CONST)

            def gla(j):
                norm_sum(hT, False)
                h_ready()
                project(GH)
                project(GH)
                pe.wait_ge(vec_in, 32 * (j + 1) + (32 if j else 0))
                pe.wait_ge(acc_out[0], t.out[0])
                for k in range(KD):
                    for h in range(2):
                        last = pe.matmul(acc[0:RANK, h, 0:HALF], wg1_sb[:, k, :], hT[:, k, h * HALF:(h + 1) * HALF],
                                         start=(k == 0), stop=(k == KD - 1))
                last.then_inc(acc_full[0], 1)
                t.use(0)
                pe.wait_ge(acc_out[0], t.out[0])
                for m in range(GH):
                    bank = 2 * ((m + 1) % 4)
                    pe.wait_ge(acc_out[bank], t.out[bank])
                    for h in range(2):
                        last = pe.matmul(acc[:, bank + h, 0:HALF], wg2_sb[:, m * P:(m + 1) * P],
                                         lowr[:, h * HALF:(h + 1) * HALF], start=True, stop=True)
                    last.then_inc(acc_full[bank], 1)
                    t.use(bank)
                project(KD)
                project_tokens(KD)

                wait_banks()
                pe.wait_ge(keys_done, j + 1)
                for tt in range(PT + 1):
                    n = P if tt < PT else NS
                    bank = 4 * (tt % 2)
                    pe.wait_ge(acc_out[bank], t.out[bank])
                    pe.wait_ge(acc_out[bank + 1], t.out[bank + 1])
                    for h in range(GH):
                        last = pe.transpose(acc[0:n, bank, h * DK:(h + 1) * DK], big[:, 4 + h, tt * P:tt * P + n],
                                            ident[:])
                    last.then_inc(acc_full[bank], 1)
                    for h in range(GH):
                        last = pe.matmul(acc[0:n, bank + 1, h * P:h * P + n], yT[:, h, tt * P:tt * P + n],
                                         big[:, h, tt * P:tt * P + n], start=True, stop=True)
                    last.then_inc(acc_full[bank + 1], 1)
                    t.use(bank)
                    t.use(bank + 1)
                wait_banks((0, 1, 4, 5))
                for c in range(NCH):
                    tt, r0 = c // 2, GLA_CHUNK * (c % 2)
                    t0 = c * GLA_CHUNK
                    ob, ub = (0, 1)[c % 2], (2, 4)[c % 2]
                    pe.wait_ge(acc_out[ub], t.out[ub])
                    for h in range(GH):
                        last = pe.matmul(acc[:, ub + h // 2, (h % 2) * DV:(h % 2 + 1) * DV],
                                         kd_nat[r0:r0 + GLA_CHUNK, tt, h, :],
                                         v_nat[r0:r0 + GLA_CHUNK, tt, h * DV:(h + 1) * DV], start=True, stop=True)
                    last.then_inc(acc_full[ub], 1)
                    t.use(ub)
                    pe.wait_ge(acc_out[ob], t.out[ob])
                    if c > 0:
                        prev = (2, 4)[(c - 1) % 2]
                        pe.wait_ge(acc_out[prev], t.out[prev])
                    for h in range(GH):
                        for v in range(VH):
                            u = h * VH + v
                            dst = acc[:, ob, u * GLA_CHUNK:(u + 1) * GLA_CHUNK]
                            last = pe.matmul(dst, v_nat[:, tt, u * P:(u + 1) * P],
                                             att[:, tt, h, r0:r0 + GLA_CHUNK], start=True, stop=(c == 0))
                            if c > 0:
                                last = pe.matmul(dst, S[:, h, v * P:(v + 1) * P],
                                                 big[:, h, t0:t0 + GLA_CHUNK], start=False, stop=True)
                    last.then_inc(acc_full[ob], 1)
                    t.use(ob)
                pe.wait_ge(acc_out[0], t.out[0])
                for g in range(DB // 2):
                    pe.wait_ge(st_in[g % 2], 16 * (g // 2 + 1 + 2 * j))
                    if g == 0:
                        for u in range(KD):
                            pe.matmul(acc[:, 0, u * NS:(u + 1) * NS], v_nat[0:NS, PT, u * P:(u + 1) * P],
                                      att_s[:, u // VH, :], start=(u == 0), stop=False, skip_group_check=True)
                    for bb in range(2):
                        b = 2 * g + bb
                        for u in range(KD):
                            h, v = u // VH, u % VH
                            last = pe.matmul(acc[:, 0, u * NS + b * DS:u * NS + (b + 1) * DS],
                                             st[:, g % 2, bb, h, v * P:(v + 1) * P],
                                             big[:, h, SEQ + b * DS:SEQ + (b + 1) * DS],
                                             start=False, stop=(g == DB // 2 - 1), skip_group_check=True)
                        if b == DB - 1:
                            last.then_inc(acc_full[0], 1)
                            t.use(0)
                        ub = (2, 4)[b % 2]
                        pe.wait_ge(acc_out[ub], t.out[ub])
                        pe.wait_ge(kdb_done, DB * j + b + 1)
                        for h in range(GH):
                            last = pe.matmul(acc[:, ub + h // 2, (h % 2) * DV:(h % 2 + 1) * DV], kd_b[:, b % 2, h, :],
                                             v_nat[0:NS, PT, h * DV:(h + 1) * DV], start=True, stop=True)
                        last.then_inc(acc_full[ub], 1)
                        t.use(ub)
                wait_banks()
                for h in range(GH):
                    for v in range(VH):
                        pe.wait_ge(sq_done, t.sq + h * VH + v + 1)
                        for q in range(2):
                            last = pe.matmul(acc[:, 2 * h + q, 0:HALF], ones[:],
                                             yT[:, h * VH + v, q * HALF:(q + 1) * HALF],
                                             start=(v == 0), stop=(v == VH - 1))
                    last.then_inc(acc_full[2 * h], 1)
                    t.use(2 * h)
                t.sq += KD
                o_ready()
                project(KD)
                norm_total(0, KD - 1)

            def ffn():
                b0, o, s0 = t.blk, list(t.out), t.split

                def up(j, it, ready=None):
                    pe.wait_ge(wlo_done, it * RING + (s0 + j + 1))
                    pe.wait_ge(acc_out[2 * j], it + o[2 * j])
                    split_mm(j % SPLITS, 2 * j, KD, 0, h_hi, h_lo, True, True, ready)

                up(0, 0, lambda k: pe.wait_ge(h_done, t.h + k + 1))
                t.h += KD
                up(1, 0)
                norm_total(6, 3)
                o[6] += 1
                up(2, 0)
                up(3, 0)
                with pe.Fori(0, KF // 2 - 1) as it:
                    for j in range(RING):
                        up(j, it + 1)
                t.blocks(2 * KF, uses=KF // 2)
                b0, o, s0 = t.blk, list(t.out), t.split + 2 * KF
                pairs = t.pair + KF
                with pe.Fori(0, KD // 4) as it:
                    for b in range(8):
                        j, bank = b % RING, b // 2 * 2
                        pe.wait_ge(wlo_done, it * 8 + (s0 + b + 1))
                        if b == 0:
                            pe.wait_ge(g_done, pairs)
                        if b % 2 == 0:
                            pe.wait_ge(acc_out[bank], it + o[bank])
                        split_mm(j % SPLITS, bank, KF2, (b % 2) * KF2, g_hi, g_lo, b % 2 == 0, b % 2 == 1)
                t.blocks(2 * KD, uses=KD // 4)
                t.split += 2 * KF + 2 * KD
                t.pair += KF
                norm_total(0, KD - 1)

            def prompt_attention():
                items = [(h, q) for h in range(FH) for q in range(PT)]
                due = []
                for i in range(len(items) + 3):
                    if i < len(items):
                        h, q = items[i]
                        r0, bank = DH * (h % 2), i % 2
                        if i >= 2:
                            pe.wait_ge(acc_out[bank], t.out[bank])
                        n = (q + 1) * P
                        pe.matmul(acc[:, bank, 0:n], big[r0:r0 + DH, h // 2, q * P:(q + 1) * P],
                                  big[r0:r0 + DH, KD + h // 2, 0:n], start=True, stop=False)
                        pe.matmul(acc[:, bank, 0:n], ident[0:FH, h:h + 1].to_broadcast([FH, P]), ncum[:, 0:n],
                                  start=False, stop=True).then_inc(acc_full[bank], 1)
                        t.use(bank)
                    for h in due:
                        pe.wait_ge(acc_out[3], t.out[3])
                        r0, bank = DH * (h % 2), 4 + (h // 2) % 2
                        if h % 2 == 0 and h >= 4:
                            pe.wait_ge(pv_out, h // 2 - 1)
                        for k in range(PT):
                            last = pe.matmul(acc[r0:r0 + DH, bank, k * P:SEQ], v_nat[:, k, h * DH:(h + 1) * DH],
                                             pT[:, h % 2, k, k * P:SEQ], start=(k == 0), stop=(k == PT - 1))
                        last.then_inc(pv_full, 1)
                    due = []
                    if 2 <= i < len(items) + 2:
                        h, q = items[i - 2]
                        bank = 2 + (i % 2)
                        pe.wait_ge(p_done, i - 1)
                        pe.wait_ge(acc_out[bank], t.out[bank])
                        for k in range(q + 1):
                            last = pe.transpose(acc[:, bank, k * P:(k + 1) * P], probs[:, i % 2, k * P:(k + 1) * P], ident[:])
                        last.then_inc(acc_full[bank], 1)
                        t.use(bank)
                        if q == PT - 1:
                            due = [h]

            def sample_attention():
                with pe.Fori(0, DB) as b:
                    def q_mm(out_cols, bank, rhs, more):
                        for q in range(2):
                            for j in range(GR):
                                last = pe.matmul(acc[32 * j:32 * (j + 1), bank, out_cols], qz[:, j, q, :], rhs(2 * j + q),
                                                 start=(q == 0), stop=(q == 1 and not more), skip_group_check=True,
                                                 tile_position=(0, 32 * j))
                        return last

                    def scores(g):
                        cols = slice((g % 4) * PAGE, (g % 4 + 1) * PAGE)
                        bank = 4 + (g // 4) % 2
                        pe.wait_ge(kt_out, b * NPAGES + (g + 1))
                        if g % 4 == 0 and g >= 8:
                            pe.wait_ge(scores_out, b * 5 + g // 4)
                        q_mm(cols, bank, lambda m: kT[:, g % 2, m, :], True)
                        for j in range(GR):
                            last = pe.matmul(acc[32 * j:32 * j + ROWS, bank, cols], lfx[:, g, j * ROWS:(j + 1) * ROWS],
                                             strict[:], start=False, stop=True, skip_group_check=True,
                                             tile_position=(0, 32 * j))
                        if g % 4 == 3:
                            last.then_inc(scores_full, 1)

                    pe.wait_ge(prepared, b + 1)
                    q_mm(slice(256, 256 + NS), 7, lambda m: big[:, KD + m, SEQ:TOK], False).then_inc(scores_full, 1)
                    for g in range(NPAGES):
                        bank = 2 * (g % 2)
                        pe.wait_ge(pages_in[g % 8], b * 64 + 16 * (g // 8 + 1))
                        if g >= 2:
                            pe.wait_ge(kt_out, b * NPAGES + (g - 1))
                        for m in range(PAIRS):
                            last = pe.transpose(acc[:, bank + m // 4, (m % 4) * P:(m % 4 + 1) * P],
                                                pages[:, g % 8, m * P:(m + 1) * P], ident[:])
                        last.then_inc(page_turned, 1)
                        if g >= 1:
                            scores(g - 1)
                    scores(NPAGES - 1)

                    def turn(u):
                        if u:
                            pe.wait_ge(pt_out, b * 5 + u)
                            for g in range(4):
                                at = ((u - 1) * 4 + g) * PAGE
                                last = pe.transpose(acc[:, 6, g * P:(g + 1) * P], z[:, at:at + PAGE], ident[:])
                        else:
                            last = pe.transpose(acc[0:NS, 6, 0:P], z[:, KEYS:KEYS + NS], ident[:])
                        last.then_inc(pt_full, 1)

                    def weigh(u):
                        if u:
                            pe.wait_ge(pt_out, b * 5 + (u + 1))
                        else:
                            for j in range(GR):
                                pe.matmul(acc[32 * j:32 * (j + 1), 7, 0:256], ptb[0:NS, 0, 32 * j:32 * (j + 1)],
                                          v_nat[0:NS, PT, j * 256:(j + 1) * 256], start=True, stop=False,
                                          skip_group_check=True, tile_position=(0, 32 * j))
                            return
                        for g in range(4):
                            s = NPAGES + (u - 1) * 4 + g
                            pe.wait_ge(pages_in[s % 8], b * 64 + 16 * (s // 8 + 1))
                            for j in range(GR):
                                last = pe.matmul(acc[32 * j:32 * (j + 1), 7, 0:256],
                                                 ptb[:, u % 2, g * P + 32 * j:g * P + 32 * (j + 1)],
                                                 pages[:, s % 8, j * 256:(j + 1) * 256], start=False,
                                                 stop=(s == 2 * NPAGES - 1), skip_group_check=True,
                                                 tile_position=(0, 32 * j))
                            last.then_inc(v_used, 1)

                    pe.wait_ge(probs_done, b + 1)
                    turn(0)
                    for u in range(1, 5):
                        turn(u)
                        weigh(u - 1)
                    weigh(4)
                    pe.wait_ge(orow_done, b + 1)
                    for q in range(2):
                        last = pe.transpose(acc[:, 6, q * P:(q + 1) * P], orow[:, q * P:(q + 1) * P], ident[:])
                    last.then_inc(ot_full, 1)
                    pe.wait_ge(ot_out, b + 1)

            def fox():
                norm_sum(hT, False)
                h_ready()
                project(KD)
                project(KD)
                pe.wait_ge(vec_in, VEC_FOX)
                pe.wait_ge(acc_out[0], t.out[0])
                for k in range(KD):
                    for h in range(2):
                        last = pe.matmul(acc[0:FH, h, 0:HALF], wg1_sb[:, k, :], hT[:, k, h * HALF:(h + 1) * HALF],
                                         start=(k == 0), stop=(k == KD - 1))
                last.then_inc(acc_full[0], 1)
                t.use(0)
                project_tokens(KD)
                wait_banks()
                for tt in range(PT + 1):
                    n = P if tt < PT else NS
                    bank = 2 * (tt % 4)
                    pe.wait_ge(acc_out[bank], t.out[bank])
                    for k in range(KD):
                        last = pe.transpose(acc[0:n, bank + k // 4, (k % 4) * P:(k % 4 + 1) * P],
                                            big[:, KD + k, tt * P:tt * P + n], ident[:])
                    last.then_inc(acc_full[bank], 1)
                    t.use(bank)
                pe.wait_ge(logf_done, 1)
                pe.wait_ge(acc_out[0], t.out[0])
                for tt in range(PT + 1):
                    n = P if tt < PT else NS
                    last = pe.transpose(acc[0:n, 0, tt * FH:(tt + 1) * FH], logf[:, tt * P:tt * P + n], ident[0:FH, 0:FH])
                last.then_inc(acc_full[0], 1)
                t.use(0)
                for tt in range(PT):
                    last = pe.transpose(acc[:, 1, tt * FH:(tt + 1) * FH], ncum[:, tt * P:(tt + 1) * P], ident[0:FH, 0:FH])
                last.then_inc(acc_full[1], 1)
                t.use(1)
                pe.wait_ge(dmat_done, 1)
                wait_banks((2,))
                pe.matmul(acc[:, 2, 0:DB], lnx, m_in[:], start=True, stop=True)
                pe.matmul(acc[:, 2, DB:2 * DB], lng, m_in[:], start=True, stop=True)
                pe.matmul(acc[:, 2, 32:32 + NS], lnx, m_gt[:].rearrange("p b i -> p (b i)"), start=True, stop=True)
                pe.matmul(acc[:, 2, 256:256 + DB * NS], sel_i[:], newm[:].rearrange("p b k -> p (b k)"),
                          start=True, stop=True).then_inc(acc_full[2], 1)
                t.use(2)
                wait_banks()
                prompt_attention()
                wait_banks((0, 1, 2, 3))
                pe.wait_ge(pv_out, PAIRS)
                pe.wait_ge(later_done, 1)
                for c in range(LFN // 512):
                    bank = 2 * (c % 4)
                    pe.wait_ge(acc_out[bank], t.out[bank])
                    pe.matmul(acc[:, bank, :], ones[:], later.rearrange("p b g h -> p (b g h)")[:, c * 512:(c + 1) * 512],
                              start=True, stop=True).then_inc(acc_full[bank], 1)
                    t.use(bank)
                wait_banks()
                sample_attention()
                o_ready()
                wait_banks()
                project(KD)
                norm_total(0, KD - 1)

            def conv():
                norm_sum(hT, False)
                pe.wait_ge(rows_in, 16)
                for k in range(KD):
                    bank = 2 * (k % 4)
                    pe.wait_ge(acc_out[bank], t.out[bank])
                    for r in range(2):
                        last = pe.transpose(acc[:, bank, r * SR:(r + 1) * SR], st_rows[:, r, k * P:(k + 1) * P],
                                            ident[0:SR, 0:SR])
                    last.then_inc(acc_full[bank], 1)
                    t.use(bank)
                h_ready()
                b0, o = t.blk, list(t.out)
                with pe.Fori(0, KD // 2) as it:
                    for j in range(RING):
                        pe.wait_ge(w_in[j], 16 * (it + (b0 // RING + 1)))
                        pe.wait_ge(acc_out[2 * j], it + o[2 * j])
                        block_mm(j, 2 * j, KD, 0, hT, True, True)
                t.blocks(2 * KD, uses=KD // 2)
                wait_banks()
                for k in range(KD):
                    pe.wait_ge(conv_done, k // 2 + 1)
                    for h in range(2):
                        last = pe.matmul(acc[:, h, 0:HALF], ones[:], dw[:, k, h * HALF:(h + 1) * HALF],
                                         start=(k == 0), stop=(k == KD - 1))
                last.then_inc(acc_full[0], 1)
                t.use(0)
                for k in range(KD):
                    last = pe.transpose(acc[0:CB, 2 + k // 4, (k % 4) * P:(k % 4 + 1) * P], ext_p[:, k, SEQ:EP], ident[:])
                last.then_inc(acc_full[2], 1)
                t.use(2)
                pe.wait_ge(packed, 1)
                for r in range(2):
                    for k in range(KD):
                        last = pe.transpose(acc[0:SR, 4 + 2 * r + k // 4, (k % 4) * P:(k % 4 + 1) * P],
                                            st_new[:, k, r * HB:(r + 1) * HB, :].rearrange("p b w -> p (b w)"), ident[:])
                    last.then_inc(acc_full[4 + 2 * r], 1)
                    t.use(4 + 2 * r)
                norm_sum(hT, False)
                pe.wait_ge(silu_done, KD)
                wait_banks()
                project(KD)
                norm_total(0, KD - 1)

            for i in range(depth):
                kind, j = i % 3, i // 3
                if kind == 0:
                    gla(j)
                elif kind == 1:
                    fox()
                else:
                    conv()
                ffn()
            pe.wait_ge(x_done, 2 * depth * KD)
            for tt in range(PT + 1):
                n = P if tt < PT else NS
                bank = 2 * (tt % 4)
                pe.wait_ge(acc_out[bank], t.out[bank])
                for k in range(KD):
                    last = pe.transpose(acc[0:n, bank + k // 4, (k % 4) * P:(k % 4 + 1) * P],
                                        xT[:, k, tt * P:tt * P + n], ident[:])
                last.then_inc(acc_full[bank], 1)
                t.use(bank)

        @block.vector
        def _(dve):
            t = Tally()
            steps = [0]

            def step(ins):
                steps[0] += 1
                ins.then_inc(s_dve, 1)

            def stepped():
                dve.wait_ge(s_dve, steps[0])

            rstds = [0]

            def low(slot, tiles, done):
                s = slot % SPLITS
                dve.wait_ge(whi_done, done)
                dve.tensor_tensor(wsp[:, s, 1, 0:tiles * P], ring[:, slot, 0:tiles * P], wsp[:, s, 0, 0:tiles * P],
                                  ALU.subtract).then_inc(wlo_done, 1)

            def reciprocal_root(bank=0):
                if bank == 0:
                    t.use(0)
                dve.wait_ge(acc_out[bank], t.out[bank] + (bank != 0))
                dve.reciprocal(rstd[:], root[:]).then_inc(rstd_done, 1)
                rstds[0] += 1
                dve.wait_ge(rstd_done, rstds[0])

            def norm_pre(layer, which):
                reciprocal_root()
                for k in range(KD):
                    dve.scalar_tensor_tensor(out=hT[:, k, :], in0=xT[:, k, :], scalar=gcol(layer, which, k),
                                             in1=rstd[:], op0=ALU.mult, op1=ALU.mult).then_inc(h_done, 1)
                t.h += KD

            def norm_post(layer, which):
                if which == 1:
                    low(0, KD, t.split + 1)
                    low(1, KD, t.split + 2)
                reciprocal_root()
                for k in range(KD):
                    dve.scalar_tensor_tensor(out=yT[:, k, :], in0=yT[:, k, :], scalar=gcol(layer, which, k),
                                             in1=rstd[:], op0=ALU.mult, op1=ALU.mult).then_inc(z_done, 1)
                t.z += KD

            def add_square(squares, k):
                if k == 1:
                    dve.tensor_tensor(rstd[:], squares[:, 0, :], squares[:, 1, :], ALU.add).then_inc(sum_done, 1)
                else:
                    dve.wait_ge(sum_done, t.sum)
                    dve.tensor_tensor(rstd[:], rstd[:], squares[:, k, :], ALU.add).then_inc(sum_done, 1)
                t.sum += 1

            def sum_squares(squares):
                for k in range(KD):
                    dve.wait_ge(acc_out[2 * (k % 4)], t.out[2 * (k % 4)] - 1 + k // 4)
                    if k:
                        add_square(squares, k)

            for k in range(KD):
                bank = 2 * (k % 4)
                if k % 2 == 1:
                    dve.wait_ge(acc_full[bank], t.full[bank] + 1)
                    dve.tensor_copy(xT[:, k, :], accflat(bank)).then_inc(acc_out[bank], 1)
                t.use(bank)
            t.use(0)
            dve.wait_ge(const_made, N_CONST)

            def gla(j):
                norm_pre(3 * j, 0)
                t.blocks(2 * GH, uses=2)
                t.use(0)
                step(dve.memset(part(M1, M3 - M1), 0.0))
                for m in range(GH):
                    bank = 2 * ((m + 1) % 4)
                    dve.wait_ge(abs_done, GH * j + m + 1)
                    dve.tensor_scalar(two(big[:, 8 + m, :]), acc2(bank), vcol("bg", GH * j + m), 0.0, ALU.add, ALU.min)\
                       .then_inc(acc_out[bank], 1)
                    t.use(bank)
                dve.wait_ge(soft_done, j + 1)
                for m in range(GH):
                    dve.wait_ge(acc_out[2 * ((m + 1) % 4)], t.out[2 * ((m + 1) % 4)])
                step(dve.tensor_tensor(big[:, 8:12, :], big[:, 8:12, :], yT[:, 4:8, :], ALU.subtract))
                stepped()
                for m in range(GH):
                    dve.tensor_tensor_scan(yT[:, 4 + m, :], reset[:], big[:, 8 + m, :], 0.0, ALU.mult, ALU.add)\
                       .then_inc(cum_done, 1)
                dve.wait_ge(cum_done, GH * (j + 1))
                for t0, n, c in ((0, SEQ, GLA_CHUNK), (SEQ, NS, DS)):
                    for h in range(GH):
                        cum = yT[:, 4 + h, t0:t0 + n].rearrange("p (c t) -> p c t", t=c)
                        last = dve.tensor_tensor(g_diff[:, h, t0:t0 + n].rearrange("p (c t) -> p c t", t=c),
                                                 cum[:, :, c - 1:c].to_broadcast([P, n // c, c]), cum, ALU.subtract)
                last.then_inc(diff_done, 1)
                dve.wait_ge(decay_done, 2 * j + 1)
                dve.tensor_tensor(big[:, 0:4, :], big[:, 0:4, :], big[:, 8:12, :], ALU.mult)
                dve.wait_ge(decay_done, 2 * j + 2)
                dve.tensor_tensor(yT[:, 0:4, :], yT[:, 0:4, :], big[:, 4:8, :], ALU.mult)
                dve.wait_ge(kdec_done, j + 1)
                dve.tensor_tensor(big[:, 4:8, :], big[:, 4:8, :], g_diff, ALU.mult).then_inc(keys_done, 1)
                t.blocks(KD, uses=2)
                b0 = t.blk
                with dve.Fori(0, KD // RING) as it:
                    for a in range(RING):
                        dve.wait_ge(blk_done, it * RING + (b0 + a + 1))
                        dve.tensor_copy(v_nat[:, 0:PT, ds((it * RING + a) * P, P)],
                                        acc[:, 2 * a, :].rearrange("p (t n) -> p t n", t=PT))
                        dve.tensor_copy(v_nat[0:NS, PT, ds((it * RING + a) * P, P)], acc[0:NS, 2 * a + 1, 0:P])\
                           .then_inc(acc_out[2 * a], 1)
                t.blocks(KD, uses=2)
                stepped()
                for tt in range(PT + 1):
                    bank = 4 * (tt % 2)
                    t.use(bank)
                    dve.wait_ge(acc_full[bank + 1], t.full[bank + 1] + 1)
                    if tt < PT:
                        dve.copy_predicated(att[:, tt], m_chunk[:].bitcast(U32).rearrange("p (a t) -> p a t", a=1)
                                            .to_broadcast([P, GH, P]),
                                            acc[:, bank + 1, :].rearrange("p (h t) -> p h t", h=GH))\
                           .then_inc(acc_out[bank + 1], 1)
                    else:
                        mle = m_le[:].rearrange("p b t -> p (b t)").bitcast(U32).rearrange("p (a t) -> p a t", a=1)
                        dve.copy_predicated(att_s, mle.to_broadcast([NS, GH, NS]),
                                            acc[0:NS, bank + 1, :].rearrange("p (h t) -> p h t", h=GH)[:, :, 0:NS])\
                           .then_inc(acc_out[bank + 1], 1)
                    t.use(bank + 1)
                for c in range(NCH):
                    ob, ub = (0, 1)[c % 2], (2, 4)[c % 2]
                    dve.wait_ge(acc_full[ub], t.full[ub] + 1)
                    t.use(ub)
                    dve.wait_ge(acc_full[ob], t.full[ob] + 1)
                    t.use(ob)
                    if c > 0:
                        prev = (2, 4)[(c - 1) % 2]
                        dve.wait_ge(acc_out[prev], t.out[prev])
                    for h in range(GH):
                        add = acc[:, ub + h // 2, (h % 2) * DV:(h % 2 + 1) * DV]
                        end = (c + 1) * GLA_CHUNK - 1
                        if c == 0:
                            last = dve.tensor_copy(S[:, h, :], add)
                        else:
                            last = dve.scalar_tensor_tensor(out=S[:, h, :], in0=S[:, h, :],
                                                            scalar=big[:, 8 + h, end:end + 1], in1=add,
                                                            op0=ALU.mult, op1=ALU.add)
                    last.then_inc(acc_out[ub], 1)

                def keys_of(b):
                    dve.tensor_scalar(kd_b[:, b % 2], kd_nat[0:NS, PT], m_in[:, b:b + 1], None, ALU.mult)\
                       .then_inc(kdb_done, 1)

                bank = 4 * (PT % 2)
                dve.wait_ge(acc_out[0], t.out[0])
                keys_of(0)
                keys_of(1)
                for b in range(DB):
                    ub = (2, 4)[b % 2]
                    if b == DB - 1:
                        t.use(0)
                    dve.wait_ge(acc_full[ub], t.full[ub] + 1)
                    t.use(ub)
                    for h in range(GH):
                        end = SEQ + b * DS + DS - 1
                        state = st[:, (b // 2) % 2, b % 2, h, :]
                        last = dve.scalar_tensor_tensor(out=state, in0=state, scalar=big[:, 8 + h, end:end + 1],
                                                        in1=acc[:, ub + h // 2, (h % 2) * DV:(h % 2 + 1) * DV],
                                                        op0=ALU.mult, op1=ALU.add)
                    last.then_inc(acc_out[ub], 1)
                    if b + 2 < DB:
                        keys_of(b + 2)
                for h in range(GH):
                    t.use(2 * h)
                    dve.wait_ge(acc_out[2 * h], t.out[2 * h])
                    step(dve.reciprocal(big[:, h, :], big[:, h, :]))
                    stepped()
                    for v in range(VH):
                        u = h * VH + v
                        step(dve.scalar_tensor_tensor(out=hT[:, u, :], in0=hT[:, u, :], scalar=vcol("gn", VH * j + v),
                                                      in1=big[:, h, :], op0=ALU.mult, op1=ALU.mult))
                    stepped()
                    for u in range(h * VH, (h + 1) * VH):
                        dve.tensor_tensor(hT[:, u, :], hT[:, u, :], big[:, 12 + u, :], ALU.mult).then_inc(o_done, 1)
                t.blocks(KD, uses=2)
                sum_squares(big)
                norm_post(3 * j, 1)

            def ffn(i):
                s0, p0 = t.split, t.pair
                b0, o = t.blk, list(t.out)

                def gates(a, it, pair):
                    dve.wait_ge(blk_done, it * RING + (b0 + 2 * a + 1))
                    if pair is not None:
                        dve.wait_ge(g_done, pair)
                    dve.tensor_tensor(two(sil[:, a, :]), acc2(4 * a), two(rstd[:]), ALU.mult).then_inc(acc_out[4 * a], 1)

                def gated(a, it, pair):
                    dve.wait_ge(blk_done, it * RING + (b0 + 2 * a + 2))
                    dve.tensor_tensor(two(root[:]), acc2(4 * a + 2), two(rstd[:]), ALU.mult)\
                       .then_inc(acc_out[4 * a + 2], 1)
                    dve.wait_ge(acc_out[4 * a + 2], it + (o[4 * a + 2] + 1))
                    dve.wait_ge(silu_made, pair + 1)
                    dve.tensor_tensor(sil[:, a, :], sil[:, a, :], root[:], ALU.mult).then_inc(prod_done, 1)
                    dve.wait_ge(prod_done, pair * 2 + 1)
                    hi = g_hi[:, ds(it * 2 + a, 1), :].rearrange("p a t -> p (a t)")
                    lo = g_lo[:, ds(it * 2 + a, 1), :].rearrange("p a t -> p (a t)")
                    dve.tensor_copy(hi, sil[:, a, :]).then_inc(prod_done, 1)
                    dve.wait_ge(prod_done, pair * 2 + 2)
                    dve.tensor_tensor(lo, sil[:, a, :], hi, ALU.subtract).then_inc(g_done, 1)

                for k in range(KD):
                    dve.wait_ge(hhi_done, t.hhi + k + 1)
                    dve.scalar_tensor_tensor(out=h_lo[:, k, :], in0=xT[:, k, :], scalar=gcol(i, 2, k),
                                             in1=h_hi[:, k, :], op0=ALU.mult, op1=ALU.subtract).then_inc(h_done, 1)
                t.h += KD
                t.hhi += KD
                dve.wait_ge(xsq_done, i + 1)
                for n in (4, 2, 1):
                    if n < 4:
                        dve.wait_ge(sum_done, t.sum)
                    dst = big[:, 0:n, :] if n > 1 else rstd[:].rearrange("p (a t) -> p a t", a=1)
                    dve.tensor_tensor(dst, big[:, 0:n, :], big[:, n:2 * n, :], ALU.add).then_inc(sum_done, 1)
                    t.sum += 1
                low(2, KD, s0 + 3)
                low(3, KD, s0 + 4)
                reciprocal_root(6)
                o[6] += 1
                gates(0, 0, None)
                gated(0, 0, p0)
                with dve.Fori(0, KF // 2 - 1) as it:
                    low(0, KD, it * RING + (s0 + 5))
                    gates(1, it, it * 2 + (p0 + 1))
                    low(1, KD, it * RING + (s0 + 6))
                    gated(1, it, it * 2 + (p0 + 1))
                    low(2, KD, it * RING + (s0 + 7))
                    gates(0, it + 1, it * 2 + (p0 + 2))
                    low(3, KD, it * RING + (s0 + 8))
                    gated(0, it + 1, it * 2 + (p0 + 2))
                it = KF // 2 - 1
                s1 = s0 + 2 * KF
                low(0, KF2, s1 + 1)
                gates(1, it, p0 + KF - 1)
                low(1, KF2, s1 + 2)
                gated(1, it, p0 + KF - 1)
                t.out[6] += 1
                t.full[6] += 1
                t.blocks(2 * KF, uses=KF // 2)
                t.blocks(2 * KD)
                t.pair += KF
                for m in range(KD):
                    for b in (2 * m + 2, 2 * m + 3):
                        if b < 2 * KD:
                            low(b % RING, KF2, s1 + b + 1)
                    bank = 2 * (m % 4)
                    t.out[bank] += 1
                    dve.wait_ge(acc_out[bank], t.out[bank])
                    if m:
                        add_square(hT, m)
                t.split += 2 * KF + 2 * KD
                norm_post(i, 3)

            def prompt_scores(i, h, q):
                bank = i % 2
                dve.wait_ge(acc_full[bank], t.full[bank] + 1)
                if i >= 2:
                    tb = 2 + (i % 2)
                    dve.wait_ge(acc_full[tb], t.full[tb] + 1)
                if q:
                    dve.tensor_scalar(probs[:, i % 2, 0:q * P], acc[:, bank, 0:q * P], cumq[:, q, h:h + 1], None, ALU.add)
                dve.scalar_tensor_tensor(out=probs[:, i % 2, q * P:(q + 1) * P], in0=acc[:, bank, q * P:(q + 1) * P],
                                         scalar=cumq[:, q, h:h + 1], in1=causal[:], op0=ALU.add, op1=ALU.add)\
                   .then_inc(acc_out[bank], 1)
                t.use(bank)
                dve.wait_ge(acc_out[bank], t.out[bank])
                dve.tensor_reduce(nmax[:, i % 4:i % 4 + 1], probs[:, i % 2, 0:(q + 1) * P], AX.X, ALU.max, negate=True)\
                   .then_inc(pmax_done, 1)

            def prompt_probs(i, h, q):
                dve.wait_ge(pexp_done, i + 1)
                step(dve.reciprocal(rsum[:, i % 4:i % 4 + 1], rsum[:, i % 4:i % 4 + 1]))
                stepped()
                dve.tensor_scalar(probs[:, i % 2, 0:(q + 1) * P], probs[:, i % 2, 0:(q + 1) * P],
                                  rsum[:, i % 4:i % 4 + 1], None, ALU.mult).then_inc(p_done, 1)

            def sample_attention():
                base = steps[0]
                steps[0] += DB
                with dve.Fori(0, DB) as b:
                    dve.wait_ge(scores_full, b * 5 + 1)
                    dve.tensor_tensor(z[:, KEYS:KEYS + NS], acc[:, 7, 256:256 + NS],
                                      newb[:, ds(b, 1), :].rearrange("p a k -> p (a k)"), ALU.add).then_inc(scores_out, 1)
                    for n in range(4):
                        dve.wait_ge(scores_full, b * 5 + (n + 2))
                        for g in range(4 * n, 4 * n + 4):
                            last = dve.tensor_scalar(z[:, g * PAGE:(g + 1) * PAGE],
                                                     acc[:, 4 + n % 2, (g % 4) * PAGE:(g % 4 + 1) * PAGE],
                                                     behind[:, ds(b * NPAGES + g, 1)], None, ALU.add)
                        last.then_inc(scores_out, 1)
                    dve.wait_ge(scores_out, b * 5 + 5)
                    dve.tensor_reduce(nmx, z, AX.X, ALU.max, negate=True).then_inc(mx_done, 1)
                    dve.wait_ge(probs_done, b + 1)
                    dve.reciprocal(ssum, ssum).then_inc(s_dve, 1)
                    dve.wait_ge(s_dve, b + (base + 1))
                    dve.wait_ge(v_used, b * NPAGES + NPAGES)
                    dve.tensor_scalar(orow, acc[:, 7, 0:256], ssum, None, ALU.mult).then_inc(orow_done, 1)
                    dve.wait_ge(ot_full, b + 1)
                    for q in range(2):
                        for e in range(2):
                            rows = slice(e * DH, (e + 1) * DH)
                            src = acc[rows, 6, q * P:(q + 1) * P].rearrange("p (j n) -> p j n", j=GR)
                            at = q * 2 * DS + e * DS
                            last = dve.tensor_copy(hT[rows, q:PAIRS:2, ds(b * DS + SEQ, DS)], src[:, :, at:at + DS])
                    last.then_inc(ot_out, 1)

            def fox():
                norm_pre(1, 0)
                t.blocks(2 * KD, uses=4)
                t.use(0)
                dve.wait_ge(fabs_done, 1)
                dve.tensor_scalar(two(logf), acc[0:FH, 0:2, 0:HALF], fbias[:, 0:1], 0.0, ALU.add, ALU.min)\
                   .then_inc(acc_out[0], 1)
                dve.wait_ge(fexp_done, 1)
                dve.tensor_scalar(l_u, l_e, 1.0, None, ALU.add).then_inc(fu_done, 1)
                dve.wait_ge(fln_done, 1)
                step(dve.tensor_scalar(l_u, l_u, -1.0, None, ALU.add))
                stepped()
                step(dve.tensor_scalar(l_m, l_u, 0.0, None, ALU.is_equal))
                stepped()
                step(dve.tensor_tensor(l_u, l_u, l_m, ALU.add))
                step(dve.tensor_tensor(l_m, l_m, rstd[0:FH, :], ALU.add))
                stepped()
                step(dve.reciprocal(l_u, l_u))
                step(dve.tensor_tensor(l_m, l_m, l_e, ALU.mult))
                stepped()
                step(dve.tensor_tensor(l_m, l_m, l_u, ALU.mult))
                stepped()
                step(dve.tensor_tensor(logf, logf, l_m, ALU.subtract))
                stepped()
                step(dve.tensor_tensor_scan(ncum, ones[0:FH, 0:1].to_broadcast([FH, SEQ]), logf[:, 0:SEQ], 0.0,
                                            ALU.mult, ALU.subtract))
                stepped()
                dve.tensor_copy(l_u[:, 0:1], ncum[:, 0:1]).then_inc(logf_done, 1)
                step(dve.memset(qblk, 0.0))
                step(dve.memset(qz, 0.0))
                stepped()
                for e in range(2):
                    rows = slice(e * DH, (e + 1) * DH)
                    last = dve.tensor_copy(qblk[rows, :, :, e * DS:(e + 1) * DS],
                                           big[rows, 0:KD, SEQ:TOK].rearrange("p m (b i) -> p b m i", b=DB))
                last.then_inc(qblk_done, 1)
                b0 = t.blk
                with dve.Fori(0, KD // RING) as it:
                    for a in range(RING):
                        dve.wait_ge(blk_done, it * RING + (b0 + a + 1))
                        dve.tensor_copy(v_nat[:, 0:PT, ds((it * RING + a) * P, P)],
                                        acc[:, 2 * a, :].rearrange("p (t n) -> p t n", t=PT))
                        dve.tensor_copy(v_nat[0:NS, PT, ds((it * RING + a) * P, P)], acc[0:NS, 2 * a + 1, 0:P])\
                           .then_inc(acc_out[2 * a], 1)
                t.blocks(KD, uses=2)
                for tt in range(PT + 1):
                    t.use(2 * (tt % 4))
                dve.wait_ge(acc_full[0], t.full[0] + 1)
                dve.tensor_copy(lnat[:, 0:PT, :], acc[:, 0, 0:PT * FH].rearrange("p (t h) -> p t h", t=PT))
                dve.tensor_copy(lnat[0:NS, PT, :], acc[0:NS, 0, PT * FH:(PT + 1) * FH]).then_inc(acc_out[0], 1)
                t.use(0)
                dve.wait_ge(acc_full[1], t.full[1] + 1)
                dve.tensor_scalar(cumq, acc[:, 1, 0:PT * FH].rearrange("p (t h) -> p t h", t=PT), -1.0, None, ALU.mult)\
                   .then_inc(acc_out[1], 1)
                t.use(1)
                dve.wait_ge(acc_out[0], t.out[0])
                step(dve.memset(lnx, 0.0))
                step(dve.tensor_reduce(gt4, m_gt[:].rearrange("p b i -> p i b"), AX.X, ALU.add))
                stepped()
                step(dve.tensor_copy(lnx.rearrange("p (j c i) -> p j c i", j=GR, i=DS)[:, :, 0:GH4, :],
                                     lnat[0:NS, PT, :].rearrange("p (j c i) -> p j c i", j=GR, i=1)
                                     .to_broadcast([NS, GR, GH4, DS])))
                stepped()
                dve.tensor_tensor(lng.rearrange("p (g i) -> p g i", i=DS), lnx.rearrange("p (g i) -> p g i", i=DS),
                                  gt4.rearrange("p (g i) -> p g i", g=1).to_broadcast([NS, P // DS, DS]), ALU.mult)\
                   .then_inc(dmat_done, 1)
                dve.wait_ge(acc_full[2], t.full[2] + 1)
                step(dve.tensor_copy(aft, acc[:, 2, DB:2 * DB]))
                step(dve.tensor_copy(sufn, acc[:, 2, 32:32 + NS]))
                stepped()
                step(dve.tensor_tensor(tot, acc[:, 2, 0:DB], aft, ALU.subtract))
                step(dve.tensor_tensor(newb, acc[:, 2, 256:256 + DB * NS].rearrange("p (b k) -> p b k", b=DB),
                                       sufn.rearrange("p (b k) -> p b k", b=1).to_broadcast([P, DB, NS]), ALU.add))
                stepped()
                dve.tensor_tensor(newb, newb, aft.rearrange("p (b k) -> p b k", k=1).to_broadcast([P, DB, NS]),
                                  ALU.subtract).then_inc(acc_out[2], 1)
                t.use(2)
                dve.wait_ge(acc_out[2], t.out[2])
                stepped()
                items = [(h, q) for h in range(FH) for q in range(PT)]
                for i in range(len(items) + 1):
                    if i >= 1:
                        prompt_probs(i - 1, *items[i - 1])
                    if i < len(items):
                        prompt_scores(i, *items[i])
                    if i >= 2 or i == len(items):
                        t.use(2 + (i % 2))
                t.use(2 + (len(items) + 1) % 2)
                dve.wait_ge(lf_in, 16 * DB * NPAGES)
                step(dve.memset(later[:, :, NPAGES - 1, :], 0.0))
                for g in reversed(range(NPAGES - 1)):
                    stepped()
                    step(dve.tensor_tensor(later[:, :, g, :], later[:, :, g + 1, :], lf[:, :, g + 1, :], ALU.add))
                stepped()
                dve.tensor_copy(l_u[:, 0:1], ncum[:, 0:1]).then_inc(later_done, 1)
                for c in range(LFN // 512):
                    bank = 2 * (c % 4)
                    dve.wait_ge(acc_full[bank], t.full[bank] + 1)
                    dve.tensor_tensor(picked[:, 2 * c:2 * c + 2].rearrange("p b g h -> p (b g) h"),
                                      acc[:, bank, :].rearrange("p (n h) -> p n h", h=FH),
                                      onehot[:].rearrange("p (n h) -> p n h", n=1).to_broadcast([P, 2 * NPAGES, FH]),
                                      ALU.mult).then_inc(acc_out[bank], 1)
                    t.use(bank)
                for b in (0, 2, 4, 6):
                    dve.wait_ge(acc_out[b], t.out[b])
                step(dve.tensor_reduce(behind, picked.rearrange("p b g h -> p (b g) h"), AX.X, ALU.add))
                stepped()
                bh = behind.rearrange("p (b g) -> p b g", b=DB)
                dve.tensor_tensor(bh, bh, tot.rearrange("p (b g) -> p b g", g=1).to_broadcast([P, DB, NPAGES]), ALU.add)\
                   .then_inc(picked_done, 1)
                dve.wait_ge(picked_done, 1)
                stepped()
                sample_attention()
                dve.wait_ge(ot_out, DB)
                dve.tensor_copy(l_u[:, 0:1], l_m[:, 0:1]).then_inc(o_done, KD)
                t.blocks(KD, uses=2)
                sum_squares(big)
                norm_post(1, 1)

            def conv():
                for k in range(KD):
                    t.use(2 * (k % 4))
                norm_pre(2, 0)
                step(dve.memset(ext_p[:, :, 0:CB], 0.0))
                b0, o = t.blk, list(t.out)
                base = steps[0]
                with dve.Fori(0, KD // 2) as it:
                    for a in range(2):
                        dve.wait_ge(acc_out[4 * a + 2], it + (o[4 * a + 2] + 1))
                        dve.wait_ge(blk_done, it * RING + (b0 + 2 * a + 1))
                        bias = vecs[:, ds(it * 2 + (col["b1"] + a), 1)]
                        gate, bank = sil[:, a, :], 4 * a
                        m = it * 2 + a
                        dve.scalar_tensor_tensor(out=ext_p[:, ds(m, 1), CB:CB + HALF].rearrange("p a t -> p (a t)"),
                                                 in0=acc[:, bank, 0:HALF], scalar=bias, in1=gate[:, 0:HALF],
                                                 op0=ALU.add, op1=ALU.mult)
                        dve.scalar_tensor_tensor(out=ext_p[:, ds(m, 1), CB + HALF:EP].rearrange("p a t -> p (a t)"),
                                                 in0=acc[:, bank + 1, 0:SEQ - HALF], scalar=bias,
                                                 in1=gate[:, HALF:SEQ], op0=ALU.add, op1=ALU.mult)
                        dve.scalar_tensor_tensor(out=ext_s[:, ds(m, 1), :, CB:ES].rearrange("p a b t -> p (a b) t"),
                                                 in0=acc[:, bank + 1, SEQ - HALF:HALF].rearrange("p (b t) -> p b t", b=DB),
                                                 scalar=bias, in1=gate[:, SEQ:TOK].rearrange("p (b t) -> p b t", b=DB),
                                                 op0=ALU.add, op1=ALU.mult).then_inc(acc_out[bank], 1)
                    for a in range(2):
                        dve.wait_ge(acc_out[4 * a], it + (o[4 * a] + 1))
                    for w in range(CW):
                        for a in range(2):
                            m = it * 2 + a
                            tap = vecs[:, ds(it * 2 + (col["wdw"] + w * KD + a), 1)]
                            for q in range(2):
                                if q == 0:
                                    src = ext_p[:, ds(m, 1), w:w + SEQ].rearrange("p a t -> p (a t)")
                                    dst = dw[:, ds(m, 1), 0:SEQ].rearrange("p a t -> p (a t)")
                                else:
                                    src = ext_s[:, ds(m, 1), :, w:w + DS].rearrange("p a b t -> p (a b) t")
                                    dst = dw[:, ds(m, 1), SEQ:TOK].rearrange("p a (b t) -> p (a b) t", b=DB)
                                if w == 0:
                                    ins = dve.tensor_scalar(dst, src, tap, vecs[:, ds(it * 2 + (col["bdw"] + a), 1)],
                                                            ALU.mult, ALU.add)
                                else:
                                    dve.wait_ge(s_dve, it * (4 * CW - 4) + (base + 4 * w + 2 * a + q - 3))
                                    ins = dve.scalar_tensor_tensor(out=dst, in0=src, scalar=tap, in1=dst,
                                                                   op0=ALU.mult, op1=ALU.add)
                                if w == CW - 1 and a == 1 and q == 1:
                                    ins.then_inc(conv_done, 1)
                                elif w == CW - 1:
                                    pass
                                else:
                                    ins.then_inc(s_dve, 1)
                steps[0] += (4 * CW - 4) * (KD // 2)
                t.blocks(2 * KD, uses=KD // 2)
                t.use(0)
                dve.wait_ge(acc_out[0], t.out[0])
                dve.wait_ge(conv_done, KD // 2)
                for k in range(KD):
                    dve.tensor_tensor(dw[:, k, :], dw[:, k, :], root[:], ALU.subtract).then_inc(mean_done, 1)
                for b in (2, 4, 6):
                    t.use(b)
                reciprocal_root()
                for k in range(KD):
                    dve.tensor_tensor(dw[:, k, :], dw[:, k, :], rstd[:], ALU.mult).then_inc(scaled_done, 1)
                t.blocks(KD, uses=2)
                sum_squares(big)
                norm_post(2, 1)

            for i in range(depth):
                kind, j = i % 3, i // 3
                if kind == 0:
                    gla(j)
                elif kind == 1:
                    fox()
                else:
                    conv()
                ffn(i)

        @block.scalar
        def _(act):
            t = Tally()
            steps = [0]

            def step(ins):
                steps[0] += 1
                ins.then_inc(s_act, 1)

            def stepped():
                act.wait_ge(s_act, steps[0])

            rstds = [0]

            def high(slot, tiles, loaded, used):
                act.wait_ge(w_in[slot], loaded)
                if used is not None:
                    act.wait_ge(blk_done, used)
                act.activation(wsp[:, slot % SPLITS, 0, 0:tiles * P], ring[:, slot, 0:tiles * P], ACT.Copy)\
                   .then_inc(whi_done, 1)

            def first_high():
                act.wait_ge(state_out, 16 * states[0])
                for b in range(2):
                    high(b, KD, 16 * (t.blk // RING + 1), t.blk)

            states = [0]

            def root_of_mean(eps=0, bank=0):
                act.wait_ge(acc_full[bank], t.full[bank] + 1)
                if rstds[0]:
                    act.wait_ge(rstd_done, rstds[0])
                act.activation(two(root[:]), acc2(bank), ACT.Sqrt, bias=epsb[:, eps:eps + 1], scale=1.0 / D)\
                   .then_inc(acc_out[bank], 1)
                t.use(bank)
                rstds[0] += 1

            def squares_of_x():
                for k in range(KD):
                    if t.x:
                        act.wait_ge(x_done, t.x - KD + k + 1)
                    act.activation(hT[:, k, :], xT[:, k, :], ACT.Square).then_inc(sq_done, 1)
                t.sq += KD
                root_of_mean()

            def read_y():
                b0 = t.blk
                with act.Fori(0, KD // 4) as it:
                    for a in range(4):
                        act.wait_ge(blk_done, it * 4 + (b0 + a + 1))
                        act.activation(two(yT[:, ds(it * 4 + a, 1), :].rearrange("p a t -> p (a t)")), acc2(2 * a), ACT.Copy)
                        act.activation(two(big[:, ds(it * 4 + a, 1), :].rearrange("p a t -> p (a t)")), acc2(2 * a),
                                       ACT.Square).then_inc(acc_out[2 * a], 1)
                t.blocks(KD, uses=KD // 4)
                first_high()
                root_of_mean()
                t.x += KD

            for k in range(KD):
                bank = 2 * (k % 4)
                if k % 2 == 0:
                    act.wait_ge(acc_full[bank], t.full[bank] + 1)
                    act.activation(xT[:, k, :], accflat(bank), ACT.Copy).then_inc(acc_out[bank], 1)
                t.use(bank)
            act.wait_ge(acc_full[0], t.full[0] + 1)
            step(act.activation(vecs[:, 0:P + VN[1]], acc[:, 0, 0:P + VN[1]], ACT.Copy))
            act.activation(vecs[:, 2 * P:3 * P + VN[3]], acc[:, 0, 2 * P:3 * P + VN[3]], ACT.Copy).then_inc(acc_out[0], 1)
            t.use(0)
            for b in (0, 2, 4, 6):
                act.wait_ge(acc_out[b], t.out[b])
            act.wait_ge(const_made, N_CONST)

            def gla(j):
                states[0] += 1
                squares_of_x()
                for base, scale in ((0, DK ** -0.5), (GH, 1.0)):
                    for m in range(GH):
                        act.wait_ge(blk_done, t.blk + m + 1)
                        act.activation(two(big[:, base + m, :]), acc2(2 * m), ACT.Copy, scale=scale)\
                           .then_inc(acc_out[2 * m], 1)
                    t.blocks(GH, uses=1)
                act.wait_ge(acc_full[0], t.full[0] + 1)
                act.activation(two(lowr), acc[0:RANK, 0:2, 0:HALF], ACT.Copy).then_inc(acc_out[0], 1)
                t.use(0)
                for m in range(GH):
                    bank = 2 * ((m + 1) % 4)
                    act.wait_ge(acc_full[bank], t.full[bank] + 1)
                    act.activation(two(yT[:, 4 + m, :]), acc2(bank), ACT.Abs, bias=vcol("bg", GH * j + m))\
                       .then_inc(abs_done, 1)
                    t.use(bank)
                act.wait_ge(abs_done, GH * (j + 1))
                step(act.activation(yT[:, 4:8, :], yT[:, 4:8, :], ACT.Exp, scale=-1.0))
                stepped()
                act.activation(yT[:, 4:8, :], yT[:, 4:8, :], ACT.Ln, bias=1.0).then_inc(soft_done, 1)
                act.wait_ge(cum_done, GH * (j + 1))
                act.activation(big[:, 8:12, :], yT[:, 4:8, :], ACT.Exp, scale=1.0 / 16).then_inc(decay_done, 1)
                act.activation(yT[:, 0:4, :], yT[:, 4:8, :], ACT.Exp, scale=-1.0 / 16).then_inc(decay_done, 1)
                act.wait_ge(diff_done, j + 1)
                act.activation(g_diff, g_diff, ACT.Exp, scale=1.0 / 16).then_inc(kdec_done, 1)
                b0 = t.blk
                with act.Fori(0, KD // RING) as it:
                    for a in range(RING):
                        act.wait_ge(blk_done, it * RING + (b0 + a + 1))
                        act.activation(two(big[:, ds(it * RING + (12 + a), 1), :].rearrange("p a t -> p (a t)")),
                                       acc2(2 * a), ACT.Silu).then_inc(acc_out[2 * a], 1)
                t.blocks(KD, uses=2)
                t.blocks(KD, uses=2)
                for tt in range(PT + 1):
                    n = P if tt < PT else NS
                    bank = 4 * (tt % 2)
                    act.wait_ge(acc_full[bank], t.full[bank] + 1)
                    act.activation(kd_nat[0:n, tt], acc[0:n, bank, :].rearrange("p (h k) -> p h k", h=GH), ACT.Copy)\
                       .then_inc(acc_out[bank], 1)
                    t.use(bank)
                    t.use(bank + 1)
                for c in range(NCH):
                    ob, ub = (0, 1)[c % 2], (2, 4)[c % 2]
                    act.wait_ge(acc_full[ob], t.full[ob] + 1)
                    act.activation(hT[:, :, c * GLA_CHUNK:(c + 1) * GLA_CHUNK],
                                   acc[:, ob, :].rearrange("p (u t) -> p u t", u=KD), ACT.Copy).then_inc(acc_out[ob], 1)
                    t.use(ub)
                    t.use(ob)
                for b in range(DB):
                    ub = (2, 4)[b % 2]
                    if b == DB - 1:
                        act.wait_ge(acc_full[0], t.full[0] + 1)
                        act.activation(hT[:, :, SEQ:TOK], acc[:, 0, 0:KD * NS].rearrange("p (u t) -> p u t", u=KD),
                                       ACT.Copy).then_inc(acc_out[0], 1)
                        t.use(0)
                    t.use(ub)
                    if b % 2 == 1:
                        for q in (2, 4):
                            act.wait_ge(acc_out[q], t.out[q])
                        act.dma_start(gla_ss[j, b - 1:b + 1].rearrange("b h k v -> k b h v"), st[:, (b // 2) % 2])\
                           .then_inc(st_out[(b // 2) % 2], 16)
                act.wait_ge(acc_out[0], t.out[0])
                act.wait_ge(acc_out[1], t.out[1])
                for u in range(KD):
                    act.activation(yT[:, u, :], hT[:, u, :], ACT.Square).then_inc(sq_done, 1)
                t.sq += KD
                for h in range(GH):
                    act.wait_ge(acc_full[2 * h], t.full[2 * h] + 1)
                    act.activation(two(big[:, h, :]), acc2(2 * h), ACT.Sqrt, bias=epsb[:, 0:1], scale=1.0 / DV)\
                       .then_inc(acc_out[2 * h], 1)
                    t.use(2 * h)
                for q in st_out:
                    act.wait_ge(q, 16 * (DB // 4) * (j + 1))
                read_y()

            def ffn(i):
                b0, o, l0 = t.blk, list(t.out), t.blk // RING
                p0 = t.pair

                def silu(a, scaled):
                    act.wait_ge(acc_out[4 * a], scaled)
                    act.activation(sil[:, a, :], sil[:, a, :], ACT.Silu).then_inc(silu_made, 1)

                for k in range(KD):
                    act.wait_ge(x_done, t.x - KD + k + 1)
                    act.activation(h_hi[:, k, :], xT[:, k, :], ACT.Copy, scale=gcol(i, 2, k)).then_inc(hhi_done, 1)
                act.activation(big[:, 0:KD, :], xT[:], ACT.Square).then_inc(xsq_done, 1)
                high(2, KD, 16 * (l0 + 1), b0 + 1)
                high(3, KD, 16 * (l0 + 1), b0 + 2)
                root_of_mean(bank=6)
                silu(0, o[0] + 1)
                with act.Fori(0, KF // 2 - 1) as it:
                    for a in range(2):
                        high(2 * a, KD, (it + (l0 + 2)) * 16, it * RING + (b0 + 2 * a + 3))
                        silu(1 - a, it + (o[4 - 4 * a] + 1 + a))
                        high(2 * a + 1, KD, (it + (l0 + 2)) * 16, it * RING + (b0 + 2 * a + 4))
                l1 = l0 + KF // 2
                b1 = b0 + 2 * KF
                high(0, KF2, 16 * (l1 + 1), b1 - 1)
                silu(1, o[4] + KF // 2)
                high(1, KF2, 16 * (l1 + 1), b1)
                t.blocks(2 * KF, uses=KF // 2)
                t.pair += KF
                for m in range(KD):
                    for b in (2 * m + 2, 2 * m + 3):
                        if b < 2 * KD:
                            high(b % RING, KF2, 16 * (l1 + b // RING + 1), b1 + b - 1)
                    act.wait_ge(blk_done, b1 + 2 * m + 2)
                    act.activation(two(yT[:, m, :]), acc2(2 * (m % 4)), ACT.Copy)
                    act.activation(two(hT[:, m, :]), acc2(2 * (m % 4)), ACT.Square).then_inc(acc_out[2 * (m % 4)], 1)
                t.blocks(2 * KD, uses=KD // 4)
                root_of_mean()
                t.x += KD

            def store(dst, src, done=out_in):
                act.dma_start(dst, src).then_inc(done, 16)
                outputs.append(dst) if done is out_in else None

            def fox():
                squares_of_x()
                act.wait_ge(state_out, 16)
                for base, scale in ((0, DH ** -0.5), (KD, 1.0)):
                    b0 = t.blk
                    with act.Fori(0, KD // RING) as it:
                        for a in range(RING):
                            act.wait_ge(blk_done, it * RING + (b0 + a + 1))
                            act.activation(two(big[:, ds(it * RING + (base + a), 1), :].rearrange("p a t -> p (a t)")),
                                           acc2(2 * a), ACT.Copy, scale=scale).then_inc(acc_out[2 * a], 1)
                    t.blocks(KD, uses=2)
                act.wait_ge(acc_full[0], t.full[0] + 1)
                act.activation(two(l_e), acc[0:FH, 0:2, 0:HALF], ACT.Abs, bias=fbias[:, 0:1]).then_inc(fabs_done, 1)
                t.use(0)
                act.wait_ge(fabs_done, 1)
                act.activation(l_e, l_e, ACT.Exp, scale=-1.0).then_inc(fexp_done, 1)
                act.wait_ge(fu_done, 1)
                act.activation(rstd[0:FH, :], l_u, ACT.Ln).then_inc(fln_done, 1)
                t.blocks(KD, uses=2)
                for b in (0, 2, 4, 6):
                    act.wait_ge(acc_out[b], t.out[b])
                store(fox_vp[0, 0].rearrange("(t p) h d -> p t (h d)", p=P), v_nat[:, 0:PT, :], nat_out)
                store(fox_vs[0].rearrange("b s h d -> (b s) (h d)"), v_nat[0:NS, PT, :], nat_out)
                for tt in range(PT + 1):
                    n = P if tt < PT else NS
                    bank = 2 * (tt % 4)
                    rows = k_rows[:, tt, :] if tt < PT else k_rows_s
                    act.wait_ge(acc_full[bank], t.full[bank] + 1)
                    act.activation(rows, acc[0:n, bank:bank + 2, :].rearrange("p b n -> p (b n)"), ACT.Copy)\
                       .then_inc(acc_out[bank], 1)
                    t.use(bank)
                    act.wait_ge(acc_out[bank], t.out[bank])
                    store(fox_kp[0, 0, tt * P:(tt + 1) * P].rearrange("p h d -> p (h d)") if tt < PT
                          else fox_ks[0].rearrange("b s h d -> (b s) (h d)"), rows, nat_out)
                t.use(0)
                act.wait_ge(acc_out[0], t.out[0])
                store(fox_lp[0, 0].rearrange("(t p) h -> p t h", p=P), lnat[:, 0:PT, :], nat_out)
                store(fox_ls[0].rearrange("b s h -> (b s) h"), lnat[0:NS, PT, :], nat_out)
                for b in (1, 2):
                    t.use(b)
                items = [(h, q) for h in range(FH) for q in range(PT)]
                for i in range(len(items) + 3):
                    if i < len(items):
                        h, q = items[i]
                        act.wait_ge(pmax_done, i + 1)
                        act.activation(probs[:, i % 2, 0:(q + 1) * P], probs[:, i % 2, 0:(q + 1) * P], ACT.Exp,
                                       bias=nmax[:, i % 4:i % 4 + 1], accum_out=rsum[:, i % 4:i % 4 + 1])\
                           .then_inc(pexp_done, 1)
                        t.use(i % 2)
                    if 2 <= i < len(items) + 2:
                        h, q = items[i - 2]
                        bank = 2 + (i % 2)
                        if q == 0 and h >= 2:
                            act.wait_ge(pv_full, h - 1)
                        act.wait_ge(acc_full[bank], t.full[bank] + 1)
                        act.activation(pT[:, h % 2, 0:q + 1, q * P:(q + 1) * P],
                                       acc[:, bank, 0:(q + 1) * P].rearrange("p (k n) -> p k n", n=P), ACT.Copy)\
                           .then_inc(acc_out[bank], 1)
                        t.use(bank)
                    if i >= 3:
                        h, q = items[i - 3]
                        if q == PT - 1 and h % 2 == 1:
                            act.wait_ge(pv_full, h + 1)
                            act.activation(hT[:, h // 2, 0:SEQ], acc[:, 4 + (h // 2) % 2, :], ACT.Copy).then_inc(pv_out, 1)
                for b in (0, 2, 4, 6):
                    t.use(b)
                with act.Fori(0, DB) as b:
                    for g in range(NPAGES):
                        act.wait_ge(page_turned, b * NPAGES + (g + 1))
                        bank = 2 * (g % 2)
                        act.activation(kT[:, g % 2].rearrange("p m k -> p (m k)"),
                                       acc[:, bank:bank + 2, :].rearrange("p b n -> p (b n)"), ACT.Copy).then_inc(kt_out, 1)
                    act.wait_ge(mx_done, b + 1)
                    act.activation(z, z, ACT.Exp, bias=nmx, accum_out=ssum).then_inc(probs_done, 1)
                    for u in range(5):
                        act.wait_ge(pt_full, b * 5 + (u + 1))
                        if u == 0:
                            act.activation(ptb[0:NS, 0, 0:P], acc[0:NS, 6, 0:P], ACT.Copy).then_inc(pt_out, 1)
                        else:
                            act.activation(ptb[:, u % 2, :], acc[:, 6, :], ACT.Copy).then_inc(pt_out, 1)
                read_y()

            def conv():
                for k in range(KD):
                    act.wait_ge(x_done, t.x - KD + k + 1)
                    act.activation(hT[:, k, :], xT[:, k, :], ACT.Square).then_inc(sq_done, 1)
                t.sq += KD
                root_of_mean()
                for k in range(KD):
                    bank = 2 * (k % 4)
                    act.wait_ge(acc_full[bank], t.full[bank] + 1)
                    act.activation(ext_s[:, k, :, 0:CB], acc[:, bank, 0:2 * SR].rearrange("p (b w) -> p b w", b=DB),
                                   ACT.Copy).then_inc(acc_out[bank], 1)
                    t.use(bank)
                b0, o = t.blk, list(t.out)
                with act.Fori(0, KD // 2) as it:
                    for a in range(2):
                        act.wait_ge(blk_done, it * RING + (b0 + 2 * a + 2))
                        act.wait_ge(acc_out[4 * a], it + o[4 * a])
                        act.activation(two(sil[:, a, :]), acc2(4 * a + 2), ACT.Sigmoid,
                                       bias=vecs[:, ds(it * 2 + (col["b1"] + KD + a), 1)]).then_inc(acc_out[4 * a + 2], 1)
                t.blocks(2 * KD, uses=KD // 2)
                for a in (0, 4):
                    act.wait_ge(acc_out[a], t.out[a])
                act.activation(st_new, ext_s[:, :, :, DS:ES], ACT.Copy).then_inc(packed, 1)
                act.wait_ge(acc_full[0], t.full[0] + 1)
                act.wait_ge(rstd_done, rstds[0])
                act.activation(two(root[:]), acc2(0), ACT.Copy, scale=1.0 / D).then_inc(acc_out[0], 1)
                t.use(0)
                base = t.x
                for k in range(KD):
                    act.wait_ge(mean_done, k + 1)
                    act.activation(hT[:, k, :], dw[:, k, :], ACT.Square).then_inc(sq_done, 1)
                t.sq += KD
                act.wait_ge(acc_full[2], t.full[2] + 1)
                act.activation(cp_rows, acc[0:CB, 2:4, :].rearrange("p b n -> p (b n)"), ACT.Copy).then_inc(acc_out[2], 1)
                t.use(2)
                for r in range(2):
                    bank = 4 + 2 * r
                    act.wait_ge(acc_full[bank], t.full[bank] + 1)
                    act.activation(cs_rows[:, r, :], acc[0:SR, bank:bank + 2, :].rearrange("p b n -> p (b n)"), ACT.Copy)\
                       .then_inc(acc_out[bank], 1)
                    t.use(bank)
                root_of_mean(eps=1)
                for b in (2, 4, 6):
                    act.wait_ge(acc_out[b], t.out[b])
                store(cv_p[0, 0], cp_rows, nat_out)
                store(cv_s[0].rearrange("(r b) w n -> (b w) r n", r=2), cs_rows, nat_out)
                for k in range(KD):
                    act.wait_ge(scaled_done, k + 1)
                    act.activation(hT[:, k, :], dw[:, k, :], ACT.Silu, bias=vcol("lnb", k), scale=vcol("lng", k))\
                       .then_inc(silu_done, 1)
                for m in range(KD):
                    act.wait_ge(blk_done, t.blk + m + 1)
                    act.activation(two(yT[:, m, :]), acc2(2 * (m % 4)), ACT.Identity, bias=vcol("b2", m))
                    act.activation(two(big[:, m, :]), acc2(2 * (m % 4)), ACT.Square, bias=vcol("b2", m))\
                       .then_inc(acc_out[2 * (m % 4)], 1)
                t.blocks(KD, uses=2)
                act.wait_ge(nat_out, 16 * (PT + 7))
                first_high()
                root_of_mean()
                t.x += KD

            for i in range(depth):
                kind, j = i % 3, i // 3
                if kind == 0:
                    gla(j)
                elif kind == 1:
                    fox()
                else:
                    conv()
                ffn(i)
            act.wait_ge(x_done, t.x)
            for tt in range(PT + 1):
                n = P if tt < PT else NS
                bank = 2 * (tt % 4)
                act.wait_ge(acc_full[bank], t.full[bank] + 1)
                act.activation(xin[0:n, tt, :], acc[0:n, bank:bank + 2, :].rearrange("p b n -> p (b n)"), ACT.Copy)\
                   .then_inc(acc_out[bank], 1)
                t.use(bank)
                act.wait_ge(acc_out[bank], t.out[bank])
                dst = y_prompt[0, tt * P:(tt + 1) * P, :] if tt < PT else y_sample.rearrange("b s n -> (b s) n")
                act.dma_start(dst, xin[0:n, tt, :]).then_inc(out_in, 16)
                outputs.append(dst)
            act.wait_ge(out_in, 16 * len(outputs))
            act.wait_ge(state_out, 16 * ((depth + 2) // 3))


_OUTS = [("y_prompt", (1, 512, 1024)), ("y_sample", (8, 4, 1024)),
         ("gla_sp", (2, 1, 4, 128, 256)), ("gla_ss", (2, 8, 4, 128, 256)),
         ("fox_kp", (1, 1, 512, 16, 64)), ("fox_vp", (1, 1, 512, 16, 64)), ("fox_lp", (1, 1, 512, 16)),
         ("fox_ks", (1, 8, 4, 16, 64)), ("fox_vs", (1, 8, 4, 16, 64)), ("fox_ls", (1, 8, 4, 16)),
         ("cv_p", (1, 1, 30, 1024)), ("cv_s", (1, 8, 30, 1024))]
_INS = ['x_prompt', 'x_sample', 'state_gla', 'cache_fox_k', 'cache_fox_v', 'cache_fox_logf', 'state_conv', 'page_table',
        'norm_g', 'gla_wq', 'gla_wk', 'gla_wv', 'gla_wg1', 'gla_wg2', 'gla_bg', 'gla_wr', 'gla_gn', 'gla_wo',
        'fox_wq', 'fox_wk', 'fox_wv', 'fox_wf', 'fox_bf', 'fox_wo', 'conv_w1', 'conv_b1', 'conv_wdw', 'conv_bdw',
        'conv_ln_g', 'conv_ln_b', 'conv_w2', 'conv_b2', 'ffn_w1', 'ffn_w3', 'ffn_w2']


def kernel(**inputs):
    import numpy as _np
    import concourse.bacc as _bacc
    from concourse import mybir as _mybir
    from concourse.bass_utils import run_bass_kernel_spmd as _run

    nc = _bacc.Bacc("TRN2", target_bir_lowering=False, num_devices=1)
    arrays, ins = {}, []
    for name in _INS:
        a = _np.ascontiguousarray(inputs[name])
        arrays[f"in_{name}"] = a
        ins.append(nc.dram_tensor(f"in_{name}", a.shape, _mybir.dt.from_np(a.dtype), kind="ExternalInput").ap())
    outs = [nc.dram_tensor(f"out_{n}", s, _mybir.dt.float32, kind="ExternalOutput").ap() for n, s in _OUTS]
    build(nc, ins, outs)
    r = _run(nc, [arrays], core_ids=[0])
    return tuple(r.results[0][f"out_{n}"] for n, _ in _OUTS)
```
